# Optimizing a Trainium2 kernel written in Bass

```python
import math
import jax, jax.numpy as jnp
from jax import lax
import numpy as np

D_MODEL = 1024
BATCH = 1
SEQ = 256
DEPTH = 1

CHUNK = 64
N_HEADS_A = 4
HEAD_DIM_A = 64
WIDTH_A = N_HEADS_A * 2 * HEAD_DIM_A
Q_BLOCK = 128
N_HEADS_B = 8
HEAD_DIM_B = 64
WIDTH_B = N_HEADS_B * HEAD_DIM_B
N_PREV_CHUNKS = 8
REL_CLIP = 128
IN_COLS = 3 * WIDTH_A + 3 * WIDTH_B + 2 * D_MODEL
N_EXPERTS = 32
TOP_K = 4
D_FF = 1024
SWIGLU_ALPHA = 1.702
SWIGLU_LIMIT = 7.0
EXPERT_BLOCK = 128
DEEPNORM_ALPHA = (2 * DEPTH) ** 0.25
DEEPNORM_BETA = (8 * DEPTH) ** -0.25
LN_EPS = 1e-5


def layer_norm(x, g, b):
    xf = x.astype(jnp.float32)
    mu = jnp.mean(xf, axis=-1, keepdims=True)
    var = jnp.mean(jnp.square(xf - mu), axis=-1, keepdims=True)
    y = (xf - mu) * lax.rsqrt(var + LN_EPS) * g.astype(jnp.float32) + b.astype(jnp.float32)
    return y.astype(x.dtype)

def rms_norm(x, w):
    xf = x.astype(jnp.float32)
    y = xf * lax.rsqrt(jnp.mean(jnp.square(xf), axis=-1, keepdims=True) + LN_EPS) * w.astype(jnp.float32)
    return y.astype(x.dtype)

def alibi_slopes(n):
    return jnp.asarray(np.array([2.0 ** (-8.0 * (i + 1) / n) for i in range(n)], dtype=np.float32))

def diff_attention(q, k, v, lam, lam_init, subln_w):
    B, S = q.shape[0], q.shape[1]
    scale = HEAD_DIM_A ** -0.5
    q = q.transpose(0, 2, 1, 3, 4) * scale
    k = k.transpose(0, 2, 1, 3, 4)
    v = v.transpose(0, 2, 1, 3)
    n_qb = S // Q_BLOCK
    qb = q.reshape(B, N_HEADS_A, n_qb, Q_BLOCK, 2, HEAD_DIM_A).transpose(2, 0, 1, 3, 4, 5)
    kpos = jnp.arange(S, dtype=jnp.int32)
    kchunk = kpos // CHUNK
    slopes = alibi_slopes(N_HEADS_A)

    def one_block(args):
        q_blk, i = args
        qpos = i * Q_BLOCK + jnp.arange(Q_BLOCK, dtype=jnp.int32)
        s = jnp.einsum('bhqcd,bhkcd->cbhqk', q_blk, k).astype(jnp.float32)
        dist = jnp.abs(qpos[:, None] - kpos[None, :]).astype(jnp.float32)
        bias = -slopes[:, None, None] * dist
        allowed = kchunk[None, :] <= (qpos // CHUNK)[:, None]
        p = jax.nn.softmax(jnp.where(allowed, s + bias, -jnp.inf), axis=-1)
        a = p[0] - lam * p[1]
        return jnp.einsum('bhqk,bhkd->bhqd', a.astype(v.dtype), v)

    o = lax.map(one_block, (qb, jnp.arange(n_qb, dtype=jnp.int32)))
    o = o.transpose(1, 0, 3, 2, 4).reshape(B, S, N_HEADS_A, 2 * HEAD_DIM_A)
    o = rms_norm(o, subln_w) * (1.0 - lam_init)
    return o.reshape(B, S, WIDTH_A)

def chunk_band_attention(q, k, v, rel_bias):
    B, S = q.shape[0], q.shape[1]
    n_chunks = S // CHUNK
    pad_len = N_PREV_CHUNKS * CHUNK
    band = (N_PREV_CHUNKS + 1) * CHUNK
    scale = HEAD_DIM_B ** -0.5
    q = q.transpose(0, 2, 1, 3) * scale
    kp = jnp.pad(k.transpose(0, 2, 1, 3), ((0, 0), (0, 0), (pad_len, 0), (0, 0)))
    vp = jnp.pad(v.transpose(0, 2, 1, 3), ((0, 0), (0, 0), (pad_len, 0), (0, 0)))
    qc = q.reshape(B, N_HEADS_B, n_chunks, CHUNK, HEAD_DIM_B).transpose(2, 0, 1, 3, 4)
    qi = jnp.arange(CHUNK, dtype=jnp.int32)
    kj = jnp.arange(band, dtype=jnp.int32)
    rel = (kj[None, :] - pad_len) - qi[:, None]
    bias = rel_bias.astype(jnp.float32)[:, jnp.clip(rel, -REL_CLIP, REL_CLIP) + REL_CLIP]

    def one_chunk(args):
        q_blk, c = args
        start = c * CHUNK
        kb = lax.dynamic_slice_in_dim(kp, start, band, axis=2)
        vb = lax.dynamic_slice_in_dim(vp, start, band, axis=2)
        s = jnp.einsum('bhqd,bhkd->bhqk', q_blk, kb).astype(jnp.float32) + bias
        valid = (start - pad_len + kj) >= 0
        p = jax.nn.softmax(jnp.where(valid, s, -jnp.inf), axis=-1)
        return jnp.einsum('bhqk,bhkd->bhqd', p.astype(vb.dtype), vb)

    o = lax.map(one_chunk, (qc, jnp.arange(n_chunks, dtype=jnp.int32)))
    return o.transpose(1, 0, 3, 2, 4).reshape(B, S, WIDTH_B)

def gated_mixer(h, w_in, b_gate, lam_q1, lam_k1, lam_q2, lam_k2, subln_w, rel_bias,
                w_branch_a, w_branch_b, w_out, lam_init):
    B, S, D = h.shape
    proj = h @ w_in
    o0 = 0
    qa = proj[..., o0:o0 + WIDTH_A].reshape(B, S, N_HEADS_A, 2, HEAD_DIM_A); o0 += WIDTH_A
    ka = proj[..., o0:o0 + WIDTH_A].reshape(B, S, N_HEADS_A, 2, HEAD_DIM_A); o0 += WIDTH_A
    va = proj[..., o0:o0 + WIDTH_A].reshape(B, S, N_HEADS_A, 2 * HEAD_DIM_A); o0 += WIDTH_A
    qb = proj[..., o0:o0 + WIDTH_B].reshape(B, S, N_HEADS_B, HEAD_DIM_B); o0 += WIDTH_B
    kb = proj[..., o0:o0 + WIDTH_B].reshape(B, S, N_HEADS_B, HEAD_DIM_B); o0 += WIDTH_B
    vb = proj[..., o0:o0 + WIDTH_B].reshape(B, S, N_HEADS_B, HEAD_DIM_B); o0 += WIDTH_B
    gates = jax.nn.sigmoid(proj[..., o0:] + b_gate).reshape(B, S, 2, D)

    lam = (jnp.exp(jnp.sum(lam_q1.astype(jnp.float32) * lam_k1.astype(jnp.float32)))
           - jnp.exp(jnp.sum(lam_q2.astype(jnp.float32) * lam_k2.astype(jnp.float32))) + lam_init)
    out_a = diff_attention(qa, ka, va, lam, lam_init, subln_w)
    out_b = chunk_band_attention(qb, kb, vb, rel_bias)
    merged = gates[:, :, 0] * (out_a @ w_branch_a) + gates[:, :, 1] * (out_b @ w_branch_b)
    return merged @ w_out

def moe_ffn(h, w_router, b_router, w_exp_in, b_exp_in, w_exp_out, b_exp_out):
    B, S, D = h.shape
    t = h.reshape(-1, D)
    n_tok = t.shape[0]
    logits = (t @ w_router + b_router).astype(jnp.float32)
    top_val, top_idx = lax.top_k(logits, TOP_K)
    gate_w = jax.nn.softmax(top_val, axis=-1).astype(h.dtype)

    n_slots = n_tok * TOP_K
    e_flat = top_idx.reshape(-1).astype(jnp.int32)
    tok_flat = jnp.arange(n_slots, dtype=jnp.int32) // TOP_K
    order = jnp.argsort(e_flat)
    e_sorted = e_flat[order]
    counts = jnp.bincount(e_flat, length=N_EXPERTS).astype(jnp.int32)
    padded = (counts + EXPERT_BLOCK - 1) // EXPERT_BLOCK * EXPERT_BLOCK
    start = jnp.cumsum(counts) - counts
    pend = jnp.cumsum(padded)
    pstart = pend - padded
    rank = jnp.arange(n_slots, dtype=jnp.int32) - start[e_sorted]
    dest_sorted = pstart[e_sorted] + rank
    buf_len = (-(-n_slots // EXPERT_BLOCK)) * EXPERT_BLOCK + N_EXPERTS * EXPERT_BLOCK
    n_blocks = buf_len // EXPERT_BLOCK
    buf_tok = jnp.full((buf_len,), n_tok, jnp.int32).at[dest_sorted].set(tok_flat[order])
    dest = jnp.zeros((n_slots,), jnp.int32).at[order].set(dest_sorted)
    block_start = jnp.arange(n_blocks, dtype=jnp.int32) * EXPERT_BLOCK
    block_exp = jnp.minimum(jnp.searchsorted(pend, block_start, side='right'), N_EXPERTS - 1).astype(jnp.int32)
    t_pad = jnp.concatenate([t, jnp.zeros((1, D), t.dtype)], axis=0)

    def expert_block(args):
        tok_idx, e = args
        xb = t_pad[tok_idx]
        hb = xb @ w_exp_in[e] + b_exp_in[e]
        g = jnp.minimum(hb[:, :D_FF], SWIGLU_LIMIT)
        u = jnp.clip(hb[:, D_FF:], -SWIGLU_LIMIT, SWIGLU_LIMIT)
        a = g * jax.nn.sigmoid(SWIGLU_ALPHA * g) * (u + 1.0)
        return a @ w_exp_out[e] + b_exp_out[e]

    y_buf = lax.map(expert_block, (buf_tok.reshape(n_blocks, EXPERT_BLOCK), block_exp)).reshape(buf_len, D)
    y_slot = y_buf[dest].reshape(n_tok, TOP_K, D)
    y = jnp.einsum('nk,nkd->nd', gate_w, y_slot)
    return y.reshape(B, S, D)

def first_inputs(seed: int = 0) -> dict:
    key = jax.random.key(seed)
    ks = jax.random.split(key, 24)
    L, D, E, F = DEPTH, D_MODEL, N_EXPERTS, D_FF
    nrm = lambda k, shape: jax.random.normal(k, shape, jnp.float32)
    col_scale = np.ones((IN_COLS,), np.float32)
    col_scale[2 * WIDTH_A:3 * WIDTH_A] = DEEPNORM_BETA
    col_scale[3 * WIDTH_A + 2 * WIDTH_B:3 * WIDTH_A + 3 * WIDTH_B] = DEEPNORM_BETA
    return {
        "x": nrm(ks[0], (BATCH, SEQ, D)),
        "ln_in_g": 1.0 + 0.05 * nrm(ks[1], (D,)),
        "ln_in_b": 0.02 * nrm(ks[2], (D,)),
        "w_in": nrm(ks[3], (L, D, IN_COLS)) * (D ** -0.5) * jnp.asarray(col_scale),
        "b_gate": 0.02 * nrm(ks[4], (L, 2 * D)),
        "lambda_q1": 0.1 * nrm(ks[5], (L, HEAD_DIM_A)),
        "lambda_k1": 0.1 * nrm(ks[6], (L, HEAD_DIM_A)),
        "lambda_q2": 0.1 * nrm(ks[7], (L, HEAD_DIM_A)),
        "lambda_k2": 0.1 * nrm(ks[8], (L, HEAD_DIM_A)),
        "subln_w": 1.0 + 0.05 * nrm(ks[9], (L, 2 * HEAD_DIM_A)),
        "rel_bias": 0.1 * nrm(ks[10], (L, N_HEADS_B, 2 * REL_CLIP + 1)),
        "w_branch_a": nrm(ks[11], (L, WIDTH_A, D)) * (WIDTH_A ** -0.5) * DEEPNORM_BETA,
        "w_branch_b": nrm(ks[12], (L, WIDTH_B, D)) * (WIDTH_B ** -0.5) * DEEPNORM_BETA,
        "w_out": nrm(ks[13], (L, D, D)) * (D ** -0.5) * DEEPNORM_BETA,
        "ln1_g": 1.0 + 0.05 * nrm(ks[14], (L, D)),
        "ln1_b": 0.02 * nrm(ks[15], (L, D)),
        "w_router": nrm(ks[16], (L, D, E)) * (D ** -0.5),
        "b_router": 0.01 * nrm(ks[17], (L, E)),
        "w_exp_in": nrm(ks[18], (L, E, D, 2 * F)) * (D ** -0.5) * DEEPNORM_BETA,
        "b_exp_in": 0.01 * nrm(ks[19], (L, E, 2 * F)),
        "w_exp_out": nrm(ks[20], (L, E, F, D)) * (F ** -0.5) * DEEPNORM_BETA,
        "b_exp_out": 0.01 * nrm(ks[21], (L, E, D)),
        "ln2_g": 1.0 + 0.05 * nrm(ks[22], (L, D)),
        "ln2_b": 0.02 * nrm(ks[23], (L, D)),
    }

def first_block(x, ln_in_g, ln_in_b, w_in, b_gate, lambda_q1, lambda_k1, lambda_q2, lambda_k2,
              subln_w, rel_bias, w_branch_a, w_branch_b, w_out, ln1_g, ln1_b,
              w_router, b_router, w_exp_in, b_exp_in, w_exp_out, b_exp_out, ln2_g, ln2_b):
    h = layer_norm(x, ln_in_g, ln_in_b)
    for l in range(DEPTH):
        lam_init = 0.8 - 0.6 * math.exp(-0.3 * l)
        m = gated_mixer(h, w_in[l], b_gate[l], lambda_q1[l], lambda_k1[l], lambda_q2[l], lambda_k2[l],
                        subln_w[l], rel_bias[l], w_branch_a[l], w_branch_b[l], w_out[l], lam_init)
        h = layer_norm(DEEPNORM_ALPHA * h + m, ln1_g[l], ln1_b[l])
        f = moe_ffn(h, w_router[l], b_router[l], w_exp_in[l], b_exp_in[l], w_exp_out[l], b_exp_out[l])
        h = layer_norm(DEEPNORM_ALPHA * h + f, ln2_g[l], ln2_b[l])
    return h


DEPTH_2 = 2

CONV_DIM = D_MODEL // 2
CONV_WIDTH = 3
HG_HEADS = 4
HG_DK = 128
HG_DV = (D_MODEL // 2) // HG_HEADS
HG_FDIM = HG_HEADS * HG_DK
HG_WIDTH = HG_HEADS * HG_DV
SB_HEADS = 16
SB_HEAD_DIM = D_MODEL // SB_HEADS
SB_WIDTH = SB_HEADS * SB_HEAD_DIM
D_FF_2 = 4 * D_MODEL
N_EVEN = (DEPTH_2 + 1) // 2
N_ODD = DEPTH_2 // 2
AB_IN = 3 * CONV_DIM + 2 * HG_FDIM + 2 * HG_WIDTH
AB_MIX = CONV_DIM + HG_WIDTH
AB_SPLITS = [CONV_DIM, 2 * CONV_DIM, 3 * CONV_DIM,
             3 * CONV_DIM + HG_FDIM, 3 * CONV_DIM + 2 * HG_FDIM,
             3 * CONV_DIM + 2 * HG_FDIM + HG_WIDTH]
EPS = 1e-6


def rms_norm_2(x, g):
    xf = x.astype(jnp.float32)
    y = xf * lax.rsqrt(jnp.mean(xf * xf, axis=-1, keepdims=True) + EPS)
    return (y * g.astype(jnp.float32)).astype(x.dtype)

def causal_depthwise_conv(u, w):
    width, ch = w.shape
    return lax.conv_general_dilated(
        u, w[:, None, :], window_strides=(1,), padding=[(width - 1, 0)],
        dimension_numbers=('NWC', 'WIO', 'NWC'), feature_group_count=ch)

def hgrn2_chunkwise(q, k, v, log_f):
    B, S, H, Dk = q.shape
    Dv = v.shape[-1]
    n = S // CHUNK

    def to_chunks(t):
        return t.reshape(B, n, CHUNK, H, t.shape[-1]).transpose(1, 0, 3, 2, 4)

    qc, kc, vc, gc = to_chunks(q), to_chunks(k), to_chunks(v), to_chunks(log_f)
    bc = jnp.cumsum(gc, axis=3)
    causal = jnp.tril(jnp.ones((CHUNK, CHUNK), dtype=bool))

    def step(state, inp):
        q_, k_, v_, b_ = inp
        inter = jnp.einsum('bhtk,bhkv->bhtv', q_ * jnp.exp(b_), state)
        diff = jnp.where(causal[None, None, :, :, None],
                         b_[:, :, :, None, :] - b_[:, :, None, :, :], -jnp.inf)
        decay = jnp.exp(diff)
        scores = jnp.einsum('bhtk,bhsk,bhtsk->bhts', q_, k_, decay)
        intra = jnp.einsum('bhts,bhsv->bhtv', scores, v_)
        b_last = b_[:, :, -1:, :]
        new_state = (jnp.exp(b_last[:, :, 0, :])[..., None] * state
                     + jnp.einsum('bhsk,bhsv->bhkv', k_ * jnp.exp(b_last - b_), v_))
        return new_state, inter + intra

    init = jnp.zeros((B, H, Dk, Dv), jnp.float32)
    _, out = lax.scan(step, init, (qc, kc, vc, bc))
    return out.transpose(1, 0, 3, 2, 4).reshape(B, S, H, Dv)

def stick_breaking_attention(q, k, v):
    S = q.shape[2]
    scale = SB_HEAD_DIM ** -0.5
    outs = []
    for blk in range(S // Q_BLOCK):
        q0 = blk * Q_BLOCK
        end = q0 + Q_BLOCK
        qb = q[:, :, q0:end]
        kb = k[:, :, :end]
        vb = v[:, :, :end]
        z = jnp.einsum('bhqd,bhkd->bhqk', qb, kb) * scale
        qpos = q0 + jnp.arange(Q_BLOCK)
        kpos = jnp.arange(end)
        mask = (kpos[None, :] < qpos[:, None])[None, None]
        log_beta = jax.nn.log_sigmoid(z)
        log_one_minus = jnp.where(mask, log_beta - z, 0.0)
        later = lax.cumsum(log_one_minus, axis=3, reverse=True) - log_one_minus
        w = jnp.where(mask, jnp.exp(log_beta + later), 0.0)
        outs.append(jnp.einsum('bhqk,bhkd->bhqd', w, vb))
    return jnp.concatenate(outs, axis=2)

def mixer_conv_hgrn(h, w_in, conv_w, hg_norm, lower_bound, w_out):
    B, S, _ = h.shape
    u = h @ w_in
    a_b, a_c, a_h, hq, hf, hi, hg = jnp.split(u, AB_SPLITS, axis=-1)
    y_a = a_b * causal_depthwise_conv(a_c * a_h, conv_w)
    f = lower_bound + (1.0 - lower_bound) * jax.nn.sigmoid(hf.astype(jnp.float32))
    log_f = jnp.log(f)
    k_in = 1.0 - f
    heads_k = lambda t: t.reshape(B, S, HG_HEADS, HG_DK)
    o = hgrn2_chunkwise(heads_k(hq.astype(jnp.float32)), heads_k(k_in), 
                        hi.astype(jnp.float32).reshape(B, S, HG_HEADS, HG_DV), heads_k(log_f))
    o = rms_norm_2(o, hg_norm.reshape(HG_HEADS, HG_DV))
    y_b = (o.reshape(B, S, HG_WIDTH) * jax.nn.silu(hg.astype(jnp.float32))).astype(h.dtype)
    return jnp.concatenate([y_a, y_b], axis=-1) @ w_out

def mixer_stick_breaking(h, w_qkv, q_norm, k_norm, w_out):
    B, S, _ = h.shape
    qkv = (h @ w_qkv).reshape(B, S, 3, SB_HEADS, SB_HEAD_DIM)
    q = rms_norm_2(qkv[:, :, 0], q_norm)
    k = rms_norm_2(qkv[:, :, 1], k_norm)
    v = qkv[:, :, 2]
    to_bhsd = lambda t: t.astype(jnp.float32).transpose(0, 2, 1, 3)
    o = stick_breaking_attention(to_bhsd(q), to_bhsd(k), to_bhsd(v))
    o = o.transpose(0, 2, 1, 3).reshape(B, S, SB_WIDTH).astype(h.dtype)
    return o @ w_out

def second_inputs(seed: int = 0) -> dict:
    key = jax.random.key(seed)
    ks = jax.random.split(key, 20)
    nrm = lambda k, shape, s: jax.random.normal(k, shape, jnp.float32) * s
    gain = lambda k, shape: 1.0 + 0.02 * jax.random.normal(k, shape, jnp.float32)
    return {
        "x": nrm(ks[0], (BATCH, SEQ, D_MODEL), 1.0),
        "c": nrm(ks[1], (BATCH, D_MODEL), 1.0),
        "ada_w": nrm(ks[2], (DEPTH_2, D_MODEL, 6 * D_MODEL), 0.5 * D_MODEL ** -0.5),
        "ada_b": nrm(ks[3], (DEPTH_2, 6 * D_MODEL), 0.02),
        "norm_mix": gain(ks[4], (DEPTH_2, D_MODEL)),
        "norm_mlp": gain(ks[5], (DEPTH_2, D_MODEL)),
        "w_in_ab": nrm(ks[6], (N_EVEN, D_MODEL, AB_IN), D_MODEL ** -0.5),
        "conv_w": nrm(ks[7], (N_EVEN, CONV_WIDTH, CONV_DIM), CONV_WIDTH ** -0.5),
        "hg_norm": gain(ks[8], (N_EVEN, HG_WIDTH)),
        "lb_logits": nrm(ks[9], (DEPTH_2 + 1, HG_FDIM), 0.1),
        "w_out_ab": nrm(ks[10], (N_EVEN, AB_MIX, D_MODEL), AB_MIX ** -0.5),
        "w_qkv": nrm(ks[11], (N_ODD, D_MODEL, 3 * SB_WIDTH), D_MODEL ** -0.5),
        "q_norm": gain(ks[12], (N_ODD, SB_HEAD_DIM)),
        "k_norm": gain(ks[13], (N_ODD, SB_HEAD_DIM)),
        "w_out_c": nrm(ks[14], (N_ODD, SB_WIDTH, D_MODEL), SB_WIDTH ** -0.5),
        "mlp_w1": nrm(ks[15], (DEPTH_2, D_MODEL, D_FF_2), D_MODEL ** -0.5),
        "mlp_w2": nrm(ks[16], (DEPTH_2, D_FF_2, D_MODEL), D_FF_2 ** -0.5),
    }

def second_block(x, c, ada_w, ada_b, norm_mix, norm_mlp, w_in_ab, conv_w, hg_norm,
              lb_logits, w_out_ab, w_qkv, q_norm, k_norm, w_out_c, mlp_w1, mlp_w2):
    c_act = jax.nn.silu(c)
    lower_bounds = jnp.cumsum(jax.nn.softmax(lb_logits.astype(jnp.float32), axis=0), axis=0)
    for layer in range(DEPTH_2):
        mod = c_act @ ada_w[layer] + ada_b[layer]
        shift1, scale1, gate1, shift2, scale2, gate2 = jnp.split(mod[:, None, :], 6, axis=-1)
        h = rms_norm_2(x, norm_mix[layer]) * (1.0 + scale1) + shift1
        j = layer // 2
        if layer % 2 == 0:
            y = mixer_conv_hgrn(h, w_in_ab[j], conv_w[j], hg_norm[j],
                                lower_bounds[layer], w_out_ab[j])
        else:
            y = mixer_stick_breaking(h, w_qkv[j], q_norm[j], k_norm[j], w_out_c[j])
        x = x + gate1 * y
        h = rms_norm_2(x, norm_mlp[layer]) * (1.0 + scale2) + shift2
        x = x + gate2 * (jnp.square(jax.nn.relu(h @ mlp_w1[layer])) @ mlp_w2[layer])
    return x


def setup_inputs(seed=0):
    out = dict(first_inputs(seed))
    for name, value in second_inputs(seed + 1).items():
        if name != "x":
            out[name + "_2"] = value
    return out


def reference(
    x, ln_in_g, ln_in_b, w_in, b_gate, lambda_q1, lambda_k1, lambda_q2, lambda_k2, subln_w,
    rel_bias, w_branch_a, w_branch_b, w_out, ln1_g, ln1_b, w_router, b_router, w_exp_in,
    b_exp_in, w_exp_out, b_exp_out, ln2_g, ln2_b, c_2, ada_w_2, ada_b_2, norm_mix_2, norm_mlp_2,
    w_in_ab_2, conv_w_2, hg_norm_2, lb_logits_2, w_out_ab_2, w_qkv_2, q_norm_2, k_norm_2,
    w_out_c_2, mlp_w1_2, mlp_w2_2,
):
    x = first_block(
        x, ln_in_g, ln_in_b, w_in, b_gate, lambda_q1, lambda_k1, lambda_q2, lambda_k2, subln_w,
        rel_bias, w_branch_a, w_branch_b, w_out, ln1_g, ln1_b, w_router, b_router, w_exp_in,
        b_exp_in, w_exp_out, b_exp_out, ln2_g, ln2_b,
    )
    return second_block(
        x, c_2, ada_w_2, ada_b_2, norm_mix_2, norm_mlp_2, w_in_ab_2, conv_w_2, hg_norm_2,
        lb_logits_2, w_out_ab_2, w_qkv_2, q_norm_2, k_norm_2, w_out_c_2, mlp_w1_2, mlp_w2_2,
    )


_drawn_inputs = setup_inputs


def setup_inputs(seed=0):
    import zlib

    import numpy as np

    out = dict(_drawn_inputs(seed))
    spreads = {}
    factors = {'b_gate': 8.0,
     'lambda_q1': 24.707,
     'lambda_k1': 3.845,
     'lambda_q2': 4.682,
     'lambda_k2': 6.963,
     'subln_w': 5.234,
     'rel_bias': 8.0,
     'w_branch_b': 2.9,
     'b_router': 8.0,
     'b_exp_in': 8.0,
     'b_exp_out': 8.0,
     'norm_mix_2': 4.687,
     'norm_mlp_2': 23.16,
     'hg_norm_2': 64.0,
     'lb_logits_2': 7.597,
     'q_norm_2': 200.0,
     'k_norm_2': 200.0,
     'w_qkv_2': 8.0,
     'w_out_c_2': 8.0}
    for name, (base, spread) in spreads.items():
        noise = np.random.default_rng([zlib.crc32(name.encode()), seed]).standard_normal(out[name].shape)
        drawn = base * np.exp(spread * noise) if base else spread * noise
        out[name] = __import__('jax').numpy.asarray(drawn.astype(out[name].dtype))
    for name, factor in factors.items():
        out[name] = (out[name] * factor).astype(out[name].dtype)
    return out
```

```python
import math
from contextlib import ExitStack

import concourse.bass as bass
import concourse.mybir as mybir

F32 = mybir.dt.float32
F32R = mybir.dt.float32r
I32 = mybir.dt.int32
ALU = mybir.AluOpType
ACT = mybir.ActivationFunctionType
AX = mybir.AxisListType.X
ds = bass.ds

P = 128
D = 1024
S = 256
TT = S // P
KT = D // P
COLS = 512
CK = 4
RING = 4
AHEAD = 2
LOADED = AHEAD + RING
NEG = -1e30
EPS_LN = 1e-5
EPS_RMS = 1e-6
SCALE = 64 ** -0.5

HA, DA = 4, 64
HB = 8
CHUNK = 64
CLIP = 128
LAM_INIT = 0.8 - 0.6 * math.exp(-0.3 * 0)
RES = 2.0 ** 0.25
E = 32
TOPK = 4
CAP = 64
PASSES = S // CAP


def bcast(ap, shape):
    return ap.to_broadcast(shape)


class Core:

    def __init__(self, nc, ctx, dram):
        self.nc, self.ctx, self.dram = nc, ctx, dram
        self.chunk = 0
        self.stream = []
        self.norms = 0
        self.turns = 0
        self.chain = 0

    def sb(self, name, shape, dt=F32, ctx=None):
        return (ctx or self.ctx).enter_context(self.nc.sbuf_tensor(name, shape, dt))

    def sem(self, name):
        return self.ctx.enter_context(self.nc.semaphore(name))


class Stream:

    def __init__(self, c, name, first, first_lap):
        self.raw, self.wh, self.wl = c.raw, c.wh, c.wl
        self.first, self.first_lap = first, first_lap
        self.arrived = [c.sem(f"{name}arrived{s}") for s in range(RING)]
        self.high_ready = c.sem(name + "high_ready")
        self.low_ready = c.sem(name + "low_ready")
        self.used = c.sem(name + "used")


def rows_cols(matrix, row, col):
    return matrix[ds(row, CK * P), ds(col, COLS)].rearrange("(k p) n -> p k n", p=P)


def make(nc, ctx, dram):
    c = Core(nc, ctx, dram)
    c.ident = c.sb("ident", [P, P])
    c.raw = c.sb("raw", [P, RING, CK, COLS])
    c.wh = c.sb("wh", [P, RING, CK, COLS], F32R)
    c.wl = c.sb("wl", [P, RING, CK, COLS], F32R)
    c.xth = c.sb("xth", [P, KT, S], F32R)
    c.xtl = c.sb("xtl", [P, KT, S], F32R)
    c.x = c.sb("x", [P, TT, D])
    c.stats = c.sb("stats", [P, TT, 2, 6])
    c.mv = c.sb("mv", [P, TT, 2])
    c.rv = c.sb("rv", [P, TT])
    c.rs = c.sb("rs", [P, TT])
    c.psum = ctx.enter_context(nc.psum_tensor("banks", [P, 8, COLS], F32))
    c.bank = [c.psum[:, b, :] for b in range(8)]
    c.arrived = [c.sem(f"arrived{s}") for s in range(RING)]
    c.high_ready = c.sem("high_ready")
    c.low_ready = c.sem("low_ready")
    c.used = c.sem("used")
    c.rv_ready = c.sem("rv_ready")
    c.rs_ready = c.sem("rs_ready")
    c.turned = c.sem("turned")
    c.xh_ready = c.sem("xh_ready")
    c.xl_ready = c.sem("xl_ready")
    c.vec_step = c.sem("vec_step")
    return c



def load_chunk(c, sp, n, slot, src):
    if not isinstance(n, int) or n >= RING:
        sp.wait_ge(c.low_ready, n - RING + 1)
    sp.dma_start(c.raw[:, slot], src).then_inc(c.arrived[slot], 16)


def turn_of(n, slot, static):
    return n // RING + 1 if isinstance(n, int) else (static - slot) // RING + 1


def split_high(c, act, n, lap, slot):
    act.wait_ge(c.arrived[slot], lap * 16)
    if not isinstance(n, int) or n >= RING:
        act.wait_ge(c.used, n - RING + 1)
    act.activation(c.wh[:, slot], c.raw[:, slot], ACT.Copy).then_inc(c.high_ready, 1)


def split_low(c, dve, n, slot):
    dve.wait_ge(c.high_ready, n + 1)
    dve.tensor_tensor(c.wl[:, slot], c.raw[:, slot], c.wh[:, slot].bitcast(F32),
                      ALU.subtract).then_inc(c.low_ready, 1)


def multiply_rows(c, pe, n, slot, k0, banks, first, last, xh=None, xl=None, long=False):
    xh, xl = xh or c.xth, xl or c.xtl
    pe.wait_ge(c.low_ready, n + 1)
    for k in range(CK):
        for m in range(len(banks)):
            toks = slice(m * P, m * P + P)
            for j, (x, w) in enumerate(((xh, c.wh), (xh, c.wl), (xl, c.wh))):
                mm = pe.matmul(banks[m][:, :], x[:, k0 + k, toks], w[:, slot, k],
                               start=first and k == 0 and j == 0, stop=last and k == CK - 1 and j == 2,
                               skip_group_check=long)
    mm.then_inc(c.used, 1)


def multiply_cols(c, pe, n, slot, k0, banks, first, last, xh=None, xl=None):
    xh, xl = xh or c.xth, xl or c.xtl
    pe.wait_ge(c.low_ready, n + 1)
    for k in range(CK):
        for b in range(COLS // P):
            out = banks[b // 2][:, (b % 2) * S:(b % 2) * S + S]
            cols = slice(b * P, b * P + P)
            for j, (w, x) in enumerate(((c.wh, xh), (c.wh, xl), (c.wl, xh))):
                mm = pe.matmul(out, w[:, slot, k, cols], x[:, k0 + k, :],
                               start=first and k == 0 and j == 0 and b % 2 == 0,
                               stop=last and k == CK - 1 and j == 2, skip_group_check=True)
    mm.then_inc(c.used, 1)



def linked(c, dve, ins):
    c.chain += 1
    ins.then_inc(c.vec_step, 1)
    dve.wait_ge(c.vec_step, c.chain)


def root_act(c, act, v):
    act.wait_ge(c.rv_ready, v + 1)
    act.activation(c.rs[:, :], c.rv[:, :], ACT.Sqrt).then_inc(c.rs_ready, 1)


def layer_norm_dve(c, dve, v, x, gain, shift):
    for m in range(TT):
        for h in range(2):
            st = dve.bn_stats(c.stats[:, m, h, :], x[:, m, h * 512:h * 512 + 512])
    linked(c, dve, st)
    for m in range(TT):
        agg = dve.bn_aggr(c.mv[:, m, :], c.stats[:, m].rearrange("p a b -> p (a b)"))
    linked(c, dve, agg)
    linked(c, dve, dve.tensor_scalar(c.rv[:, :], c.mv[:, :, 1], EPS_LN, None, ALU.add))
    dve.reciprocal(c.rv[:, :], c.rv[:, :]).then_inc(c.rv_ready, 1)
    dve.wait_ge(c.rs_ready, v + 1)
    for m in range(TT):
        last = dve.tensor_scalar(x[:, m], x[:, m], c.mv[:, m, 0:1], c.rs[:, m:m + 1], ALU.subtract, ALU.mult)
    linked(c, dve, last)
    for m in range(TT):
        last = dve.tensor_tensor(x[:, m], x[:, m], gain, ALU.mult)
    linked(c, dve, last)
    for m in range(TT):
        last = dve.tensor_tensor(x[:, m], x[:, m], shift, ALU.add)
    linked(c, dve, last)


def turn_pe(c, pe, v, x, banks, kt=KT):
    for k in range(kt):
        for m in range(TT):
            t = pe.transpose(banks[k // 2][:, (k % 2) * S + m * P:(k % 2) * S + m * P + P],
                             x[:, m, k * P:k * P + P], c.ident[:, :])
        if k % 2:
            t.then_inc(c.turned, 1)


def turn_act(c, act, v, banks, kt=KT, at=0):
    for b in range(kt // 2):
        act.wait_ge(c.turned, v + b + 1)
        act.activation(c.xth[:, at + 2 * b:at + 2 * b + 2, :], banks[b][:, :].rearrange("p (k s) -> p k s", k=2),
                       ACT.Copy).then_inc(c.xh_ready, 1)


def turn_dve(c, dve, v, banks, kt=KT, at=0):
    for b in range(kt // 2):
        dve.wait_ge(c.xh_ready, v + b + 1)
        part = slice(at + 2 * b, at + 2 * b + 2)
        dve.tensor_tensor(c.xtl[:, part, :], banks[b][:, :].rearrange("p (k s) -> p k s", k=2),
                          c.xth[:, part, :].bitcast(F32), ALU.subtract).then_inc(c.xl_ready, 1)


def turned_all(c, pe, v, kt=KT):
    pe.wait_ge(c.xl_ready, v + kt // 2)


def over_partitions(vector, n):
    return vector.rearrange("(a n) -> a n", a=1).broadcast(0, n)



def phase_in(c):
    nc, d = c.nc, c.dram
    W = c.chunk
    panels = 10
    after = panels * 2
    w_in, wa, wb = d["w_in"][0], d["w_branch_a"][0], d["w_branch_b"][0]
    c.qka = c.sb("qka", [P, 2, 4, S], ctx=c.mix)
    c.qkb = c.sb("qkb", [P, 2, 4, S], ctx=c.mix)
    c.va = c.sb("va", [P, TT, 512], ctx=c.mix)
    c.vb = c.sb("vb", [P, TT, 512], ctx=c.mix)
    c.gates = c.sb("gates", [P, TT, 2 * D], ctx=c.mix)
    c.flip = c.sb("flip", [P, P], ctx=c.mix)
    c.mask = c.sb("mask", [P, TT, S], ctx=c.mix)
    c.alibi = c.sb("alibi", [P, HA, TT, S], ctx=c.mix)
    c.rel = c.sb("rel", [P, HB, 384], ctx=c.mix)
    c.lam_in = c.sb("lam_in", [P, 2, 2, DA], ctx=c.mix)
    c.subln = c.sb("subln", [P, 128], ctx=c.mix)
    rel_rows = nc.dram_tensor("rel_rows", [HB, 512], F32).ap()
    x_loaded = c.sem("x_loaded")
    bias_loaded = c.sem("bias_loaded")
    rel_stored = c.sem("rel_stored")
    c.rel_loaded = c.sem("rel_loaded")
    pool_step = c.sem("pool_step")
    c.bias_ready = c.sem("bias_ready")
    c.small_loaded = c.sem("small_loaded")
    norm_loaded = c.sem("norm_loaded")
    gate_loaded = c.sem("gate_loaded")
    ident_step = c.sem("ident_step")
    normed = c.sem("normed")
    evacuated = c.sem("in_evacuated")
    gates_ready = c.gates_ready = c.sem("gates_ready")
    kinds = "TTNTTNNNNN"
    outs = [c.qka[:, 0], c.qka[:, 1], c.va, c.qkb[:, 0], c.qkb[:, 1], c.vb]

    with ExitStack() as local, nc.Block() as block:
        gain = c.sb("ln_in_gain", [P, D], ctx=local)
        shift = c.sb("ln_in_shift", [P, D], ctx=local)
        rel_wide = c.sb("rel_wide", [HB, 512], ctx=local)
        dist = c.sb("dist", [P, TT, S], ctx=local)
        away = c.sb("away", [P, TT, S], ctx=local)

        @block.sync
        def _(sp):
            for m in range(TT):
                sp.dma_start(c.x[:, m], d["x"][0, m * P:m * P + P, :]).then_inc(x_loaded, 16)
            for n in range(LOADED):
                load_chunk(c, sp, W + n, n % RING, rows_cols(w_in, n % 2 * 512, n // 2 * COLS))
            with sp.Fori(0, 3) as i:
                for j in range(4):
                    load_chunk(c, sp, i * 4 + (W + LOADED + j), (LOADED + j) % RING,
                               rows_cols(w_in, j % 2 * 512, i * (2 * COLS) + (3 + j // 2) * COLS))
            for n in range(18, after):
                load_chunk(c, sp, W + n, n % RING, rows_cols(w_in, n % 2 * 512, n // 2 * COLS))
            for n in range(after, after + 4):
                load_chunk(c, sp, W + n, n % RING, rows_cols((wa, wb)[n % 2], 0, (n - after) // 2 * COLS))
            for n in range(after + 4, after + LOADED):
                load_chunk(c, sp, W + n, n % RING, rows_cols(d["w_out"][0], n % 2 * 512, 0))

        @block.gpsimd
        def _(pool):
            pool.memset(c.ident[:, :], 0.0).then_inc(ident_step, 1)
            pool.wait_ge(ident_step, 1)
            pool.affine_select(out=c.ident[:, :], in_=c.ident[:, :], compare_op=ALU.not_equal, fill=1.0, base=0,
                               pattern=[[-1, P]], channel_multiplier=1).then_inc(ident_step, 1)
            steps = 0

            def done(ins):
                nonlocal steps
                steps += 1
                ins.then_inc(pool_step, 1)
                pool.wait_ge(pool_step, steps)

            pool.wait_ge(bias_loaded, 16)
            lo, hi = S - 1 - CLIP, S - 1 + CLIP
            pool.tensor_copy(rel_wide[:, 0:lo], rel_wide[:, lo:lo + 1].to_broadcast([HB, lo]))
            done(pool.tensor_copy(rel_wide[:, hi + 1:512], rel_wide[:, hi:hi + 1].to_broadcast([HB, 511 - hi])))
            pool.dma_start(rel_rows, rel_wide[:, :]).then_inc(rel_stored, 16)
            pool.wait_ge(rel_stored, 16)
            for h in range(HB):
                pool.dma_start(c.rel[:, h, :], bass.AP(tensor=rel_rows.tensor, offset=h * 512, ap=[[1, P], [1, 384]])
                               ).then_inc(c.rel_loaded, 16)
            done(pool.memset(c.flip[:, :], 0.0))
            done(pool.affine_select(out=c.flip[:, :], in_=c.flip[:, :], compare_op=ALU.not_equal, fill=1.0,
                                    base=1 - P, pattern=[[1, P]], channel_multiplier=1))
            done(pool.memset(c.mask[:, :, :], 0.0))
            for m in range(TT):
                done(pool.memset(c.mask[0:CHUNK, m, m * P + CHUNK:S], NEG))
                if m < TT - 1:
                    done(pool.memset(c.mask[CHUNK:P, m, m * P + P:S], NEG))
            done(pool.iota(dist[:, :, :], pattern=[[P, TT], [-1, S]], base=0, channel_multiplier=1,
                           allow_small_or_imprecise_dtypes=True))
            done(pool.tensor_scalar(away[:, :, :], dist[:, :, :], -1.0, None, ALU.mult))
            for t, sign in ((dist, 1), (away, -1)):
                done(pool.affine_select(out=t[:, :, :], in_=t[:, :, :], compare_op=ALU.is_ge, fill=0.0, base=0,
                                        pattern=[[sign * P, TT], [-sign, S]], channel_multiplier=sign))
            done(pool.tensor_tensor(dist[:, :, :], dist[:, :, :], away[:, :, :], ALU.add))
            for h in range(HA):
                done(pool.tensor_scalar(away[:, :, :], dist[:, :, :], -2.0 ** (-8.0 * (h + 1) / HA), None, ALU.mult))
                done(pool.tensor_tensor(c.alibi[:, h], away[:, :, :], c.mask[:, :, :], ALU.add))
            pool.sem_inc(c.bias_ready, 1)

        @block.scalar
        def _(act):
            act.dma_start(gain[:, :], d["ln_in_g"].partition_broadcast(P)).then_inc(norm_loaded, 16)
            act.dma_start(shift[:, :], d["ln_in_b"].partition_broadcast(P)).then_inc(norm_loaded, 16)
            for m in range(TT):
                act.dma_start(c.gates[:, m, :], d["b_gate"][0].partition_broadcast(P)).then_inc(gate_loaded, 16)
            act.dma_start(rel_wide[:, S - 1 - CLIP:S + CLIP], d["rel_bias"][0]).then_inc(bias_loaded, 16)
            for j, name in enumerate(("lambda_q1", "lambda_k1", "lambda_q2", "lambda_k2")):
                act.dma_start(c.lam_in[:, j // 2, j % 2, :], d[name][0].partition_broadcast(P)
                              ).then_inc(c.small_loaded, 16)
            act.dma_start(c.subln[:, :], d["subln_w"][0].partition_broadcast(P)).then_inc(c.small_loaded, 16)
            root_act(c, act, 0)
            for n in range(AHEAD):
                split_high(c, act, W + n, 1, n)
            turn_act(c, act, 0, c.bank)
            for n in range(AHEAD, after + AHEAD):
                split_high(c, act, W + n, (W + n) // RING + 1, n % RING)

        @block.vector
        def _(dve):
            dve.wait_ge(x_loaded, 16 * TT)
            dve.wait_ge(norm_loaded, 32)
            layer_norm_dve(c, dve, 0, c.x, gain[:, :], shift[:, :])
            dve.sem_inc(normed, 1)
            for n in range(AHEAD):
                split_low(c, dve, W + n, n)
            turn_dve(c, dve, 0, c.bank)
            for p in range(panels):
                for n in range(2 * p + AHEAD, 2 * p + AHEAD + 2):
                    split_low(c, dve, W + n, n % RING)
                dve.wait_ge(c.used, W + 2 * p + 2)
                banks = c.bank[p % 2 * 2:p % 2 * 2 + 2]
                if p == 6:
                    dve.wait_ge(gate_loaded, 16 * TT)
                for b in range(2):
                    if kinds[p] == "T":
                        last = dve.tensor_scalar(outs[p][:, 2 * b:2 * b + 2, :],
                                                 banks[b][:, :].rearrange("p (k s) -> p k s", k=2),
                                                 SCALE if p in (0, 3) else 1.0, None, ALU.mult)
                    elif p < 6:
                        last = dve.tensor_copy(outs[p][:, b, :], banks[b][:, :])
                    else:
                        g = slice((p - 6) * COLS, (p - 5) * COLS)
                        last = dve.tensor_tensor(c.gates[:, b, g], banks[b][:, :], c.gates[:, b, g], ALU.add)
                last.then_inc(evacuated, 1)
            dve.sem_inc(gates_ready, 1)

        @block.tensor
        def _(pe):
            pe.wait_ge(ident_step, 2)
            pe.wait_ge(normed, 1)
            turn_pe(c, pe, 0, c.x, c.bank)
            turned_all(c, pe, 0)
            for p in range(panels):
                if p >= 2:
                    pe.wait_ge(evacuated, p - 1)
                for h in range(2):
                    n = 2 * p + h
                    (multiply_cols if kinds[p] == "T" else multiply_rows)(
                        c, pe, W + n, n % RING, h * CK, c.bank[p % 2 * 2:p % 2 * 2 + 2], h == 0, h == 1)
    c.chunk += after



def phase_attend(c):
    nc, d = c.nc, c.dram
    units = 2 * HA + HB
    diff = 2 * HA
    lam_step = c.sem("lam_step")
    lam_exp = c.sem("lam_exp")
    scored = c.sem("scored")
    biased = c.sem("biased")
    maxed = c.sem("maxed")
    exped = c.sem("exped")
    weighed = c.sem("weighed")
    flipped = c.sem("flipped")
    keyed = c.sem("keyed")
    mixed = c.sem("mixed")
    kept = c.sem("kept")
    gate_act = c.sem("gate_act")
    c.gated = gate_act
    c.mixer_turned = c.sem("mixer_turned")
    o = c.o = c.sb("o", [P, TT, D], ctx=c.mix)
    sub_rv, sub_rs = c.sem("sub_rv"), c.sem("sub_rs")

    with ExitStack() as local, nc.Block() as block:
        s = c.sb("s", [P, 2, 2, S], ctx=local)
        e = s
        a = c.sb("a", [P, 2, 2, S], ctx=local)
        at = c.sb("at", [P, 2, 512], ctx=local)
        sq = e[:, :, :, :].rearrange("p a b s -> p a (b s)")
        nmax = c.sb("nmax", [P, 2, 2], ctx=local)
        total = c.sb("total", [P, 2, 2], ctx=local)
        part = c.sb("part", [P, 2], ctx=local)
        lam = c.sb("lam", [P, 4], ctx=local)
        prod = c.sb("prod", [P, 2, DA], ctx=local)
        ss = c.sb("ss", [P, TT, HA], ctx=local)

        @block.tensor
        def _(pe):
            def scores(u):
                if u >= 2:
                    pe.wait_ge(biased, u - 1)
                h, m = u % diff // 2, u % 2
                qk = c.qka if u < diff else c.qkb
                for j in range(2):
                    half = slice(j * 64, j * 64 + 64)
                    out = c.bank[2 * (u % 2) + j][:, 0:S]
                    mm = pe.matmul(out, qk[half, 0, h, m * P:m * P + P], qk[half, 1, h, :],
                                   start=True, stop=u < diff)
                    if u >= diff:
                        mm = pe.matmul(out, c.flip[:, :], c.rel[:, 2 * h + j, P - m * P:P - m * P + S],
                                       start=False, stop=True)
                mm.then_inc(scored, 1)

            def flip(u):
                pe.wait_ge(weighed, u + 1)
                if u >= 2:
                    pe.wait_ge(keyed, u - 1)
                for j in range(1 if u < diff else 2):
                    for k in range(TT):
                        t = pe.transpose(c.bank[4 + u % 2][:, (2 * j + k) * P:(2 * j + k) * P + P],
                                         a[:, u % 2, j, k * P:k * P + P], c.ident[:, :])
                t.then_inc(flipped, 1)

            def mix(u):
                pe.wait_ge(keyed, u + 1)
                if u >= 2:
                    pe.wait_ge(kept, u - 1)
                h = u % diff // 2
                for j in range(1 if u < diff else 2):
                    for k in range(TT):
                        wt = at[:, u % 2, (2 * j + k) * P:(2 * j + k) * P + P]
                        if u < diff:
                            mm = pe.matmul(c.bank[6 + u % 2][:, 0:P], wt, c.va[:, k, h * P:h * P + P],
                                           start=k == 0, stop=k == 1)
                        else:
                            v0 = (2 * h + j) * 64
                            mm = pe.matmul(c.bank[6 + u % 2][:, j * 64:j * 64 + 64], wt, c.vb[:, k, v0:v0 + 64],
                                           start=k == 0, stop=k == 1)
                mm.then_inc(mixed, 1)

            for u in range(units + 2):
                if u == diff:
                    pe.wait_ge(c.rel_loaded, 16 * HB)
                    pe.wait_ge(c.bias_ready, 1)
                if u < units:
                    scores(u)
                if u >= 2:
                    mix(u - 2)
                if 1 <= u <= units:
                    flip(u - 1)
            pe.wait_ge(c.mixer_turned, 1)
            turn_pe(c, pe, 4, o, c.bank)

        @block.scalar
        def _(act):
            act.wait_ge(lam_step, 2)
            act.activation(lam[:, 0:2], lam[:, 0:2], ACT.Exp).then_inc(lam_exp, 1)

            def exps(u):
                act.wait_ge(maxed, u + 1)
                for j in range(2):
                    x = act.activation(e[:, u % 2, j], s[:, u % 2, j], ACT.Exp, bias=nmax[:, u % 2, j:j + 1],
                                       accum_out=total[:, u % 2, j:j + 1])
                x.then_inc(exped, 1)

            def key(u):
                act.wait_ge(flipped, u + 1)
                if u >= 2:
                    act.wait_ge(mixed, u - 1)
                w = 256 if u < diff else 512
                act.activation(at[:, u % 2, 0:w], c.bank[4 + u % 2][:, 0:w], ACT.Copy).then_inc(keyed, 1)

            for u in range(units + 1):
                if u < units:
                    exps(u)
                if u >= 1:
                    key(u - 1)
            act.wait_ge(c.gates_ready, 1)
            act.activation(c.gates[:, :, :], c.gates[:, :, :], ACT.Sigmoid).then_inc(gate_act, 1)
            act.wait_ge(sub_rv, 1)
            act.activation(ss[:, :, :], ss[:, :, :], ACT.Sqrt).then_inc(sub_rs, 1)
            turn_act(c, act, 4, c.bank)

        @block.vector
        def _(dve):
            dve.wait_ge(c.small_loaded, 16 * 5)
            dve.tensor_tensor(prod[:, :, :], c.lam_in[:, :, 0], c.lam_in[:, :, 1], ALU.mult).then_inc(lam_step, 1)
            dve.wait_ge(lam_step, 1)
            dve.tensor_reduce(lam[:, 0:2], prod[:, :, :], AX, ALU.add).then_inc(lam_step, 1)
            dve.wait_ge(lam_exp, 1)
            linked(c, dve, dve.tensor_tensor(lam[:, 2:3], lam[:, 1:2], lam[:, 0:1], ALU.subtract))
            linked(c, dve, dve.tensor_scalar(lam[:, 2:3], lam[:, 2:3], -LAM_INIT, None, ALU.add))
            linked(c, dve, dve.tensor_scalar(c.subln[:, :], c.subln[:, :], 1.0 - LAM_INIT, None, ALU.mult))
            dve.wait_ge(c.bias_ready, 1)

            def bias(u):
                h, m = u % diff // 2, u % 2
                dve.wait_ge(scored, u + 1)
                if u >= 2:
                    dve.wait_ge(weighed, u - 1)
                b = c.alibi[:, h, m] if u < diff else c.mask[:, m]
                dve.tensor_tensor(s[:, u % 2], c.psum[:, 2 * (u % 2):2 * (u % 2) + 2, 0:S],
                                  b.unsqueeze(1).to_broadcast([P, 2, S]), ALU.add).then_inc(biased, 1)
                dve.wait_ge(biased, u + 1)
                dve.tensor_reduce(nmax[:, u % 2, :], s[:, u % 2], AX, ALU.max, negate=True).then_inc(maxed, 1)

            def weigh(u):
                dve.wait_ge(exped, u + 1)
                if u >= 1:
                    dve.wait_ge(weighed, u)
                if u >= 2:
                    dve.wait_ge(flipped, u - 1)
                linked(c, dve, dve.reciprocal(part[:, :], total[:, u % 2]))
                if u < diff:
                    linked(c, dve, dve.tensor_tensor(part[:, 1:2], part[:, 1:2], lam[:, 2:3], ALU.mult))
                    linked(c, dve, dve.tensor_scalar(a[:, u % 2, 1], e[:, u % 2, 1], part[:, 1:2], None, ALU.mult))
                    dve.scalar_tensor_tensor(a[:, u % 2, 0], e[:, u % 2, 0], part[:, 0:1], a[:, u % 2, 1],
                                             ALU.mult, ALU.add).then_inc(weighed, 1)
                else:
                    dve.tensor_tensor(a[:, u % 2], e[:, u % 2], part[:, :].unsqueeze(2).to_broadcast([P, 2, S]),
                                      ALU.mult).then_inc(weighed, 1)

            def keep(u):
                dve.wait_ge(mixed, u + 1)
                h, m = u // 2, u % 2
                dve.tensor_copy(o[:, m, h * P:h * P + P], c.bank[6 + u % 2][:, 0:P]).then_inc(kept, 1)

            for u in range(units + 2):
                if u < units:
                    bias(u)
                if 1 <= u <= units:
                    weigh(u - 1)
                if u >= 2:
                    keep(u - 2)
            oa = o[:, :, 0:512]
            dve.wait_ge(kept, units)
            linked(c, dve, dve.tensor_tensor(sq[:, :, :], oa, oa, ALU.mult))
            for m in range(TT):
                last = dve.tensor_reduce(ss[:, m], sq[:, m].rearrange("p (h n) -> p h n", h=HA), AX, ALU.add)
            linked(c, dve, last)
            linked(c, dve, dve.tensor_scalar(ss[:, :, :], ss[:, :, :], 1.0 / 128, EPS_LN, ALU.mult, ALU.add))
            dve.reciprocal(ss[:, :, :], ss[:, :, :]).then_inc(sub_rv, 1)
            dve.wait_ge(sub_rs, 1)
            for m in range(TT):
                oh = o[:, m, 0:512].rearrange("p (h n) -> p h n", h=HA)
                linked(c, dve, dve.tensor_tensor(oh, oh, ss[:, m].unsqueeze(2).to_broadcast([P, HA, 128]), ALU.mult))
                last = dve.tensor_tensor(oh, oh, c.subln[:, :].unsqueeze(1).to_broadcast([P, HA, 128]), ALU.mult)
            linked(c, dve, last)
            dve.sem_inc(c.mixer_turned, 1)
            turn_dve(c, dve, 4, c.bank)


def make_routing(c):
    c.pick = c.sb("pick", [P, TT, E], ctx=c.moe)
    c.weight = c.sb("weight", [P, TT, E], ctx=c.moe)
    c.place = c.sb("place", [P, TT, PASSES, E], ctx=c.moe)
    c.spill = c.sb("spill", [1, PASSES * E + 1], I32, ctx=c.moe)
    c.counts = c.sb("counts", [P, E], ctx=c.moe)



def phase_merge(c):
    nc, d = c.nc, c.dram
    W = c.chunk
    after = 8
    w_out, w_e = d["w_out"][0], d["w_exp_in"][0, 0]
    ln_loaded = c.sem("ln1_loaded")
    merged = c.sem("merged")
    added = c.sem("added")
    h_ready = c.sem("h_ready")
    logits_done = c.sem("logits_done")
    top_ready = c.sem("top_ready")
    exp_ready = c.sem("exp_ready")
    picked = c.sem("picked")
    ranked = c.sem("ranked")
    tri_step = c.sem("tri_step")

    with ExitStack() as local, nc.Block() as block:
        mg = c.o
        gb = c.sb("gb", [P, TT, COLS], ctx=local)
        norm = c.qka[:, :, :, :].rearrange("p j h s -> p j (h s)")
        wr = c.sb("wr", [P, KT, E], ctx=local)
        br = c.sb("br", [P, E], ctx=local)
        before = c.sb("before", [P, P], ctx=local)
        ones = c.sb("ones", [P, P], ctx=local)
        number = c.sb("number", [P, E], ctx=local)
        lg = c.sb("lg", [P, TT, E], ctx=local)
        top = c.sb("top", [P, TT, 8], ctx=local)
        index = c.sb("index", [P, TT, 8], mybir.dt.uint32, ctx=local)
        indexf = c.sb("indexf", [P, TT, 8], ctx=local)
        gate = c.sb("gate", [P, TT, TOPK], ctx=local)
        gsum = c.sb("gsum", [P, TT], ctx=local)
        hit = c.sb("hit", [P, TT, TOPK, E], ctx=local)
        spillf = c.sb("spillf", [1, PASSES * E + 1], ctx=local)

        @block.sync
        def _(sp):
            for n in range(LOADED, after):
                load_chunk(c, sp, W + n, n % RING, rows_cols(w_out, n % 2 * 512, (n - 4) // 2 * COLS))
            for n in range(after, after + LOADED):
                j = n - after
                load_chunk(c, sp, W + n, n % RING, rows_cols(w_e, j % 2 * 512, j // 2 * COLS))

        @block.gpsimd
        def _(pool):
            pool.memset(ones[:, :], 1.0).then_inc(tri_step, 1)
            pool.wait_ge(tri_step, 1)
            pool.affine_select(out=before[:, :], in_=ones[:, :], compare_op=ALU.is_gt, fill=0.0, base=0,
                               pattern=[[1, P]], channel_multiplier=-1).then_inc(tri_step, 1)
            pool.wait_ge(tri_step, 2)
            pool.iota(number[:, :], pattern=[[1, E]], base=0, channel_multiplier=0,
                      allow_small_or_imprecise_dtypes=True).then_inc(tri_step, 1)

        @block.scalar
        def _(act):
            for j, name in enumerate(("ln1_g", "ln1_b")):
                act.dma_start(norm[:, j, :], d[name][0].partition_broadcast(P)).then_inc(ln_loaded, 16)
            act.dma_start(wr[:, :, :], d["w_router"][0].rearrange("(k p) e -> p k e", p=P)).then_inc(ln_loaded, 16)
            act.dma_start(br[:, :], d["b_router"][0].partition_broadcast(P)).then_inc(ln_loaded, 16)
            for n in range(AHEAD, 4 + AHEAD):
                split_high(c, act, W + n, (W + n) // RING + 1, n % RING)
            turn_act(c, act, 8, c.bank[4:8])
            for n in range(4 + AHEAD, after + AHEAD):
                split_high(c, act, W + n, (W + n) // RING + 1, n % RING)
            root_act(c, act, 1)
            turn_act(c, act, 12, c.bank[4:8])
            act.wait_ge(top_ready, 1)
            act.activation(gate[:, :, :], gate[:, :, :], ACT.Exp).then_inc(exp_ready, 1)

        @block.vector
        def _(dve):
            dve.wait_ge(c.gated, 1)
            for p in range(2):
                for n in range(2 * p + AHEAD, 2 * p + AHEAD + 2):
                    split_low(c, dve, W + n, n % RING)
                dve.wait_ge(c.used, W + 2 * p + 2)
                cols = slice(p * COLS, p * COLS + COLS)
                for m in range(TT):
                    linked(c, dve, dve.tensor_tensor(mg[:, m, cols], c.bank[4 * p + m][:, :],
                                                     c.gates[:, m, cols], ALU.mult))
                    linked(c, dve, dve.tensor_tensor(gb[:, m, :], c.bank[4 * p + 2 + m][:, :],
                                                     c.gates[:, m, D + p * COLS:D + p * COLS + COLS], ALU.mult))
                    dve.tensor_tensor(mg[:, m, cols], mg[:, m, cols], gb[:, m, :], ALU.add).then_inc(merged, 1)
                    dve.wait_ge(merged, 2 * p + m + 1)
            turn_dve(c, dve, 8, c.bank[4:8])
            for p in range(2):
                for n in range(4 + 2 * p + AHEAD, 4 + 2 * p + AHEAD + 2):
                    split_low(c, dve, W + n, n % RING)
                dve.wait_ge(c.used, W + 4 + 2 * p + 2)
                cols = slice(p * COLS, p * COLS + COLS)
                for m in range(TT):
                    last = dve.scalar_tensor_tensor(c.x[:, m, cols], c.x[:, m, cols], RES, c.bank[2 * p + m][:, :],
                                                    ALU.mult, ALU.add)
            last.then_inc(added, 1)
            dve.wait_ge(added, 1)
            dve.wait_ge(ln_loaded, 64)
            layer_norm_dve(c, dve, 1, c.x, norm[:, 0, :], norm[:, 1, :])
            dve.sem_inc(h_ready, 1)
            turn_dve(c, dve, 12, c.bank[4:8])
            dve.wait_ge(logits_done, 1)
            linked(c, dve, dve.tensor_tensor(lg[:, :, :], c.bank[0][:, 0:TT * E].rearrange("p (m e) -> p m e", m=TT),
                                             br[:, :].unsqueeze(1).to_broadcast([P, TT, E]), ALU.add))
            for m in range(TT):
                last = dve.max(top[:, m, :], lg[:, m, :])
            linked(c, dve, last)
            for m in range(TT):
                last = dve.max_index(index[:, m, :], top[:, m, :], lg[:, m, :])
            linked(c, dve, last)
            linked(c, dve, dve.tensor_copy(indexf[:, :, :], index[:, :, :]))
            dve.tensor_tensor(gate[:, :, :], top[:, :, 0:TOPK], top[:, :, 0:1].to_broadcast([P, TT, TOPK]),
                              ALU.subtract).then_inc(top_ready, 1)
            dve.wait_ge(exp_ready, 1)
            linked(c, dve, dve.tensor_reduce(gsum[:, :], gate[:, :, :], AX, ALU.add))
            linked(c, dve, dve.reciprocal(gsum[:, :], gsum[:, :]))
            linked(c, dve, dve.tensor_tensor(gate[:, :, :], gate[:, :, :],
                                             gsum[:, :].unsqueeze(2).to_broadcast([P, TT, TOPK]), ALU.mult))
            dve.wait_ge(tri_step, 3)
            for m in range(TT):
                last = dve.tensor_tensor(hit[:, m], number[:, :].unsqueeze(1).to_broadcast([P, TOPK, E]),
                                         indexf[:, m, 0:TOPK].unsqueeze(2).to_broadcast([P, TOPK, E]), ALU.is_equal)
            linked(c, dve, last)
            for m in range(TT):
                last = dve.tensor_reduce(c.pick[:, m], hit[:, m].rearrange("p k e -> p e k"), AX, ALU.add)
            last.then_inc(picked, 1)
            dve.wait_ge(picked, 1)
            for m in range(TT):
                last = dve.tensor_tensor(hit[:, m], hit[:, m], gate[:, m].unsqueeze(2).to_broadcast([P, TOPK, E]),
                                         ALU.mult)
            linked(c, dve, last)
            for m in range(TT):
                last = dve.tensor_reduce(c.weight[:, m], hit[:, m].rearrange("p k e -> p e k"), AX, ALU.add)
            linked(c, dve, last)
            dve.wait_ge(ranked, 1)
            for m in range(TT):
                last = dve.scalar_tensor_tensor(c.place[:, m, 0], c.bank[1][:, m * E:m * E + E], 1.0, c.pick[:, m],
                                                ALU.add, ALU.mult)
            linked(c, dve, last)
            linked(c, dve, dve.tensor_scalar(c.place[:, :, 0], c.place[:, :, 0], -1.0, None, ALU.add))
            for b in range(1, PASSES):
                last = dve.tensor_scalar(c.place[:, :, b], c.place[:, :, 0], -float(CAP * b), None, ALU.add)
            linked(c, dve, last)
            for b in range(PASSES):
                last = dve.tensor_scalar(spillf[:, b * E:b * E + E], c.bank[2][0:1, 0:E], float(CAP * b), None,
                                         ALU.is_gt)
            linked(c, dve, last)
            linked(c, dve, dve.tensor_reduce(spillf[:, PASSES * E:PASSES * E + 1], spillf[:, E:PASSES * E],
                                             AX, ALU.max))
            linked(c, dve, dve.tensor_copy(c.spill[:, :], spillf[:, :]))

        @block.tensor
        def _(pe):
            for p in range(2):
                multiply_rows(c, pe, W + 2 * p, 2 * p, 0, c.bank[4 * p:4 * p + 2], True, True)
                multiply_rows(c, pe, W + 2 * p + 1, 2 * p + 1, CK, c.bank[4 * p + 2:4 * p + 4], True, True)
            pe.wait_ge(merged, 4)
            turn_pe(c, pe, 8, mg, c.bank[4:8])
            turned_all(c, pe, 8)
            for p in range(2):
                for h in range(2):
                    n = 4 + 2 * p + h
                    multiply_rows(c, pe, W + n, n % RING, h * CK, c.bank[2 * p:2 * p + 2], h == 0, h == 1)
            pe.wait_ge(h_ready, 1)
            turn_pe(c, pe, 12, c.x, c.bank[4:8])
            turned_all(c, pe, 12)
            pe.wait_ge(ln_loaded, 64)
            for m in range(TT):
                for k in range(KT):
                    for j, x in enumerate((c.xth, c.xtl)):
                        mm = pe.matmul(c.bank[0][:, m * E:m * E + E], x[:, k, m * P:m * P + P].bitcast(F32),
                                       wr[:, k, :], start=k == 0 and j == 0, stop=k == KT - 1 and j == 1)
            mm.then_inc(logits_done, 1)
            pe.wait_ge(picked, 1)
            pe.wait_ge(tri_step, 3)
            pe.matmul(c.bank[1][:, 0:E], before[:, :], c.pick[:, 0], start=True, stop=True)
            pe.matmul(c.bank[1][:, E:2 * E], before[:, :], c.pick[:, 1], start=True, stop=False)
            pe.matmul(c.bank[1][:, E:2 * E], ones[:, :], c.pick[:, 0], start=False, stop=True)
            pe.matmul(c.bank[2][:, 0:E], ones[:, :], c.pick[:, 0], start=True, stop=False)
            pe.matmul(c.bank[2][:, 0:E], ones[:, :], c.pick[:, 1], start=False, stop=True).then_inc(ranked, 1)
    c.chunk += after



ITEM = 12
HID = 4
SLOTS = 2 * CAP


class Items:

    def __init__(self, c, name):
        def sem(signal):
            return c.sem(name + signal)

        self.chosen = sem("chosen")
        self.gathered = sem("gathered")
        self.rows = sem("rows")
        self.hid_kept = sem("hid_kept")
        self.folded = sem("folded")
        self.turned = sem("turned")
        self.turn_kept = sem("turn_kept")
        self.glu_ready = sem("glu_ready")
        self.sig_ready = sem("sig_ready")
        self.hidden = sem("hidden")
        self.y_high = sem("y_high")
        self.y_low = sem("y_low")
        self.step = sem("step")


def chunk_number(st, seq, j):
    return seq * ITEM + (st.first + j) if not isinstance(seq, int) else st.first + ITEM * seq + j


def lap_of(st, seq, j):
    return seq * (ITEM // RING) + (st.first_lap + j // RING + 1)


def choose(c, dve, it, seq, item):
    for m in range(TT):
        x = dve.tensor_scalar(c.choice[:, m, :], c.slot_number[:, :], c.place_of[:, m, ds(item, 1)], None, ALU.is_equal)
    x.then_inc(it.chosen, 1)


def gather(c, pe, it, seq, free):
    pe.wait_ge(it.chosen, seq + 1)
    for g in range(2):
        if free:
            free(g)
        bank = c.bank[4 + g]
        for k in range(CK):
            kk = g * CK + k
            for j, part in enumerate((c.hh, c.hl)):
                for m in range(TT):
                    mm = pe.matmul(bank[:, (2 * k + j) * CAP:(2 * k + j + 1) * CAP],
                                   part[:, m, kk * P:kk * P + P], c.choice[:, m, 0:CAP],
                                   start=m == 0, stop=m == TT - 1)
        mm.then_inc(it.gathered, 1)


def keep_rows(c, act, it, seq):
    for g in range(2):
        act.wait_ge(it.gathered, seq * 2 + (g + 1))
        act.activation(c.xs[:, g * CK:g * CK + CK, :], c.bank[4 + g].rearrange("p (k s) -> p k s", k=CK), ACT.Copy
                       ).then_inc(it.rows, 1)


def combine(c, pe, it, seq):
    pe.wait_ge(it.y_high, seq * 2 + 4)
    pe.wait_ge(it.y_low, seq * 2 + 4)
    for m in range(TT):
        for h in range(2):
            for y in (c.yh, c.yl):
                mm = pe.matmul(c.bank[2 * m + h], c.back[:, m * P:m * P + P], y[:, h * COLS:h * COLS + COLS],
                               start=False, stop=False, skip_group_check=True)
    return mm


def item_pe(c, st, pe, it, seq, more, combine_before):
    def panel(p, lhs):
        for h in range(2):
            j = 2 * p + h
            pe.wait_ge(st.low_ready, chunk_number(st, seq, j) + 1)
            for k in range(CK):
                for q, w in enumerate((c.wh, c.wl)):
                    mm = pe.matmul(c.bank[4 + p % 2], lhs[:, h * CK + k, :], w[:, j % RING, k],
                                   start=h == 0 and k == 0 and q == 0, stop=h == 1 and k == CK - 1 and q == 1)
            mm.then_inc(st.used, 1)

    def fold(p):
        pe.wait_ge(it.hid_kept, seq * HID + (p + 1))
        for b in range(COLS // P):
            j = (p % 2) * 4 + b
            mm = pe.matmul(c.bank[6 + p // 2][:, j * CAP:j * CAP + CAP], c.hid[:, p, b * P:b * P + P],
                           c.stack[:, :], start=True, stop=True)
        mm.then_inc(it.folded, 1)

    pe.wait_ge(it.rows, seq * 2 + 2)
    pe.wait_ge(it.y_low, seq * 2 + 1)
    panel(0, c.xs)
    if combine_before:
        combine(c, pe, it, seq - 1)
    else:
        pe.wait_ge(it.y_low, seq * 2 + 2)
    pe.wait_ge(it.hidden, seq + 1)
    for m in range(TT):
        pe.transpose(c.bank[6][:, m * P:m * P + P], c.choice[:, m, :].bitcast(F32), c.ident[:, :])
    for m in range(TT):
        mm = pe.matmul(c.bank[7][:, 0:1], c.choice[:, m, :].bitcast(F32), c.weight[:, m, ds(it.expert, 1)],
                       start=m == 0, stop=m == TT - 1)
    mm.then_inc(it.turned, 1)
    panel(1, c.xs)
    pe.wait_ge(it.turn_kept, seq + 1)
    fold(0)
    pe.wait_ge(it.hid_kept, seq * HID + 1)
    panel(2, c.xs)
    fold(1)
    pe.wait_ge(it.hid_kept, seq * HID + 2)
    panel(3, c.xs)
    fold(2)
    if more:
        gather(c, pe, it, seq + 1, lambda g: pe.wait_ge(it.hid_kept, seq * HID + (3 + g)))
    fold(3)
    pe.wait_ge(it.hidden, seq + 2)
    for g in range(2):
        if more:
            pe.wait_ge(it.rows, seq * 2 + (3 + g))
        panel(4 + g, c.acts)


def item_act(c, st, act, it, seq, more):
    def high(j):
        if j < ITEM or more:
            split_high(st, act, chunk_number(st, seq, j), lap_of(st, seq, j), j % RING)

    for p in range(HID):
        high(2 * p + 2)
        high(2 * p + 3)
        act.wait_ge(st.used, chunk_number(st, seq, 2 * p + 2))
        act.activation(c.hid[:, p, :], c.bank[4 + p % 2], ACT.Copy).then_inc(it.hid_kept, 1)
        if p == 0:
            act.wait_ge(it.turned, seq + 1)
            act.activation(c.back[:, :], c.bank[6][:, 0:S], ACT.Copy)
            act.activation(c.slot_weight[:, :], c.bank[7][:, 0:1], ACT.Copy).then_inc(it.turn_kept, 1)
    if more:
        keep_rows(c, act, it, seq + 1)
    high(10)
    act.wait_ge(it.glu_ready, seq + 1)
    act.activation(c.sig[:, :, :], c.gate_half[:, :, :], ACT.Sigmoid, scale=1.702).then_inc(it.sig_ready, 1)
    high(11)
    for g in range(2):
        act.wait_ge(st.used, chunk_number(st, seq, 10 + 2 * g))
        act.activation(c.yh[:, g * COLS:g * COLS + COLS], c.bank[4 + g], ACT.Copy, scale=c.slot_weight[:, 0:1]
                       ).then_inc(it.y_high, 1)
        high(12 + g)


def item_dve(c, st, dve, it, seq, item, more):
    steps = 0
    per = 8

    def low(j):
        if j < ITEM or more:
            split_low(st, dve, chunk_number(st, seq, j), j % RING)

    def step(x):
        nonlocal steps
        steps += 1
        x.then_inc(it.step, 1)
        dve.wait_ge(it.step, seq * per + steps)

    def bias(b0):
        return c.bias_in[:, ds(it.expert * 16 + b0, 8)].unsqueeze(2).to_broadcast([P, 8, CAP])

    low(2)
    low(3)
    if more:
        dve.wait_ge(it.turned, seq + 1)
        choose(c, dve, it, seq + 1, item + 1)
    for j in range(4, 8):
        low(j)
    dve.wait_ge(it.folded, seq * HID + 2)
    step(dve.tensor_tensor(c.gate_half[:, :, :], c.bank[6].rearrange("p (j s) -> p j s", j=8), bias(0), ALU.add))
    dve.tensor_scalar(c.gate_half[:, :, :], c.gate_half[:, :, :], 7.0, None, ALU.min).then_inc(it.glu_ready, 1)
    low(8)
    low(9)
    dve.wait_ge(it.folded, seq * HID + 4)
    step(dve.tensor_tensor(c.up_half[:, :, :], c.bank[7].rearrange("p (j s) -> p j s", j=8), bias(8), ALU.add))
    step(dve.tensor_scalar(c.up_half[:, :, :], c.up_half[:, :, :], 7.0, -7.0, ALU.min, ALU.max))
    dve.wait_ge(it.glu_ready, seq + 1)
    step(dve.scalar_tensor_tensor(c.up_half[:, :, :], c.up_half[:, :, :], 1.0, c.gate_half[:, :, :],
                                  ALU.add, ALU.mult))
    low(10)
    dve.wait_ge(it.sig_ready, seq + 1)
    step(dve.tensor_tensor(c.up_half[:, :, :], c.up_half[:, :, :], c.sig[:, :, :], ALU.mult))
    step(dve.tensor_copy(c.acts[:, :, 0:CAP], c.up_half[:, :, :]))
    dve.tensor_tensor(c.acts[:, :, CAP:SLOTS], c.up_half[:, :, :], c.acts[:, :, 0:CAP].bitcast(F32),
                      ALU.subtract).then_inc(it.hidden, 1)
    low(11)
    for g in range(2):
        dve.wait_ge(it.y_high, seq * 2 + (3 + g))
        cols = slice(g * COLS, g * COLS + COLS)
        dve.scalar_tensor_tensor(c.yl[:, cols], c.bank[4 + g], c.slot_weight[:, 0:1], c.yh[:, cols].bitcast(F32),
                                 ALU.mult, ALU.subtract).then_inc(it.y_low, 1)
        low(12 + g)
    for _ in range(per - steps):
        dve.sem_inc(it.step, 1)


def phase_experts(c):
    nc, d = c.nc, c.dram
    W = c.chunk
    w1, w2 = d["w_exp_in"][0], d["w_exp_out"][0]
    it, c.spill_items = Items(c, "item_"), Items(c, "spill_")
    moe_loaded = c.sem("moe_loaded")
    moe_step = c.sem("moe_step")
    set_up = c.sem("set_up")
    bias_turned = c.sem("bias_turned")
    bias_kept = c.sem("bias_kept")
    bias_added = c.sem("bias_added")
    split_ready = c.sem("split_ready")
    c.first, c.first_lap = W, W // RING

    c.hh = c.sb("hh", [P, TT, D], F32R, ctx=c.exp)
    c.hl = c.sb("hl", [P, TT, D], F32R, ctx=c.exp)
    c.xs = c.sb("xs", [P, KT, SLOTS], F32R, ctx=c.exp)
    c.acts = c.sb("acts", [P, KT, SLOTS], F32R, ctx=c.exp)
    c.hid = c.sb("hid", [P, HID, COLS], ctx=c.exp)
    c.yh = c.sb("yh", [P, D], F32R, ctx=c.exp)
    c.yl = c.sb("yl", [P, D], F32R, ctx=c.exp)
    c.choice = c.sb("choice", [P, TT, SLOTS], F32R, ctx=c.exp)
    c.back = c.sb("back", [P, S], F32R, ctx=c.exp)
    c.slot_number = c.sb("slot_number", [P, SLOTS], ctx=c.exp)
    c.slot_weight = c.sb("slot_weight", [P, 1], ctx=c.exp)
    c.stack = c.sb("stack", [P, CAP], ctx=c.exp)
    c.gate_half = c.sb("gate_half", [P, 8, CAP], ctx=c.exp)
    c.up_half = c.sb("up_half", [P, 8, CAP], ctx=c.exp)
    c.sig = c.sb("sig", [P, 8, CAP], ctx=c.exp)
    c.bias_in = c.sb("bias_in", [P, E * 16], ctx=c.exp)
    c.place_of = c.place[:, :, :, :].rearrange("p m b e -> p m (b e)")

    with ExitStack() as local, nc.Block() as block:
        bias_rows = c.sb("bias_rows", [P, 4, P], ctx=local)
        bias_out = c.sb("bias_out", [E, D], ctx=local)
        weight_t = c.sb("weight_t", [E, S], ctx=local)

        def expert_chunk(e, j):
            if j < 2 * HID:
                return rows_cols(w1[e], j % 2 * 512, j // 2 * COLS)
            return rows_cols(w2[e], j % 2 * 512, (j // 2 - HID) * COLS)

        def by_register(w, e, j):
            m = w[ds(e, 1)].rearrange("a r c -> (a r) c")
            return rows_cols(m, j % 2 * 512, (j // 2 % HID) * COLS)

        @block.sync
        def _(sp):
            def load(seq, e, j):
                w = w1 if j < 2 * HID else w2
                load_chunk(c, sp, chunk_number(c, seq, j), j % RING, by_register(w, e, j))

            with sp.Fori(0, E - 1) as i:
                for j in range(LOADED, ITEM):
                    load(i, i, j)
                for j in range(LOADED):
                    load(i + 1, i + 1, j)
            for j in range(LOADED, ITEM):
                load_chunk(c, sp, chunk_number(c, E - 1, j), j % RING, expert_chunk(E - 1, j))

        @block.gpsimd
        def _(pool):
            pool.memset(c.stack[:, :], 0.0).then_inc(moe_step, 1)
            pool.iota(c.slot_number[:, :], pattern=[[0, 2], [1, CAP]], base=0, channel_multiplier=0,
                      allow_small_or_imprecise_dtypes=True).then_inc(moe_step, 1)
            pool.wait_ge(moe_step, 2)
            for j in range(2):
                pool.affine_select(out=c.stack[:, :], in_=c.stack[:, :], compare_op=ALU.not_equal, fill=1.0,
                                   base=-j * CAP, pattern=[[-1, CAP]], channel_multiplier=1).then_inc(moe_step, 1)
                pool.wait_ge(moe_step, 3 + j)
            for t in (c.yh, c.yl, c.back):
                pool.memset(t[:, :].bitcast(F32), 0.0).then_inc(moe_step, 1)
            pool.wait_ge(moe_step, 7)
            pool.sem_inc(set_up, 1)

        @block.scalar
        def _(act):
            act.dma_start(bias_rows[:, :, :], d["b_exp_in"][0].rearrange("e (j f) -> (e j) f", f=P)
                          .rearrange("(a p) f -> p a f", p=P)).then_inc(moe_loaded, 16)
            act.dma_start(bias_out[:, :], d["b_exp_out"][0]).then_inc(moe_loaded, 16)
            for m in range(TT):
                act.activation(c.hh[:, m], c.x[:, m], ACT.Copy).then_inc(split_ready, 1)
            act.wait_ge(bias_turned, 1)
            act.activation(weight_t[:, :], c.bank[5][0:E, 0:S], ACT.Copy).then_inc(bias_kept, 1)
            act.activation(c.bias_in[:, :], c.bank[4], ACT.Copy).then_inc(bias_kept, 1)
            act.sem_inc(it.y_high, 2)
            keep_rows(c, act, it, 0)
            with act.Fori(0, E - 1) as i:
                item_act(c, c, act, it, i, True)
            item_act(c, c, act, it, E - 1, False)

        @block.vector
        def _(dve):
            for m in range(TT):
                dve.wait_ge(split_ready, m + 1)
                x = dve.tensor_tensor(c.hl[:, m], c.x[:, m], c.hh[:, m].bitcast(F32), ALU.subtract)
            x.then_inc(split_ready, 1)
            dve.wait_ge(set_up, 1)
            choose(c, dve, it, 0, 0)
            dve.wait_ge(bias_kept, 2)
            dve.sem_inc(it.hidden, 1)
            dve.sem_inc(it.y_low, 2)
            with dve.Fori(0, E - 1) as i:
                it.expert = i
                item_dve(c, c, dve, it, i, i, True)
            it.expert = E - 1
            item_dve(c, c, dve, it, E - 1, E - 1, False)

        @block.tensor
        def _(pe):
            pe.wait_ge(moe_loaded, 32)
            for a in range(4):
                pe.transpose(c.bank[4][:, a * P:a * P + P], bias_rows[:, a, :], c.ident[:, :])
            for m in range(TT):
                t = pe.transpose(c.bank[5][0:E, m * P:m * P + P], c.weight[:, m, :], c.ident[:, :])
            t.then_inc(bias_turned, 1)
            pe.wait_ge(bias_kept, 2)
            for m in range(TT):
                for h in range(2):
                    pe.matmul(c.bank[2 * m + h], weight_t[:, m * P:m * P + P], bias_out[:, h * COLS:h * COLS + COLS],
                              start=True, stop=False, skip_group_check=True)
            pe.wait_ge(split_ready, 3)
            gather(c, pe, it, 0, None)
            with pe.Fori(0, E - 1) as i:
                it.expert = i
                item_pe(c, c, pe, it, i, True, True)
            it.expert = E - 1
            item_pe(c, c, pe, it, E - 1, False, True)
            combine(c, pe, it, E - 1)
    c.chunk += ITEM * E



def phase_spill(c):
    nc, d = c.nc, c.dram
    w1, w2 = d["w_exp_in"][0], d["w_exp_out"][0]
    st = Stream(c, "spill_", RING, 0)
    it = c.spill_items

    def items(eng, name, body):
        any_spill = eng.value_load(c.spill[0:1, PASSES * E:PASSES * E + 1], min_val=0, max_val=1)
        count = eng.alloc_register("spill_seq_" + name)
        eng.reg_mov(count, 0)
        with eng.If(any_spill):
            with eng.Fori(1, PASSES) as b:
                with eng.Fori(0, E) as e:
                    flag = eng.value_load(c.spill[0:1, ds(b * E + e, 1)], min_val=0, max_val=1)
                    with eng.If(flag):
                        seq = eng.snap(count, min_val=0, max_val=S * TOPK // CAP - 1)
                        body(seq, b * E + e, e)
                        eng.reg_add(count, count, 1)
                    eng.nop()
            eng.nop()

    with nc.Block() as block:
        @block.sync
        def _(sp):
            def body(seq, item, e):
                for j in range(ITEM):
                    m = (w1 if j < 2 * HID else w2)[ds(e, 1)].rearrange("a r c -> (a r) c")
                    load_chunk(st, sp, chunk_number(st, seq, j), j % RING,
                               rows_cols(m, j % 2 * 512, (j // 2 % HID) * COLS))
            items(sp, "sp", body)

        @block.scalar
        def _(act):
            act.sem_inc(it.y_high, 2)
            act.sem_inc(st.high_ready, RING)

            def body(seq, item, e):
                for j in range(AHEAD):
                    split_high(st, act, chunk_number(st, seq, j), lap_of(st, seq, j), j)
                keep_rows(c, act, it, seq)
                item_act(c, st, act, it, seq, False)
            items(act, "act", body)

        @block.vector
        def _(dve):
            dve.sem_inc(it.y_low, 2)
            dve.sem_inc(it.hidden, 1)
            dve.sem_inc(st.low_ready, RING)

            def body(seq, item, e):
                it.expert = e
                choose(c, dve, it, seq, item)
                for j in range(AHEAD):
                    split_low(st, dve, chunk_number(st, seq, j), j)
                item_dve(c, st, dve, it, seq, item, False)
            items(dve, "dve", body)

        @block.tensor
        def _(pe):
            pe.sem_inc(st.used, RING)

            def body(seq, item, e):
                it.expert = e
                gather(c, pe, it, seq, None)
                item_pe(c, st, pe, it, seq, False, False)
                combine(c, pe, it, seq)
            items(pe, "pe", body)



D2 = D // 2
CONV = 3
HG = 4
CH = S // CHUNK


def high(c, act, n):
    split_high(c, act, n, n // RING + 1, n % RING)


def rms_act(c, act, v, junk):
    act.wait_ge(c.x_ready, v)
    for m in range(TT):
        a = act.activation(junk[:, m], c.x[:, m], ACT.Square, accum_out=c.ss[:, m:m + 1])
    a.then_inc(c.squared, 1)
    root_act(c, act, v)


def rms_dve(c, dve, v, h, scale, shift):
    linked(c, dve, dve.scalar_tensor_tensor(scale, scale, 1.0, c.norm[:, :], ALU.add, ALU.mult))
    dve.wait_ge(c.squared, v - FIRST_RMS + 1)
    linked(c, dve, dve.tensor_scalar(c.ss[:, :], c.ss[:, :], 1.0 / D, EPS_RMS, ALU.mult, ALU.add))
    dve.reciprocal(c.rv[:, :], c.ss[:, :]).then_inc(c.rv_ready, 1)
    dve.wait_ge(c.rs_ready, v + 1)
    for m in range(TT):
        last = dve.scalar_tensor_tensor(h[:, m], c.x[:, m], c.rs[:, m:m + 1], scale, ALU.mult, ALU.mult)
    linked(c, dve, last)
    for m in range(TT):
        last = dve.tensor_tensor(h[:, m], h[:, m], shift, ALU.add)
    last.then_inc(c.h_ready, 1)


FIRST_RMS = 3


def make_second(c):
    c.mod = c.sb("mod", [P, 6, D], ctx=c.two)
    c.ch = c.sb("ch", [P, KT, P], F32R, ctx=c.two)
    c.cl = c.sb("cl", [P, KT, P], F32R, ctx=c.two)
    c.norm = c.sb("norm", [P, D], ctx=c.two)
    c.ss = c.sb("ss2", [P, TT], ctx=c.two)
    c.x_ready = c.sem("x_ready")
    c.masks_ready = c.sem("masks_ready")
    c.squared = c.sem("squared")
    c.h_ready = c.sem("h2_ready")
    c.mod_kept = c.sem("mod_kept")
    c.mod_loaded = c.sem("mod_loaded")
    c.norm_loaded = c.sem("norm_loaded2")
    c.norms_loaded = 0



def phase_modulate(c, layer):
    nc, d = c.nc, c.dram
    W = c.chunk
    panels = 12
    after = 2 * panels
    ada = d["ada_w_2"][layer]
    nxt = d["w_in_ab_2"][0] if layer == 0 else d["w_qkv_2"][0]
    c_loaded = c_split = None
    if layer == 0:
        c_loaded, c_split, ln_loaded = c.sem("c_loaded"), c.sem("c_split"), c.sem("ln2_loaded")

    with ExitStack() as local, nc.Block() as block:
        if layer == 0:
            ln = c.sb("ln2", [P, 2, D], ctx=local)
            cv = c.sb("cv", [P, KT], ctx=local)
            cs = c.sb("cs", [P, KT], ctx=local)

        @block.sync
        def _(sp):
            if layer == 0:
                for j in range(LOADED):
                    load_chunk(c, sp, W + j, j % RING, rows_cols(ada, j % 2 * 512, j // 2 * COLS))
            with sp.Fori(0, 4) as i:
                for j in range(4):
                    load_chunk(c, sp, i * 4 + (W + LOADED + j), (W + LOADED + j) % RING,
                               rows_cols(ada, j % 2 * 512, i * (2 * COLS) + (3 + j // 2) * COLS))
            for j in range(22, after):
                load_chunk(c, sp, W + j, (W + j) % RING, rows_cols(ada, j % 2 * 512, j // 2 * COLS))
            for j in range(LOADED):
                load_chunk(c, sp, W + after + j, (W + after + j) % RING, rows_cols(nxt, j % 2 * 512, j // 2 * COLS))

        @block.scalar
        def _(act):
            for j in range(6):
                act.dma_start(c.mod[:, j, :], d["ada_b_2"][layer, j * D:j * D + D].partition_broadcast(P)
                              ).then_inc(c.mod_loaded, 16)
            act.dma_start(c.norm[:, :], d["norm_mix_2"][layer].partition_broadcast(P)).then_inc(c.norm_loaded, 16)
            if layer == 0:
                for j, name in enumerate(("ln2_g", "ln2_b")):
                    act.dma_start(ln[:, j, :], d[name][0].partition_broadcast(P)).then_inc(ln_loaded, 16)
                with nc.allow_non_contiguous_dma(reason="1024 numbers, once"):
                    act.dma_start(cv[:, :], d["c_2"][0].rearrange("(k p) -> p k", p=P)).then_inc(c_loaded, 16)
                act.wait_ge(c_loaded, 16)
                act.activation(cs[:, :], cv[:, :], ACT.Sigmoid).then_inc(c_split, 1)
                act.wait_ge(c_split, 2)
                act.activation(c.ch[:, :, :], cs[:, :].unsqueeze(2).to_broadcast([P, KT, P]), ACT.Copy
                               ).then_inc(c_split, 1)
                for j in range(AHEAD):
                    high(c, act, W + j)
                root_act(c, act, 2)
            with act.Fori(0, panels // 2) as i:
                for j in range(AHEAD, AHEAD + 4):
                    n = W + j
                    split_high(c, act, i * 4 + n, i + (n // RING + 1), n % RING)

        @block.vector
        def _(dve):
            if layer == 0:
                dve.wait_ge(c_split, 1)
                dve.tensor_tensor(cs[:, :], cs[:, :], cv[:, :], ALU.mult).then_inc(c_split, 1)
                dve.wait_ge(c_split, 3)
                dve.tensor_tensor(c.cl[:, :, :], cs[:, :].unsqueeze(2).to_broadcast([P, KT, P]),
                                  c.ch[:, :, :].bitcast(F32), ALU.subtract).then_inc(c_split, 1)
                for j in range(AHEAD):
                    split_low(c, dve, W + j, (W + j) % RING)
                for m in range(TT):
                    last = dve.scalar_tensor_tensor(c.x[:, m].rearrange("p (h n) -> p h n", h=2),
                                                    c.x[:, m].rearrange("p (h n) -> p h n", h=2), RES,
                                                    c.psum[:, 2 * m:2 * m + 2, :], ALU.mult, ALU.add)
                linked(c, dve, last)
                dve.wait_ge(ln_loaded, 32)
                layer_norm_dve(c, dve, 2, c.x, ln[:, 0, :], ln[:, 1, :])
                dve.sem_inc(c.x_ready, FIRST_RMS)
                dve.sem_inc(c.mod_kept, 2)
            dve.wait_ge(c.mod_loaded, 16 * 6 * (layer + 1))
            with dve.Fori(0, panels // 2) as i:
                for p in range(2):
                    for j in (2 * p + AHEAD, 2 * p + AHEAD + 1):
                        split_low(c, dve, i * 4 + (W + j), (W + j) % RING)
                    dve.wait_ge(c.used, i * 4 + (W + 2 * p + 2))
                    part = c.mod[:, :, :].rearrange("p s n -> p (s n)")[:, ds(i * (2 * COLS) + p * COLS, COLS)]
                    dve.tensor_tensor(part, part, c.bank[4 + p], ALU.add).then_inc(c.mod_kept, 1)

        @block.tensor
        def _(pe):
            if layer == 0:
                pe.wait_ge(c_split, 4)
            with pe.Fori(0, panels // 2) as i:
                for p in range(2):
                    pe.wait_ge(c.mod_kept, i * 2 + (layer * panels + p + 1))
                    for h in range(2):
                        n = W + 2 * p + h
                        pe.wait_ge(c.low_ready, i * 4 + (n + 1))
                        for k in range(CK):
                            for q, (x, w) in enumerate(((c.ch, c.wh), (c.ch, c.wl), (c.cl, c.wh))):
                                mm = pe.matmul(c.bank[4 + p], x[:, h * CK + k, :], w[:, n % RING, k],
                                               start=h == 0 and k == 0 and q == 0, stop=h == 1 and k == 3 and q == 2)
                        mm.then_inc(c.used, 1)
    c.chunk += after



def static_source(c, n):
    d = c.dram
    k = n - c.second
    for layer in range(2):
        k -= 24
        mats = ((d["w_in_ab_2"][0], 14), (d["w_out_ab_2"][0], 4)) if layer == 0 else \
            ((d["w_qkv_2"][0], 12), (d["w_out_c_2"][0], 4))
        for m, count in mats:
            if k < count:
                return rows_cols(m, k % 2 * 512, k // 2 * COLS)
            k -= count
        if k < 32:
            return mlp_source(c, layer, k // 8, k % 8)
        k -= 32
        if layer == 0 and k < 24:
            return rows_cols(d["ada_w_2"][1], k % 2 * 512, k // 2 * COLS)
    return None


def mlp_source(c, layer, quarter, j):
    if j < 4:
        return rows_cols(c.dram["mlp_w1_2"][layer], j % 2 * 512, quarter * 1024 + j // 2 * COLS)
    j -= 4
    return rows_cols(c.dram["mlp_w2_2"][layer], quarter * 1024 + j // 2 * 512, j % 2 * COLS)


def load_static(c, sp, count):
    for n in range(c.chunk + LOADED, c.chunk + count + LOADED):
        src = static_source(c, n)
        if src is not None:
            load_chunk(c, sp, n, n % RING, src)


def low(c, dve, n):
    split_low(c, dve, n, n % RING)


def phase_project_ab(c):
    nc, d = c.nc, c.dram
    W = c.chunk
    panels = 7
    kinds = "TTTTTNN"
    evacuated = c.sem("ab_evacuated")
    conv_loaded = c.sem("conv_loaded")
    mask_step = c.sem("mask_step")
    cm = c.hgrn
    c.h = c.sb("h", [P, TT, D], ctx=cm)
    c.ab = c.sb("ab", [P, 4, S], ctx=cm)
    c.ac = c.sb("ac", [P, 4, S], ctx=cm)
    c.ya = c.sb("ya", [P, 4, S], ctx=cm)
    c.q = c.sb("q", [P, HG, S], ctx=cm)
    c.f = c.sb("f", [P, HG, S], ctx=cm)
    c.v = c.sb("v", [P, TT, D2], ctx=cm)
    c.hg = c.sb("hg", [P, TT, D2], ctx=cm)
    c.level_mask = c.sb("level_mask", [P, 7, P], ctx=cm)
    c.conv = c.sb("conv", [P, CONV, 4], ctx=cm)
    c.lb_in = c.sb("lb_in", [P, 3, HG], ctx=cm)
    outs = [c.ab, None, None, c.q, c.f, c.v, c.hg]

    with nc.Block() as block:
        @block.sync
        def _(sp):
            load_static(c, sp, 2 * panels)

        @block.gpsimd
        def _(pool):
            steps = 0

            def done(x):
                nonlocal steps
                steps += 1
                x.then_inc(mask_step, 1)
                pool.wait_ge(mask_step, steps)

            done(pool.memset(c.level_mask[:, :, :], 0.0))
            for j in range(7):
                w = 2 ** j
                second = c.level_mask[:, j].rearrange("p (b h w) -> p b h w", h=2, w=w)[:, :, 1, :]
                done(pool.memset(second, 1.0))
                done(pool.affine_select(out=second, in_=second, compare_op=ALU.is_ge, fill=0.0, base=0,
                                        pattern=[[-2 * w, P // (2 * w)], [0, w]], channel_multiplier=1))
                done(pool.affine_select(out=second, in_=second, compare_op=ALU.is_ge, fill=0.0, base=w - 1,
                                        pattern=[[2 * w, P // (2 * w)], [0, w]], channel_multiplier=-1))
            pool.sem_inc(c.masks_ready, 1)

        @block.scalar
        def _(act):
            with nc.allow_non_contiguous_dma(reason="3072 numbers, once"):
                act.dma_start(c.conv[:, :, :], d["conv_w_2"][0].rearrange("w (k p) -> p w k", p=P)
                              ).then_inc(conv_loaded, 16)
                act.dma_start(c.lb_in[:, :, :], d["lb_logits_2"].rearrange("r (k p) -> p r k", p=P)
                              ).then_inc(conv_loaded, 16)
            rms_act(c, act, FIRST_RMS, c.h)
            turn_act(c, act, 16, c.bank[4:8])
            for n in range(AHEAD, 2 * panels + AHEAD):
                high(c, act, W + n)

        @block.vector
        def _(dve):
            dve.wait_ge(c.norm_loaded, 16)
            rms_dve(c, dve, FIRST_RMS, c.h, c.mod[:, 1], c.mod[:, 0])
            turn_dve(c, dve, 16, c.bank[4:8])
            for p in range(panels):
                low(c, dve, W + 2 * p + 2)
                low(c, dve, W + 2 * p + 3)
                dve.wait_ge(c.used, W + 2 * p + 2)
                if p == 2:
                    dve.wait_ge(evacuated, 2)
                for b in range(2):
                    bank = c.bank[p % 2 * 2 + b]
                    wide = bank.rearrange("p (k s) -> p k s", k=2)
                    tiles = slice(2 * b, 2 * b + 2)
                    if p == 1:
                        last = dve.tensor_copy(c.ac[:, tiles, :], wide)
                    elif p == 2:
                        last = dve.tensor_tensor(c.ac[:, tiles, :], wide, c.ac[:, tiles, :], ALU.mult)
                    elif kinds[p] == "T":
                        last = dve.tensor_copy(outs[p][:, tiles, :], wide)
                    else:
                        last = dve.tensor_copy(outs[p][:, b, :], bank)
                last.then_inc(evacuated, 1)
                if p == 2:
                    dve.wait_ge(conv_loaded, 32)
                    dve.wait_ge(evacuated, 3)
                    for k in range(4):
                        last = dve.tensor_scalar(c.ya[:, k, :], c.ac[:, k, :], c.conv[:, 2, k:k + 1], None, ALU.mult)
                    linked(c, dve, last)
                    for back in (1, 2):
                        for k in range(4):
                            last = dve.scalar_tensor_tensor(c.ya[:, k, back:S], c.ac[:, k, 0:S - back],
                                                            c.conv[:, 2 - back, k:k + 1], c.ya[:, k, back:S],
                                                            ALU.mult, ALU.add)
                        linked(c, dve, last)
                    linked(c, dve, dve.tensor_tensor(c.ya[:, :, :], c.ya[:, :, :], c.ab[:, :, :], ALU.mult))

        @block.tensor
        def _(pe):
            pe.wait_ge(c.h_ready, 1)
            turn_pe(c, pe, 16, c.h, c.bank[4:8])
            turned_all(c, pe, 16)
            for p in range(panels):
                if p >= 2:
                    pe.wait_ge(evacuated, p - 1)
                for h in range(2):
                    n = W + 2 * p + h
                    (multiply_cols if kinds[p] == "T" else multiply_rows)(
                        c, pe, n, n % RING, h * CK, c.bank[p % 2 * 2:p % 2 * 2 + 2], h == 0, h == 1)
    c.chunk += 2 * panels



def phase_recur(c):
    nc, d = c.nc, c.dram
    W = c.chunk
    widths = [0, 1, 2, 4, 8, 16, 32, 64, 128]
    levels = len(widths)
    lb_step, lb_exp = c.sem("lb_step"), c.sem("lb_exp")
    forget = c.sem("forget")
    spans = c.sem("spans")
    decays = c.sem("decays")
    scaled = c.sem("scaled")
    paired = c.sem("paired")
    masked = c.sem("masked")
    summed = c.sem("summed")
    zeroed = c.sem("zeroed")
    hg_loaded = c.sem("hg_loaded")
    out_step = c.sem("out_step")
    yb_ready = c.sem("yb_ready")
    ya_split = c.sem("ya_split")
    added = c.sem("ab_added")

    with ExitStack() as local, nc.Block() as block:
        dd = [c.mod[:, 0, :], c.mod[:, 1, :]]
        qq = [c.ab, c.ac]
        kk0 = c.sb("kk0", [P, HG, S], ctx=local)
        kk1 = c.sb("kk1", [P, HG, S], ctx=local)
        kk = [kk0, kk1]
        sm = [c.h[:, 0, :], c.h[:, 1, :]]
        key = c.norm[:, :].rearrange("p (h s) -> p h s", h=HG)
        b = c.f
        lb = c.sb("lb", [P, 3, HG], ctx=local)
        lb2 = c.sb("lb2", [P, 3, HG], ctx=local)
        rest = c.mod[:, 0, :]
        tail = c.sb("tail", [P, HG], ctx=local)
        hnorm = c.sb("hnorm", [P, D2], ctx=local)
        sq = c.sb("hsq", [P, TT, HG], ctx=local)

        def halves(t, w):
            flat = t.rearrange("p h s -> p (h s)") if len(t.shape) == 3 else t
            return flat.rearrange("p (b h w) -> p b h w", h=2, w=w)

        def chunks(t):
            flat = t.rearrange("p h s -> p (h s)") if len(t.shape) == 3 else t
            return flat.rearrange("p (h c s) -> p h c s", h=HG, c=CH)

        @block.sync
        def _(sp):
            load_static(c, sp, 4)

        @block.gpsimd
        def _(pool):
            pool.memset(rest, 1.0).then_inc(zeroed, 1)
            pool.wait_ge(zeroed, 1)
            pool.memset(rest.rearrange("p (c s) -> p c s", s=CHUNK)[:, :, 0:1], 0.0).then_inc(zeroed, 1)
            for t in (qq[0], qq[1], kk0, kk1):
                pool.memset(t[:, :, :], 0.0).then_inc(zeroed, 1)

        @block.scalar
        def _(act):
            act.dma_start(hnorm[:, :], d["hg_norm_2"][0].partition_broadcast(P)).then_inc(hg_loaded, 16)
            act.activation(c.f[:, :, :], c.f[:, :, :], ACT.Sigmoid).then_inc(forget, 1)
            act.wait_ge(lb_step, 1)
            act.activation(lb[:, :, :], lb[:, :, :], ACT.Exp).then_inc(lb_exp, 1)
            act.wait_ge(forget, 3)
            act.activation(c.f[:, :, :], c.f[:, :, :], ACT.Ln).then_inc(forget, 1)
            for l in range(1, levels):
                act.wait_ge(spans, l)
                x = dd[l % 2]
                act.activation(x, x, ACT.Exp).then_inc(decays, 1)
            act.wait_ge(paired, 1)
            act.wait_ge(scaled, levels - 1)
            act.activation(key, c.hg[:, :, :].rearrange("p m n -> p (m n)").rearrange(
                "p (h s) -> p h s", h=HG), ACT.Sigmoid).then_inc(out_step, 1)
            act.wait_ge(summed, levels)
            act.activation(kk0[:, :, :].rearrange("p h s -> p (h s)").rearrange("p (m n) -> p m n", m=TT),
                           c.psum[:, 4:6, :], ACT.Square).then_inc(out_step, 1)
            act.wait_ge(out_step, 4)
            act.activation(sq[:, :, :], sq[:, :, :], ACT.Sqrt).then_inc(out_step, 1)
            act.activation(c.xth[:, 0:4, :], c.ya[:, :, :], ACT.Copy).then_inc(ya_split, 1)
            turn_act(c, act, 20, c.bank[0:2], 4, 4)
            for n in range(AHEAD, 4 + AHEAD):
                high(c, act, W + n)

        @block.vector
        def _(dve):
            linked(c, dve, dve.tensor_tensor(tail[:, :], c.lb_in[:, 0], c.lb_in[:, 1], ALU.max))
            linked(c, dve, dve.tensor_tensor(tail[:, :], tail[:, :], c.lb_in[:, 2], ALU.max))
            dve.tensor_tensor(lb[:, :, :], c.lb_in[:, :, :], tail[:, :].unsqueeze(1).to_broadcast([P, 3, HG]),
                              ALU.subtract).then_inc(lb_step, 1)
            dve.wait_ge(lb_exp, 1)
            linked(c, dve, dve.tensor_reduce(tail[:, :], lb[:, :, :].rearrange("p r h -> p h r"), AX, ALU.add))
            linked(c, dve, dve.reciprocal(tail[:, :], tail[:, :]))
            linked(c, dve, dve.tensor_tensor(lb2[:, 0], lb[:, 0], tail[:, :], ALU.mult))
            linked(c, dve, dve.tensor_scalar(lb2[:, 1], lb2[:, 0], -1.0, 1.0, ALU.mult, ALU.add))
            dve.wait_ge(forget, 1)
            for h in range(HG):
                x = dve.tensor_scalar(c.f[:, h], c.f[:, h], lb2[:, 1, h:h + 1], lb2[:, 0, h:h + 1], ALU.mult, ALU.add)
            x.then_inc(forget, 1)
            dve.wait_ge(forget, 2)
            dve.tensor_scalar(key, c.f[:, :, :], -1.0, 1.0, ALU.mult, ALU.add).then_inc(forget, 1)
            dve.wait_ge(zeroed, 6)
            dve.wait_ge(forget, 4)
            fb = b[:, :, :].rearrange("p h s -> p (h s)")
            linked(c, dve, dve.tensor_tensor_scan(fb, rest, fb, 0.0, ALU.mult, ALU.add))

            def span(l):
                w = widths[l]
                x = dd[l % 2]
                if l >= 3:
                    dve.wait_ge(scaled, l - 2)
                if w <= CHUNK:
                    v, o = halves(b[:, :, :], w), halves(x, w)
                    ref = v[:, :, 0, w - 1:w].to_broadcast([P, HG * S // (2 * w), w])
                    if w < CHUNK:
                        dve.tensor_tensor(o[:, :, 1], v[:, :, 1], ref, ALU.subtract)
                    else:
                        dve.tensor_copy(o[:, :, 1], v[:, :, 1])
                    dve.tensor_tensor(o[:, :, 0], ref, v[:, :, 0], ALU.subtract).then_inc(spans, 1)
                else:
                    v, o = chunks(b[:, :, :]), chunks(x)

                    def last_of(ch):
                        return v[:, :, ch, CHUNK - 1:CHUNK].to_broadcast([P, HG, CHUNK])

                    linked(c, dve, dve.tensor_tensor(tail[:, :], v[:, :, 0, CHUNK - 1], v[:, :, 1, CHUNK - 1], ALU.add))
                    dve.tensor_tensor(o[:, :, 0], tail[:, :].unsqueeze(2).to_broadcast([P, HG, CHUNK]), v[:, :, 0],
                                      ALU.subtract)
                    dve.tensor_tensor(o[:, :, 1], last_of(1), v[:, :, 1], ALU.subtract)
                    dve.tensor_copy(o[:, :, 2], v[:, :, 2])
                    dve.tensor_tensor(o[:, :, 3], last_of(2), v[:, :, 3], ALU.add).then_inc(spans, 1)

            def scale(l):
                w = widths[l]
                dve.wait_ge(decays, l)
                if l >= 3:
                    dve.wait_ge(paired, l - 1)
                dve.tensor_tensor(halves(qq[l % 2][:, :, :], w)[:, :, 1], halves(c.q[:, :, :], w)[:, :, 1],
                                  halves(dd[l % 2], w)[:, :, 1], ALU.mult)
                dve.tensor_tensor(halves(kk[l % 2][:, :, :], w)[:, :, 0], halves(key, w)[:, :, 0],
                                  halves(dd[l % 2], w)[:, :, 0], ALU.mult).then_inc(scaled, 1)

            def mask(l):
                dve.wait_ge(paired, l + 1)
                if l >= 2:
                    dve.wait_ge(summed, l - 1)
                if l == levels - 1:
                    dve.tensor_copy(sm[l % 2][:, 0:512], c.bank[2 * (l % 2)]).then_inc(masked, 1)
                    return
                m = c.ident[:, :] if l == 0 else c.level_mask[:, l - 1]
                dve.tensor_tensor(sm[l % 2].rearrange("p (n t) -> p n t", n=8),
                                  c.psum[:, 2 * (l % 2):2 * (l % 2) + 2, :].rearrange("p b (n t) -> p (b n) t", t=P),
                                  m.unsqueeze(1).to_broadcast([P, 8, P]), ALU.mult).then_inc(masked, 1)

            dve.wait_ge(c.masks_ready, 1)
            for s in range(1, levels + 2):
                if s < levels:
                    span(s)
                if 2 <= s <= levels:
                    scale(s - 1)
                if s <= levels:
                    mask(s - 1) if s == 1 else None
                if s >= 3:
                    mask(s - 2)
            dve.wait_ge(out_step, 1)
            sig = key.rearrange("p h s -> p (h s)").rearrange("p (m n) -> p m n", m=TT)
            linked(c, dve, dve.tensor_tensor(c.hg[:, :, :], c.hg[:, :, :], sig, ALU.mult))
            dve.wait_ge(hg_loaded, 16)
            linked(c, dve, dve.tensor_tensor(c.hg[:, :, :], c.hg[:, :, :],
                                             hnorm[:, :].unsqueeze(1).to_broadcast([P, TT, D2]), ALU.mult))
            dve.wait_ge(out_step, 2)
            squares = kk0[:, :, :].rearrange("p h s -> p (h s)").rearrange("p (m h n) -> p (m h) n", m=TT, h=HG)
            linked(c, dve, dve.tensor_reduce(sq[:, :, :].rearrange("p m h -> p (m h)"), squares, AX, ALU.add))
            dve.tensor_scalar(sq[:, :, :], sq[:, :, :], 1.0 / P, EPS_RMS, ALU.mult, ALU.add).then_inc(out_step, 1)
            dve.wait_ge(out_step, 3)
            dve.reciprocal(sq[:, :, :], sq[:, :, :]).then_inc(out_step, 1)
            dve.wait_ge(out_step, 5)
            for m in range(TT):
                last = dve.tensor_tensor(c.v[:, m].rearrange("p (h n) -> p h n", h=HG),
                                         c.bank[4 + m].rearrange("p (h n) -> p h n", h=HG),
                                         sq[:, m].unsqueeze(2).to_broadcast([P, HG, P]), ALU.mult)
            linked(c, dve, last)
            dve.tensor_tensor(c.v[:, :, :], c.v[:, :, :], c.hg[:, :, :], ALU.mult).then_inc(yb_ready, 1)
            dve.wait_ge(ya_split, 1)
            dve.tensor_tensor(c.xtl[:, 0:4, :], c.ya[:, :, :], c.xth[:, 0:4, :].bitcast(F32), ALU.subtract
                              ).then_inc(ya_split, 1)
            turn_dve(c, dve, 20, c.bank[0:2], 4, 4)
            for p in range(2):
                low(c, dve, W + 2 * p + 2)
                low(c, dve, W + 2 * p + 3)
                add_gated(c, dve, W + 2 * p + 2, c.bank[2 * p + 2:2 * p + 4], p, c.mod[:, 2])
            dve.sem_inc(c.x_ready, 1)

        @block.tensor
        def _(pe):
            def pairs(l):
                q, k = (c.q, key) if l == 0 else (qq[l % 2], kk[l % 2])
                if l == 0:
                    pe.wait_ge(forget, 3)
                else:
                    pe.wait_ge(scaled, l)
                if l >= 2:
                    pe.wait_ge(masked, l - 1)
                for m in range(TT if l < levels - 1 else 1):
                    for h in range(HG):
                        m2 = m if l < levels - 1 else 1
                        mm = pe.matmul(c.bank[2 * (l % 2) + m][:, h * P:h * P + P], k[:, h, m * P:m * P + P],
                                       q[:, h, m2 * P:m2 * P + P], start=True, stop=True)
                mm.then_inc(paired, 1)

            def sums(l):
                pe.wait_ge(masked, l + 1)
                for m in range(TT if l < levels - 1 else 1):
                    for h in range(HG):
                        m2 = m if l < levels - 1 else 1
                        mm = pe.matmul(c.bank[4 + m2][:, h * P:h * P + P],
                                       sm[l % 2][:, (m * HG + h) * P:(m * HG + h + 1) * P],
                                       c.v[:, m, h * P:h * P + P], start=l == 0 and h == 0, stop=l >= levels - 2,
                                       skip_group_check=True)
                mm.then_inc(summed, 1)

            for l in range(levels + 1):
                if l < levels:
                    pairs(l)
                if l >= 1:
                    sums(l - 1)
            pe.wait_ge(yb_ready, 1)
            turn_pe(c, pe, 20, c.v, c.bank[0:2], 4)
            pe.wait_ge(ya_split, 2)
            turned_all(c, pe, 20, 4)
            for p in range(2):
                for h in range(2):
                    n = W + 2 * p + h
                    multiply_rows(c, pe, n, n % RING, h * CK, c.bank[2 * p + 2:2 * p + 4], h == 0, h == 1)
    c.chunk += 4


def add_gated(c, dve, used, banks, p, gate):
    dve.wait_ge(c.used, used)
    cols = slice(p * COLS, p * COLS + COLS)
    for m in range(TT):
        last = dve.tensor_tensor(c.h[:, m, cols], banks[m], gate[:, cols], ALU.mult)
    linked(c, dve, last)
    for m in range(TT):
        last = dve.tensor_tensor(c.x[:, m, cols], c.x[:, m, cols], c.h[:, m, cols], ALU.add)
    linked(c, dve, last)



QUARTERS = 4
QUARTER = 8


def make_mlp(c):
    c.relu_ready = c.sem("relu_ready")
    c.act_high = c.sem("act_high")
    c.square_ready = c.sem("square_ready")
    c.act_ready = c.sem("act_ready")


def phase_mlp(c, layer):
    nc, d = c.nc, c.dram
    W = c.chunk
    last_phase = layer == 1
    done = layer * 2 * QUARTERS
    v, turn = FIRST_RMS + 1 + 2 * layer, 22 + 12 * layer
    n_chunks = QUARTERS * QUARTER

    with ExitStack() as local, nc.Block() as block:
        c.h = c.sb(f"h_mlp{layer}", [P, TT, D], ctx=local)
        relu = c.sb(f"relu{layer}", [P, 2, CK, S], ctx=local)
        square = c.sb(f"square{layer}", [P, CK, S], ctx=local)
        ah = c.sb(f"act_h{layer}", [P, KT, S], F32R, ctx=local)
        al = c.sb(f"act_l{layer}", [P, KT, S], F32R, ctx=local)

        def panel_banks(p):
            return c.psum[:, 4 + 2 * p:6 + 2 * p, :].rearrange("q b (k s) -> q (b k) s", k=2)

        @block.sync
        def _(sp):
            def load(i, q, j):
                load_chunk(c, sp, i * QUARTER + (W + q * QUARTER + j), (W + j) % RING,
                           mlp_source(c, layer, i + q, j))

            with sp.Fori(0, QUARTERS - 1) as i:
                for j in range(LOADED, QUARTER):
                    load(i, 0, j)
                for j in range(LOADED):
                    load(i, 1, j)
            for n in range(n_chunks - QUARTER + LOADED, n_chunks + LOADED):
                src = static_source(c, W + n)
                if src is not None:
                    load_chunk(c, sp, W + n, (W + n) % RING, src)

        @block.scalar
        def _(act):
            act.dma_start(c.norm[:, :], d["norm_mlp_2"][layer].partition_broadcast(P)).then_inc(c.norm_loaded, 16)
            rms_act(c, act, v, c.h)
            turn_act(c, act, turn, c.bank[4:8])
            act.sem_inc(c.relu_ready, 2) if layer == 0 else None

            def quarter(i, more):
                def high_of(j):
                    if j < QUARTER or more:
                        split_high(c, act, i * QUARTER + (W + j), i * (QUARTER // RING) + ((W + j) // RING + 1),
                                   (W + j) % RING)

                for p in range(2):
                    high_of(2 * p + 2)
                    high_of(2 * p + 3)
                    act.wait_ge(c.used, i * QUARTER + (W + 2 * p + 2))
                    act.wait_ge(c.act_ready, i * 2 + (done + p + 1))
                    act.activation(relu[:, p], panel_banks(p), ACT.Relu).then_inc(c.relu_ready, 1)
                    act.wait_ge(c.relu_ready, i * 2 + (done + p + 3))
                    act.activation(ah[:, CK * p:CK * p + CK, :], relu[:, p], ACT.Square).then_inc(c.act_high, 1)
                for j in range(6, 10):
                    high_of(j)

            with act.Fori(0, QUARTERS - 1) as i:
                quarter(i, True)
            quarter(QUARTERS - 1, not last_phase)

        @block.vector
        def _(dve):
            dve.wait_ge(c.norm_loaded, 32 + 32 * layer)
            rms_dve(c, dve, v, c.h, c.mod[:, 4], c.mod[:, 3])
            turn_dve(c, dve, turn, c.bank[4:8])
            dve.sem_inc(c.act_ready, 2) if layer == 0 else None

            def quarter(i, more):
                def low_of(j):
                    if j < QUARTER or more:
                        split_low(c, dve, i * QUARTER + (W + j), (W + j) % RING)

                for p in range(2):
                    low_of(2 * p + 2)
                    low_of(2 * p + 3)
                    dve.wait_ge(c.relu_ready, i * 2 + (done + p + 3))
                    dve.wait_ge(c.act_ready, i * 2 + (done + p + 2))
                    dve.tensor_tensor(square[:, :, :], relu[:, p], relu[:, p], ALU.mult).then_inc(c.square_ready, 1)
                    dve.wait_ge(c.square_ready, i * 2 + (done + p + 1))
                    dve.wait_ge(c.act_high, i * 2 + (done + p + 1))
                    part = slice(CK * p, CK * p + CK)
                    dve.tensor_tensor(al[:, part, :], square[:, :, :], ah[:, part, :].bitcast(F32), ALU.subtract
                                      ).then_inc(c.act_ready, 1)
                for j in range(6, 10):
                    low_of(j)

            with dve.Fori(0, QUARTERS - 1) as i:
                quarter(i, True)
            quarter(QUARTERS - 1, not last_phase)
            for p in range(2):
                add_gated(c, dve, W + n_chunks - 1 + p, (c.bank[p], c.bank[2 + p]), p, c.mod[:, 5])
            dve.sem_inc(c.x_ready, 1)

        @block.tensor
        def _(pe):
            pe.wait_ge(c.h_ready, 2 * layer + 2)
            turn_pe(c, pe, turn, c.h, c.bank[4:8])
            turned_all(c, pe, turn)

            def quarter(i, first):
                for p in range(2):
                    pe.wait_ge(c.relu_ready, i * 2 + (done + p + 1))
                    for h in range(2):
                        j = 2 * p + h
                        multiply_cols(c, pe, i * QUARTER + (W + j), (W + j) % RING, h * CK,
                                      c.bank[4 + 2 * p:6 + 2 * p], h == 0, h == 1)
                for h in range(2):
                    pe.wait_ge(c.act_ready, i * 2 + (done + h + 3))
                    for p in range(2):
                        j = 4 + 2 * h + p
                        multiply_rows(c, pe, i * QUARTER + (W + j), (W + j) % RING, h * CK,
                                      (c.bank[p], c.bank[2 + p]), first and h == 0, False, ah, al, True)

            quarter(0, True)
            with pe.Fori(1, QUARTERS) as i:
                quarter(i, False)
    c.chunk += n_chunks



SB = 16
SD = D // SB


def phase_qkv(c):
    nc, d = c.nc, c.dram
    W = c.chunk
    panels = 6
    gains_loaded = c.sem("gains_loaded")
    evacuated = c.sem("qkv_evacuated")
    squares = c.sem("head_squares")
    head_rv, head_rs = c.sem("head_rv"), c.sem("head_rs")
    normed = c.sem("head_normed")
    qk_turned = c.sem("qk_turned")
    qk_kept = c.sem("qk_kept")
    masked = c.sem("strict_step")
    cm = c.sbctx
    c.v16 = c.sb("v16", [P, TT, D], ctx=cm)
    c.qt = c.sb("qt", [P, KT, S], ctx=cm)
    c.kt = c.sb("kt", [P, KT, S], ctx=cm)
    c.strict = c.sb("strict", [P, P], ctx=cm)
    c.ones = c.sb("ones_sb", [P, S], ctx=cm)

    with ExitStack() as local, nc.Block() as block:
        c.h = c.sb("h_qkv", [P, TT, D], ctx=local)
        tokens = c.sb("qk", [P, TT, D], ctx=local)
        gain = c.sb("qk_gain", [P, 2, SD], ctx=local)
        ss = c.sb("head_ss", [P, TT * SB], ctx=local)
        heads = tokens[:, :, :].rearrange("p m (h n) -> p (m h) n", n=SD)
        squared = c.h[:, :, :].rearrange("p m n -> p (m n)")

        @block.sync
        def _(sp):
            load_static(c, sp, 2 * panels)

        @block.gpsimd
        def _(pool):
            pool.memset(c.ones[:, :], 1.0).then_inc(masked, 1)
            pool.wait_ge(masked, 1)
            pool.affine_select(out=c.strict[:, :], in_=c.ones[:, 0:P], compare_op=ALU.is_gt, fill=0.0, base=0,
                               pattern=[[-1, P]], channel_multiplier=1).then_inc(masked, 1)
            pool.wait_ge(masked, 2)

        @block.scalar
        def _(act):
            for j, name in enumerate(("q_norm_2", "k_norm_2")):
                act.dma_start(gain[:, j, :], d[name][0].partition_broadcast(P)).then_inc(gains_loaded, 16)
            rms_act(c, act, FIRST_RMS + 2, c.h)
            turn_act(c, act, 26, c.bank[4:8])
            for p in range(panels):
                high(c, act, W + 2 * p + 2)
                high(c, act, W + 2 * p + 3)
                if p in (1, 3):
                    t = p // 2
                    act.wait_ge(evacuated, p + 1)
                    act.activation(squared, tokens[:, :, :].rearrange("p m n -> p (m n)"), ACT.Square
                                   ).then_inc(squares, 1)
                    act.wait_ge(head_rv, t + 1)
                    act.activation(ss[:, :], ss[:, :], ACT.Sqrt).then_inc(head_rs, 1)
                    for b in range(4):
                        act.wait_ge(qk_turned, 4 * t + b + 1)
                        act.activation((c.qt, c.kt)[t][:, 2 * b:2 * b + 2, :],
                                       c.bank[4 + b].rearrange("p (k s) -> p k s", k=2), ACT.Copy).then_inc(qk_kept, 1)

        @block.vector
        def _(dve):
            dve.wait_ge(c.norm_loaded, 48)
            rms_dve(c, dve, FIRST_RMS + 2, c.h, c.mod[:, 1], c.mod[:, 0])
            turn_dve(c, dve, 26, c.bank[4:8])
            dve.wait_ge(gains_loaded, 32)
            linked(c, dve, dve.tensor_scalar(gain[:, 0], gain[:, 0], SD ** -0.5, None, ALU.mult))
            for p in range(panels):
                low(c, dve, W + 2 * p + 2)
                low(c, dve, W + 2 * p + 3)
                dve.wait_ge(c.used, W + 2 * p + 2)
                if p == 2:
                    dve.wait_ge(qk_turned, 4)
                cols = slice(p % 2 * COLS, p % 2 * COLS + COLS)
                out = c.v16 if p >= 4 else tokens
                dve.tensor_copy(out[:, :, cols], c.psum[:, p % 2 * 2:p % 2 * 2 + 2, :]).then_inc(evacuated, 1)
                if p in (1, 3):
                    t = p // 2
                    dve.wait_ge(squares, t + 1)
                    linked(c, dve, dve.tensor_reduce(ss[:, :], c.h[:, :, :].rearrange("p m (h n) -> p (m h) n", n=SD),
                                                     AX, ALU.add))
                    linked(c, dve, dve.tensor_scalar(ss[:, :], ss[:, :], 1.0 / SD, EPS_RMS, ALU.mult, ALU.add))
                    dve.reciprocal(ss[:, :], ss[:, :]).then_inc(head_rv, 1)
                    dve.wait_ge(evacuated, p + 1)
                    linked(c, dve, dve.tensor_tensor(heads, heads, gain[:, t].unsqueeze(1).to_broadcast(
                        [P, TT * SB, SD]), ALU.mult))
                    dve.wait_ge(head_rs, t + 1)
                    dve.tensor_tensor(heads, heads, ss[:, :].unsqueeze(2).to_broadcast([P, TT * SB, SD]), ALU.mult
                                      ).then_inc(normed, 1)

        @block.tensor
        def _(pe):
            pe.wait_ge(c.h_ready, 3)
            turn_pe(c, pe, 26, c.h, c.bank[4:8])
            turned_all(c, pe, 26)
            for p in range(panels):
                if p >= 2:
                    pe.wait_ge(evacuated, p - 1)
                for h in range(2):
                    n = W + 2 * p + h
                    multiply_rows(c, pe, n, n % RING, h * CK, c.bank[p % 2 * 2:p % 2 * 2 + 2], h == 0, h == 1)
                if p in (1, 3):
                    t = p // 2
                    pe.wait_ge(normed, t + 1)
                    for k in range(KT):
                        if t == 1 and k % 2 == 0:
                            pe.wait_ge(qk_kept, k // 2 + 1)
                        for m in range(TT):
                            x = pe.transpose(c.bank[4 + k // 2][:, (k % 2) * S + m * P:(k % 2) * S + m * P + P],
                                             tokens[:, m, k * P:k * P + P], c.ident[:, :])
                        if k % 2:
                            x.then_inc(qk_turned, 1)
    c.chunk += 2 * panels



def phase_stick(c):
    nc, d = c.nc, c.dram
    W = c.chunk
    units = SB
    scored = c.sem("z_scored")
    soft = c.sem("z_soft")
    beta = c.sem("log_beta")
    swept = c.sem("swept")
    args = c.sem("stick_args")
    exped = c.sem("stick_exped")
    weighed = c.sem("stick_weighed")
    flipped = c.sem("stick_flipped")
    keyed = c.sem("stick_keyed")
    mixed = c.sem("stick_mixed")
    kept = c.sem("stick_kept")
    zero = c.sem("edge_zero")

    with ExitStack() as local, nc.Block() as block:
        c.h = o = c.sb("o16", [P, TT, D], ctx=local)
        t1 = c.sb("soft", [P, 2, 2, S], ctx=local)
        lb = c.sb("log_beta_sb", [P, 2, 2, S], ctx=local)
        lom = c.sb("lom", [P, 2, S], ctx=local)
        later = c.sb("later", [P, 2, S + 1], ctx=local)
        at = c.sb("weights_t", [P, 2, 512], ctx=local)

        def width(u):
            return P * (u % 2 + 1)

        @block.sync
        def _(sp):
            load_static(c, sp, 4)

        @block.gpsimd
        def _(pool):
            pool.memset(later[:, :, :], 0.0).then_inc(zero, 1)

        @block.tensor
        def _(pe):
            def scores(u):
                if u >= 2:
                    pe.wait_ge(beta, 3 * (u - 1) - 1)
                m = u % 2
                for j in range(2):
                    half = slice(j * 64, j * 64 + 64)
                    mm = pe.matmul(c.bank[2 * m + j][:, 0:width(u)], c.qt[half, u // 2, m * P:m * P + P],
                                   c.kt[half, u // 2, 0:width(u)], start=True, stop=True)
                mm.then_inc(scored, 1)

            def flip(u):
                pe.wait_ge(weighed, u + 1)
                if u >= 2:
                    pe.wait_ge(keyed, u - 1)
                for j in range(2):
                    for k in range(u % 2 + 1):
                        t = pe.transpose(c.bank[4 + u % 2][:, (2 * j + k) * P:(2 * j + k) * P + P],
                                         t1[:, u % 2, j, k * P:k * P + P], c.ident[:, :])
                t.then_inc(flipped, 1)

            def mix(u):
                pe.wait_ge(keyed, u + 1)
                if u >= 2:
                    pe.wait_ge(kept, u - 1)
                for j in range(2):
                    for k in range(u % 2 + 1):
                        v0 = (u // 2 * 2 + j) * SD
                        mm = pe.matmul(c.bank[6 + u % 2][:, j * SD:j * SD + SD],
                                       at[:, u % 2, (2 * j + k) * P:(2 * j + k) * P + P], c.v16[:, k, v0:v0 + SD],
                                       start=k == 0, stop=k == u % 2)
                mm.then_inc(mixed, 1)

            for u in range(units + 3):
                if u < units:
                    scores(u)
                if u >= 3:
                    mix(u - 3)
                if 2 <= u <= units + 1:
                    flip(u - 2)
            pe.wait_ge(kept, units)
            turn_pe(c, pe, 30, o, c.bank[4:8])
            turned_all(c, pe, 30)
            for p in range(2):
                for h in range(2):
                    n = W + 2 * p + h
                    multiply_rows(c, pe, n, n % RING, h * CK, c.bank[2 * p:2 * p + 2], h == 0, h == 1)

        @block.scalar
        def _(act):
            def softs(u):
                t = t1[:, u % 2, :, 0:width(u)]
                act.wait_ge(scored, u + 1)
                if u >= 2:
                    act.wait_ge(flipped, u - 1)
                act.activation(t, c.psum[:, 2 * (u % 2):2 * (u % 2) + 2, 0:width(u)], ACT.Abs).then_inc(soft, 1)
                act.wait_ge(soft, 3 * u + 1)
                act.activation(t, t, ACT.Exp, scale=-1.0).then_inc(soft, 1)
                act.wait_ge(soft, 3 * u + 2)
                act.activation(t, t, ACT.Ln, bias=1.0).then_inc(soft, 1)

            def weights(u):
                act.wait_ge(args, u + 1)
                t = t1[:, u % 2, :, 0:width(u)]
                act.activation(t, lb[:, u % 2, :, 0:width(u)], ACT.Exp).then_inc(exped, 1)

            def key(u):
                act.wait_ge(flipped, u + 1)
                if u >= 2:
                    act.wait_ge(mixed, u - 1)
                for j in range(2):
                    cols = slice(2 * j * P, 2 * j * P + width(u))
                    x = act.activation(at[:, u % 2, cols], c.bank[4 + u % 2][:, cols], ACT.Copy)
                x.then_inc(keyed, 1)

            for u in range(units + 2):
                if u >= 2:
                    key(u - 2)
                if u < units:
                    softs(u)
                if 1 <= u <= units:
                    weights(u - 1)
            turn_act(c, act, 30, c.bank[4:8])
            for n in range(AHEAD, 4 + AHEAD):
                high(c, act, W + n)

        @block.vector
        def _(dve):
            dve.wait_ge(zero, 1)

            def stick(u):
                w = width(u)
                diag = slice(w - P, w)
                z = c.psum[:, 2 * (u % 2):2 * (u % 2) + 2, 0:w]
                b = lb[:, u % 2, :, 0:w]
                dve.wait_ge(soft, 3 * u + 3)
                if u >= 2:
                    dve.wait_ge(exped, u - 1)
                dve.scalar_tensor_tensor(b, z, 0.0, t1[:, u % 2, :, 0:w], ALU.min, ALU.subtract).then_inc(beta, 1)
                dve.wait_ge(beta, 3 * u + 1)
                if u >= 1:
                    dve.wait_ge(swept, u)
                dve.tensor_tensor(lom[:, :, 0:w], b, z, ALU.subtract).then_inc(beta, 1)
                dve.wait_ge(beta, 3 * u + 2)
                dve.tensor_tensor(lom[:, :, diag], lom[:, :, diag], c.strict[:, :].unsqueeze(1).to_broadcast([P, 2, P]),
                                  ALU.mult).then_inc(beta, 1)
                dve.wait_ge(beta, 3 * u + 3)
                if u >= 1:
                    dve.wait_ge(args, u)
                for j in range(2):
                    x = dve.tensor_tensor_scan(later[:, j, S - w:S][:, ::-1], c.ones[:, 0:w], lom[:, j, 0:w][:, ::-1],
                                               0.0, ALU.mult, ALU.add)
                x.then_inc(swept, 1)
                dve.wait_ge(swept, u + 1)
                dve.tensor_tensor(b, b, later[:, :, S - w + 1:S + 1], ALU.add).then_inc(args, 1)

            def weigh(u):
                diag = slice(width(u) - P, width(u))
                dve.wait_ge(exped, u + 1)
                t = t1[:, u % 2, :, diag]
                dve.tensor_tensor(t, t, c.strict[:, :].unsqueeze(1).to_broadcast([P, 2, P]), ALU.mult
                                  ).then_inc(weighed, 1)

            def keep(u):
                dve.wait_ge(mixed, u + 1)
                dve.tensor_copy(o[:, u % 2, u // 2 * P:u // 2 * P + P], c.bank[6 + u % 2][:, 0:P]).then_inc(kept, 1)

            for u in range(units + 3):
                if u < units:
                    stick(u)
                if 1 <= u <= units:
                    weigh(u - 1)
                if u >= 3:
                    keep(u - 3)
            turn_dve(c, dve, 30, c.bank[4:8])
            for p in range(2):
                low(c, dve, W + 2 * p + 2)
                low(c, dve, W + 2 * p + 3)
                add_gated(c, dve, W + 2 * p + 2, c.bank[2 * p:2 * p + 2], p, c.mod[:, 2])
            dve.sem_inc(c.x_ready, 1)
    c.chunk += 4


def phase_store(c, out):
    stored = c.sem("stored")
    with c.nc.Block() as block:
        @block.sync
        def _(sp):
            sp.wait_ge(c.x_ready, FIRST_RMS + 4)
            for m in range(TT):
                sp.dma_start(out[0, m * P:m * P + P, :], c.x[:, m]).then_inc(stored, 16)
            sp.wait_ge(stored, 16 * TT)


def program(nc, dram, out):
    with ExitStack() as ctx:
        c = make(nc, ctx, dram)
        with ExitStack() as c.moe:
            make_routing(c)
            with ExitStack() as c.mix:
                phase_in(c)
                phase_attend(c)
                phase_merge(c)
            with ExitStack() as c.exp:
                phase_experts(c)
                phase_spill(c)
        c.second = c.chunk
        with ExitStack() as c.two:
            make_second(c)
            phase_modulate(c, 0)
            with ExitStack() as c.hgrn:
                phase_project_ab(c)
                phase_recur(c)
            make_mlp(c)
            phase_mlp(c, 0)
            phase_modulate(c, 1)
            with ExitStack() as c.sbctx:
                phase_qkv(c)
                phase_stick(c)
            phase_mlp(c, 1)
        phase_store(c, out)


NAMES = ["x", "ln_in_g", "ln_in_b", "w_in", "b_gate", "lambda_q1", "lambda_k1", "lambda_q2", "lambda_k2",
         "subln_w", "rel_bias", "w_branch_a", "w_branch_b", "w_out", "ln1_g", "ln1_b", "w_router", "b_router",
         "w_exp_in", "b_exp_in", "w_exp_out", "b_exp_out", "ln2_g", "ln2_b", "c_2", "ada_w_2", "ada_b_2",
         "norm_mix_2", "norm_mlp_2", "w_in_ab_2", "conv_w_2", "hg_norm_2", "lb_logits_2", "w_out_ab_2",
         "w_qkv_2", "q_norm_2", "k_norm_2", "w_out_c_2", "mlp_w1_2", "mlp_w2_2"]


def kernel(**inputs):
    import numpy as np
    import concourse.bacc as bacc
    from concourse.bass_utils import run_bass_kernel_spmd

    nc = bacc.Bacc("TRN2", target_bir_lowering=False, num_devices=1)
    arrays = {f"in_{n}": np.ascontiguousarray(inputs[n]) for n in NAMES}
    dram = {n: nc.dram_tensor(f"in_{n}", arrays[f"in_{n}"].shape, F32, kind="ExternalInput").ap() for n in NAMES}
    out = nc.dram_tensor("out", (1, S, D), F32, kind="ExternalOutput").ap()
    program(nc, dram, out)
    return run_bass_kernel_spmd(nc, [arrays], core_ids=[0]).results[0]["out"]
```

```python
import math
from contextlib import ExitStack

import concourse.bass as bass
import concourse.mybir as mybir

F32 = mybir.dt.float32
F32R = mybir.dt.float32r
I32 = mybir.dt.int32
ALU = mybir.AluOpType
ACT = mybir.ActivationFunctionType
AX = mybir.AxisListType.X
ds = bass.ds

P = 128
D = 1024
S = 256
TT = S // P
KT = D // P
COLS = 512
CK = 4
RING = 4
AHEAD = 2
LOADED = AHEAD + RING
NEG = -1e30
EPS_LN = 1e-5
EPS_RMS = 1e-6
SCALE = 64 ** -0.5

HA, DA = 4, 64
HB = 8
CHUNK = 64
CLIP = 128
LAM_INIT = 0.8 - 0.6 * math.exp(-0.3 * 0)
RES = 2.0 ** 0.25
E = 32
TOPK = 4
CAP = 64
PASSES = S // CAP


class Core:

    def __init__(self, nc, ctx, dram):
        self.nc, self.ctx, self.dram = nc, ctx, dram
        self.chunk = 0
        self.chain = 0
        self.parts = 0

    def sb(self, name, shape, dt=F32, ctx=None):
        return (ctx or self.ctx).enter_context(self.nc.sbuf_tensor(name, shape, dt))

    def sem(self, name):
        return self.ctx.enter_context(self.nc.semaphore(name))


class Stream:

    def __init__(self, c, name, first, first_lap):
        self.raw, self.wh, self.wl = c.raw, c.wh, c.wl
        self.first, self.first_lap = first, first_lap
        self.arrived = [c.sem(f"{name}arrived{s}") for s in range(RING)]
        self.high_ready = c.sem(name + "high_ready")
        self.low_ready = c.sem(name + "low_ready")
        self.used = c.sem(name + "used")


def rows_cols(matrix, row, col):
    return matrix[ds(row, CK * P), ds(col, COLS)].rearrange("(k p) n -> p k n", p=P)


def make(nc, ctx, dram):
    c = Core(nc, ctx, dram)
    c.ident = c.sb("ident", [P, P])
    c.raw = c.sb("raw", [P, RING, CK, COLS])
    c.wh = c.sb("wh", [P, RING, CK, COLS], F32R)
    c.wl = c.sb("wl", [P, RING, CK, COLS], F32R)
    c.xth = c.sb("xth", [P, KT, S], F32R)
    c.xtl = c.sb("xtl", [P, KT, S], F32R)
    c.x = c.sb("x", [P, TT, D])
    c.stats = c.sb("stats", [P, TT, 2, 6])
    c.mv = c.sb("mv", [P, TT, 2])
    c.rv = c.sb("rv", [P, TT])
    c.rs = c.sb("rs", [P, TT])
    c.psum = ctx.enter_context(nc.psum_tensor("banks", [P, 8, COLS], F32))
    c.bank = [c.psum[:, b, :] for b in range(8)]
    c.arrived = [c.sem(f"arrived{s}") for s in range(RING)]
    c.high_ready = c.sem("high_ready")
    c.low_ready = c.sem("low_ready")
    c.used = c.sem("used")
    c.rv_ready = c.sem("rv_ready")
    c.rs_ready = c.sem("rs_ready")
    c.turned = c.sem("turned")
    c.xh_ready = c.sem("xh_ready")
    c.xl_ready = c.sem("xl_ready")
    c.vec_step = c.sem("vec_step")
    c.silu = c.sb("silu_c", [P, KT, 2 * PANELS - 1])
    c.mod_rows = nc.dram_tensor("mod_rows", [2 * PANELS, COLS], F32).ap()
    c.mod_stored = c.sem("mod_stored")
    c.mod_loaded = c.sem("mod_loaded")
    return c



def load_chunk(c, sp, n, slot, src, whole=False):
    if not isinstance(n, int) or n >= RING:
        sp.wait_ge(c.used if whole else c.low_ready, n - RING + 1)
    sp.dma_start(c.raw[:, slot], src).then_inc(c.arrived[slot], 16)


def split_high(c, act, n, lap, slot):
    act.wait_ge(c.arrived[slot], lap * 16)
    if not isinstance(n, int) or n >= RING:
        act.wait_ge(c.used, n - RING + 1)
    act.activation(c.wh[:, slot], c.raw[:, slot], ACT.Copy).then_inc(c.high_ready, 1)


def split_low(c, dve, n, slot):
    dve.wait_ge(c.high_ready, n + 1)
    dve.tensor_tensor(c.wl[:, slot], c.raw[:, slot], c.wh[:, slot].bitcast(F32),
                      ALU.subtract).then_inc(c.low_ready, 1)


def multiply_rows(c, pe, n, slot, k0, banks, first, last, xh=None, xl=None, long=False):
    xh, xl = xh or c.xth, xl or c.xtl
    pe.wait_ge(c.low_ready, n + 1)
    for k in range(CK):
        for m in range(len(banks)):
            toks = slice(m * P, m * P + P)
            for j, (x, w) in enumerate(((xh, c.wh), (xh, c.wl), (xl, c.wh))):
                mm = pe.matmul(banks[m][:, :], x[:, k0 + k, toks], w[:, slot, k],
                               start=first and k == 0 and j == 0, stop=last and k == CK - 1 and j == 2,
                               skip_group_check=long)
    mm.then_inc(c.used, 1)


def multiply_cols(c, pe, n, slot, k0, banks, first, last, xh=None, xl=None):
    xh, xl = xh or c.xth, xl or c.xtl
    pe.wait_ge(c.low_ready, n + 1)
    for k in range(CK):
        for b in range(COLS // P):
            out = banks[b // 2][:, (b % 2) * S:(b % 2) * S + S]
            cols = slice(b * P, b * P + P)
            for j, (w, x) in enumerate(((c.wh, xh), (c.wh, xl), (c.wl, xh))):
                mm = pe.matmul(out, w[:, slot, k, cols], x[:, k0 + k, :],
                               start=first and k == 0 and j == 0 and b % 2 == 0,
                               stop=last and k == CK - 1 and j == 2, skip_group_check=True)
    mm.then_inc(c.used, 1)



def linked(c, dve, ins):
    c.chain += 1
    ins.then_inc(c.vec_step, 1)
    dve.wait_ge(c.vec_step, c.chain)


def root_act(c, act, v):
    act.wait_ge(c.rv_ready, v + 1)
    act.activation(c.rs[:, :], c.rv[:, :], ACT.Sqrt).then_inc(c.rs_ready, 1)


def layer_norm_dve(c, dve, v, x, gain, shift):
    for m in range(TT):
        for h in range(2):
            st = dve.bn_stats(c.stats[:, m, h, :], x[:, m, h * 512:h * 512 + 512])
    linked(c, dve, st)
    for m in range(TT):
        agg = dve.bn_aggr(c.mv[:, m, :], c.stats[:, m].rearrange("p a b -> p (a b)"))
    linked(c, dve, agg)
    linked(c, dve, dve.tensor_scalar(c.rv[:, :], c.mv[:, :, 1], EPS_LN, None, ALU.add))
    dve.reciprocal(c.rv[:, :], c.rv[:, :]).then_inc(c.rv_ready, 1)
    for m in range(TT):
        last = dve.scalar_tensor_tensor(x[:, m], x[:, m], c.mv[:, m, 0:1], gain, ALU.subtract, ALU.mult)
    linked(c, dve, last)
    dve.wait_ge(c.rs_ready, v + 1)
    for m in range(TT):
        last = dve.scalar_tensor_tensor(x[:, m], x[:, m], c.rs[:, m:m + 1], shift, ALU.mult, ALU.add)
    linked(c, dve, last)


def turn_pe(c, pe, v, x, banks, kt=KT):
    for k in range(kt):
        for m in range(TT):
            t = pe.transpose(banks[k // 2][:, (k % 2) * S + m * P:(k % 2) * S + m * P + P],
                             x[:, m, k * P:k * P + P], c.ident[:, :])
        if k % 2:
            t.then_inc(c.turned, 1)


def turn_act(c, act, v, banks, kt=KT, at=0):
    for b in range(kt // 2):
        act.wait_ge(c.turned, v + b + 1)
        act.activation(c.xth[:, at + 2 * b:at + 2 * b + 2, :], banks[b][:, :].rearrange("p (k s) -> p k s", k=2),
                       ACT.Copy).then_inc(c.xh_ready, 1)


def turn_dve(c, dve, v, banks, kt=KT, at=0):
    for b in range(kt // 2):
        dve.wait_ge(c.xh_ready, v + b + 1)
        part = slice(at + 2 * b, at + 2 * b + 2)
        dve.tensor_tensor(c.xtl[:, part, :], banks[b][:, :].rearrange("p (k s) -> p k s", k=2),
                          c.xth[:, part, :].bitcast(F32), ALU.subtract).then_inc(c.xl_ready, 1)


def turned_all(c, pe, v, kt=KT):
    pe.wait_ge(c.xl_ready, v + kt // 2)



PANEL = 2
PANELS = 6 * D // COLS


class ModPart:

    def __init__(self, c, layer, first, count, bank, rows, name):
        self.layer, self.first, self.count, self.bank = layer, first, count, bank
        self.chunks = PANEL * count
        self.W = c.chunk
        c.parts += 1
        self.stored = 16 * c.parts
        self.rows = rows
        self.loaded = c.sem(name + "bias_loaded")
        self.done = c.sem(name + "done")


def ada_source(c, layer, j):
    return rows_cols(c.dram["ada_w_2"][layer], j % 2 * 512, j // 2 * COLS)


def mod_chunk(c, pe, part, j):
    if j >= part.chunks:
        return
    p, h, n = j // PANEL, j % PANEL, part.W + j
    pe.wait_ge(c.arrived[n % RING], (n // RING + 1) * 16)
    for k in range(CK):
        mm = pe.matmul(c.bank[part.bank][0:part.count, :],
                       c.silu[:, h * CK + k, PANELS - 1 - p:PANELS - 1 - p + part.count],
                       c.raw[:, n % RING, k], start=j == 0 and k == 0,
                       stop=j == part.chunks - 1 and k == CK - 1, skip_group_check=True)
    mm.then_inc(c.used, 1)



LOW_ROW = 32


def mod_split_pe(c, pe, part, j, silu):
    if j >= part.chunks:
        return
    p, h, n = j // PANEL, j % PANEL, part.W + j
    pe.wait_ge(c.low_ready, n + 1)
    for k in range(CK):
        for q, w in enumerate((c.wh, c.wl)):
            mm = pe.matmul(c.bank[part.bank][0:LOW_ROW + part.count, :],
                           silu[:, h * CK + k, part.count - 1 - p:part.count - 1 - p + LOW_ROW + part.count],
                           w[:, n % RING, k], start=j == 0 and k == 0 and q == 0,
                           stop=j == part.chunks - 1 and k == CK - 1 and q == 1, skip_group_check=True)
    mm.then_inc(c.used, 1)


def mod_silu(c, name, count, ctx):
    return c.sb(name, [P, KT, LOW_ROW + 2 * count - 1], F32R, ctx=ctx)


def mod_silu_act(c, act, silu, count, zero, split):
    act.wait_ge(zero, 1)
    act.activation(silu[:, :, count - 1], c.silu[:, :, PANELS - 1], ACT.Copy).then_inc(split, 1)


def mod_silu_dve(c, dve, silu, count, split):
    dve.wait_ge(split, 1)
    dve.tensor_tensor(silu[:, :, LOW_ROW + count - 1], c.silu[:, :, PANELS - 1], silu[:, :, count - 1].bitcast(F32),
                      ALU.subtract).then_inc(split, 1)


def mod_rows_dve(c, dve, part):
    dve.wait_ge(c.used, part.W + part.chunks)
    dve.wait_ge(part.loaded, 16)
    linked(c, dve, dve.tensor_tensor(part.rows, c.bank[part.bank][0:part.count, :], part.rows, ALU.add))
    dve.tensor_tensor(part.rows, c.bank[part.bank][LOW_ROW:LOW_ROW + part.count, :], part.rows, ALU.add
                      ).then_inc(part.done, 1)


def mod_passed(c, eng, split_ready, part):
    eng.wait_ge(c.used, part.W + part.chunks)
    eng.sem_inc(split_ready, part.chunks)


def mod_bias_load(c, act, part):
    lo = part.first * COLS
    act.dma_start(part.rows, c.dram["ada_b_2"][part.layer, lo:lo + part.count * COLS].rearrange(
        "(j n) -> j n", n=COLS)).then_inc(part.loaded, 16)


def mod_bias_dve(c, dve, part):
    dve.wait_ge(c.used, part.W + part.chunks)
    dve.wait_ge(part.loaded, 16)
    dve.tensor_tensor(part.rows, c.bank[part.bank][0:part.count, :], part.rows, ALU.add).then_inc(part.done, 1)


def mod_store_act(c, act, part):
    act.wait_ge(part.done, 1)
    row = part.layer * PANELS + part.first
    act.dma_start(c.mod_rows[row:row + part.count, :], part.rows).then_inc(c.mod_stored, 16)


def mod_load(c, act, layer, pieces):
    for j in pieces:
        row = layer * PANELS + j * (D // COLS)
        act.dma_start(c.mod[:, j, :], c.mod_rows[row:row + D // COLS, :].rearrange("j n -> (j n)").partition_broadcast(P)
                      ).then_inc(c.mod_loaded, 16)



def phase_in(c):
    nc, d = c.nc, c.dram
    W = c.chunk
    panels = 10
    after = panels * 2
    w_in = d["w_in"][0]
    c.qka = c.sb("qka", [P, 2, 4, S], ctx=c.mix)
    c.qkb = c.sb("qkb", [P, 2, 4, S], ctx=c.mix)
    c.va = c.sb("va", [P, TT, 512], ctx=c.mix)
    c.vb = c.sb("vb", [P, TT, 512], ctx=c.mix)
    c.gates = c.sb("gates", [P, TT, 2 * D], ctx=c.mix)
    c.flip = c.sb("flip", [P, P], ctx=c.mix)
    c.mask = c.sb("mask", [P, TT, S], ctx=c.mix)
    c.alibi = c.sb("alibi", [P, HA, TT, S], ctx=c.mix)
    c.rel = c.sb("rel", [P, HB, 384], ctx=c.mix)
    c.lam_in = c.sb("lam_in", [P, 2, 2, DA], ctx=c.mix)
    c.subln = c.sb("subln", [P, 128], ctx=c.mix)
    rel_rows = nc.dram_tensor("rel_rows", [HB, 512], F32).ap()
    x_loaded = c.sem("x_loaded")
    bias_loaded = c.sem("bias_loaded")
    rel_stored = c.sem("rel_stored")
    c.rel_loaded = c.sem("rel_loaded")
    pool_step = c.sem("pool_step")
    c.bias_ready = c.sem("bias_ready")
    c.small_loaded = c.sem("small_loaded")
    norm_loaded = c.sem("norm_loaded")
    gate_loaded = c.sem("gate_loaded")
    ident_step = c.sem("ident_step")
    normed = c.sem("normed")
    evacuated = c.sem("in_evacuated")
    gates_ready = c.gates_ready = c.sem("gates_ready")
    kinds = "TTNTTNNNNN"
    outs = [c.qka[:, 0], c.qka[:, 1], c.va, c.qkb[:, 0], c.qkb[:, 1], c.vb]

    with ExitStack() as local, nc.Block() as block:
        gain = c.sb("ln_in_gain", [P, D], ctx=local)
        shift = c.sb("ln_in_shift", [P, D], ctx=local)
        rel_wide = c.sb("rel_wide", [HB, 512], ctx=local)
        dist = c.sb("dist", [P, TT, S], ctx=local)
        away = c.sb("away", [P, TT, S], ctx=local)

        @block.sync
        def _(sp):
            for m in range(TT):
                sp.dma_start(c.x[:, m], d["x"][0, m * P:m * P + P, :]).then_inc(x_loaded, 16)
            for n in range(LOADED):
                load_chunk(c, sp, W + n, n % RING, rows_cols(w_in, n % 2 * 512, n // 2 * COLS))
            with sp.Fori(0, 3) as i:
                for j in range(4):
                    load_chunk(c, sp, i * 4 + (W + LOADED + j), (LOADED + j) % RING,
                               rows_cols(w_in, j % 2 * 512, i * (2 * COLS) + (3 + j // 2) * COLS))
            for n in range(18, after):
                load_chunk(c, sp, W + n, n % RING, rows_cols(w_in, n % 2 * 512, n // 2 * COLS))
            for n in range(after, after + RING):
                load_chunk(c, sp, W + n, n % RING, ada_source(c, 0, n - after))

        @block.gpsimd
        def _(pool):
            pool.memset(c.ident[:, :], 0.0).then_inc(ident_step, 1)
            pool.wait_ge(ident_step, 1)
            pool.affine_select(out=c.ident[:, :], in_=c.ident[:, :], compare_op=ALU.not_equal, fill=1.0, base=0,
                               pattern=[[-1, P]], channel_multiplier=1).then_inc(ident_step, 1)
            steps = 0

            def done(ins):
                nonlocal steps
                steps += 1
                ins.then_inc(pool_step, 1)
                pool.wait_ge(pool_step, steps)

            pool.wait_ge(bias_loaded, 16)
            lo, hi = S - 1 - CLIP, S - 1 + CLIP
            pool.tensor_copy(rel_wide[:, 0:lo], rel_wide[:, lo:lo + 1].to_broadcast([HB, lo]))
            done(pool.tensor_copy(rel_wide[:, hi + 1:512], rel_wide[:, hi:hi + 1].to_broadcast([HB, 511 - hi])))
            pool.dma_start(rel_rows, rel_wide[:, :]).then_inc(rel_stored, 16)
            pool.wait_ge(rel_stored, 16)
            for h in range(HB):
                pool.dma_start(c.rel[:, h, :], bass.AP(tensor=rel_rows.tensor, offset=h * 512, ap=[[1, P], [1, 384]])
                               ).then_inc(c.rel_loaded, 16)
            done(pool.memset(c.flip[:, :], 0.0))
            done(pool.affine_select(out=c.flip[:, :], in_=c.flip[:, :], compare_op=ALU.not_equal, fill=1.0,
                                    base=1 - P, pattern=[[1, P]], channel_multiplier=1))
            done(pool.memset(c.mask[:, :, :], 0.0))
            for m in range(TT):
                done(pool.memset(c.mask[0:CHUNK, m, m * P + CHUNK:S], NEG))
                if m < TT - 1:
                    done(pool.memset(c.mask[CHUNK:P, m, m * P + P:S], NEG))
            done(pool.iota(dist[:, :, :], pattern=[[P, TT], [-1, S]], base=0, channel_multiplier=1,
                           allow_small_or_imprecise_dtypes=True))
            done(pool.tensor_scalar(away[:, :, :], dist[:, :, :], -1.0, None, ALU.mult))
            for t, sign in ((dist, 1), (away, -1)):
                done(pool.affine_select(out=t[:, :, :], in_=t[:, :, :], compare_op=ALU.is_ge, fill=0.0, base=0,
                                        pattern=[[sign * P, TT], [-sign, S]], channel_multiplier=sign))
            done(pool.tensor_tensor(dist[:, :, :], dist[:, :, :], away[:, :, :], ALU.add))
            for h in range(HA):
                done(pool.tensor_scalar(away[:, :, :], dist[:, :, :], -2.0 ** (-8.0 * (h + 1) / HA), None, ALU.mult))
                done(pool.tensor_tensor(c.alibi[:, h], away[:, :, :], c.mask[:, :, :], ALU.add))
            pool.sem_inc(c.bias_ready, 1)

        @block.scalar
        def _(act):
            act.dma_start(gain[:, :], d["ln_in_g"].partition_broadcast(P)).then_inc(norm_loaded, 16)
            act.dma_start(shift[:, :], d["ln_in_b"].partition_broadcast(P)).then_inc(norm_loaded, 16)
            act.dma_start(c.gates[:, TT - 1, :], d["b_gate"][0].partition_broadcast(P)).then_inc(gate_loaded, 16)
            act.dma_start(rel_wide[:, S - 1 - CLIP:S + CLIP], d["rel_bias"][0]).then_inc(bias_loaded, 16)
            for j, name in enumerate(("lambda_q1", "lambda_k1", "lambda_q2", "lambda_k2")):
                act.dma_start(c.lam_in[:, j // 2, j % 2, :], d[name][0].partition_broadcast(P)
                              ).then_inc(c.small_loaded, 16)
            act.dma_start(c.subln[:, :], d["subln_w"][0].partition_broadcast(P)).then_inc(c.small_loaded, 16)
            root_act(c, act, 0)
            for n in range(AHEAD):
                split_high(c, act, W + n, 1, n)
            turn_act(c, act, 0, c.bank)
            for n in range(AHEAD, after):
                split_high(c, act, W + n, (W + n) // RING + 1, n % RING)

        @block.vector
        def _(dve):
            dve.wait_ge(x_loaded, 16 * TT)
            dve.wait_ge(norm_loaded, 32)
            layer_norm_dve(c, dve, 0, c.x, gain[:, :], shift[:, :])
            dve.sem_inc(normed, 1)
            for n in range(AHEAD):
                split_low(c, dve, W + n, n)
            turn_dve(c, dve, 0, c.bank)
            for p in range(panels):
                for n in range(2 * p + AHEAD, min(2 * p + AHEAD + 2, after)):
                    split_low(c, dve, W + n, n % RING)
                dve.wait_ge(c.used, W + 2 * p + 2)
                banks = c.bank[p % 2 * 2:p % 2 * 2 + 2]
                if p == 6:
                    dve.wait_ge(gate_loaded, 16)
                for b in range(2):
                    if kinds[p] == "T":
                        last = dve.tensor_scalar(outs[p][:, 2 * b:2 * b + 2, :],
                                                 banks[b][:, :].rearrange("p (k s) -> p k s", k=2),
                                                 SCALE if p in (0, 3) else 1.0, None, ALU.mult)
                    elif p < 6:
                        last = dve.tensor_copy(outs[p][:, b, :], banks[b][:, :])
                    else:
                        g = slice((p - 6) * COLS, (p - 5) * COLS)
                        last = dve.tensor_tensor(c.gates[:, b, g], banks[b][:, :], c.gates[:, TT - 1, g], ALU.add)
                        if b < TT - 1:
                            linked(c, dve, last)
                last.then_inc(evacuated, 1)
            dve.sem_inc(gates_ready, 1)

        @block.tensor
        def _(pe):
            pe.wait_ge(ident_step, 2)
            pe.wait_ge(normed, 1)
            turn_pe(c, pe, 0, c.x, c.bank)
            turned_all(c, pe, 0)
            for p in range(panels):
                if p >= 2:
                    pe.wait_ge(evacuated, p - 1)
                for h in range(2):
                    n = 2 * p + h
                    (multiply_cols if kinds[p] == "T" else multiply_rows)(
                        c, pe, W + n, n % RING, h * CK, c.bank[p % 2 * 2:p % 2 * 2 + 2], h == 0, h == 1)
    c.chunk += after



FIRST_MOD = 10


def phase_attend(c):
    nc, d = c.nc, c.dram
    units = 2 * HA + HB
    diff = 2 * HA
    lam_step = c.sem("lam_step")
    lam_exp = c.sem("lam_exp")
    scored = c.sem("scored")
    biased = c.sem("biased")
    maxed = c.sem("maxed")
    exped = c.sem("exped")
    weighed = c.sem("weighed")
    flipped = c.sem("flipped")
    keyed = c.sem("keyed")
    mixed = c.sem("mixed")
    kept = c.sem("kept")
    gate_act = c.sem("gate_act")
    c.gated = gate_act
    c.mixer_turned = c.sem("mixer_turned")
    o = c.o = c.sb("o", [P, TT, D], ctx=c.mix)
    c_loaded = c.sem("c_loaded")
    silu_zero = c.sem("silu_zero")
    silu_step = c.sem("silu_step")
    sub_rv, sub_rs = c.sem("sub_rv"), c.sem("sub_rs")

    with ExitStack() as local, nc.Block() as block:
        s = c.sb("s", [P, 2, 2, S], ctx=local)
        e = s
        a = c.sb("a", [P, 2, 2, S], ctx=local)
        at = c.sb("at", [P, 2, 512], ctx=local)
        sq = e[:, :, :, :].rearrange("p a b s -> p a (b s)")
        nmax = c.sb("nmax", [P, 2, 2], ctx=local)
        total = c.sb("total", [P, 2, 2], ctx=local)
        share = c.sb("share", [P, 2], ctx=local)
        lam = c.sb("lam", [P, 4], ctx=local)
        prod = a[:, 0, 0, 0:2 * DA].rearrange("p (j n) -> p j n", j=2)
        ss = c.sb("ss", [P, TT, HA], ctx=local)
        cv = c.sb("cv", [P, KT], ctx=local)
        sig = c.sb("sig_c", [P, KT], ctx=local)
        part = ModPart(c, 0, 0, FIRST_MOD, 7, at[0:FIRST_MOD, 0, :], "mod0a_")
        W, after = part.W, part.chunks
        EXTRA = after - units

        @block.gpsimd
        def _(pool):
            pool.memset(c.silu[:, :, :], 0.0).then_inc(silu_zero, 1)

        @block.sync
        def _(sp):
            wa, wb = d["w_branch_a"][0], d["w_branch_b"][0]
            for n in range(RING, after):
                load_chunk(c, sp, W + n, n % RING, ada_source(c, 0, n), True)
            for n in range(after, after + 4):
                load_chunk(c, sp, W + n, n % RING, rows_cols((wa, wb)[n % 2], 0, (n - after) // 2 * COLS), True)
            for n in range(after + 4, after + LOADED):
                load_chunk(c, sp, W + n, n % RING, rows_cols(d["w_out"][0], n % 2 * 512, 0))
            sp.wait_ge(c.mod_stored, part.stored)

        @block.tensor
        def _(pe):
            def scores(u):
                if u >= 2:
                    pe.wait_ge(biased, u - 1)
                h, m = u % diff // 2, u % 2
                qk = c.qka if u < diff else c.qkb
                for j in range(2):
                    half = slice(j * 64, j * 64 + 64)
                    out = c.bank[2 * (u % 2) + j][:, 0:S]
                    mm = pe.matmul(out, qk[half, 0, h, m * P:m * P + P], qk[half, 1, h, :],
                                   start=True, stop=u < diff)
                    if u >= diff:
                        mm = pe.matmul(out, c.flip[:, :], c.rel[:, 2 * h + j, P - m * P:P - m * P + S],
                                       start=False, stop=True)
                mm.then_inc(scored, 1)

            def flip(u):
                pe.wait_ge(weighed, u + 1)
                if u >= 2:
                    pe.wait_ge(keyed, u - 1)
                for j in range(1 if u < diff else 2):
                    for k in range(TT):
                        t = pe.transpose(c.bank[4 + u % 2][:, (2 * j + k) * P:(2 * j + k) * P + P],
                                         a[:, u % 2, j, k * P:k * P + P], c.ident[:, :])
                t.then_inc(flipped, 1)

            def mix(u):
                pe.wait_ge(keyed, u + 1)
                if u >= 1:
                    pe.wait_ge(kept, u)
                h = u % diff // 2
                for j in range(1 if u < diff else 2):
                    for k in range(TT):
                        wt = at[:, u % 2, (2 * j + k) * P:(2 * j + k) * P + P]
                        if u < diff:
                            mm = pe.matmul(c.bank[6][:, 0:P], wt, c.va[:, k, h * P:h * P + P],
                                           start=k == 0, stop=k == 1)
                        else:
                            v0 = (2 * h + j) * 64
                            mm = pe.matmul(c.bank[6][:, j * 64:j * 64 + 64], wt, c.vb[:, k, v0:v0 + 64],
                                           start=k == 0, stop=k == 1)
                mm.then_inc(mixed, 1)

            scores(0)
            pe.wait_ge(silu_step, 2)
            for u in range(units + 2):
                if u + 1 == diff:
                    pe.wait_ge(c.rel_loaded, 16 * HB)
                if u + 1 < units:
                    scores(u + 1)
                mod_chunk(c, pe, part, u + min(u, EXTRA))
                if u >= 2:
                    mix(u - 2)
                if 1 <= u <= units:
                    flip(u - 1)
                if u < EXTRA:
                    mod_chunk(c, pe, part, 2 * u + 1)
            pe.wait_ge(c.mixer_turned, 1)
            turn_pe(c, pe, 4, o, c.bank)

        @block.scalar
        def _(act):
            with nc.allow_non_contiguous_dma(reason="1024 numbers, once"):
                act.dma_start(cv[:, :], d["c_2"][0].rearrange("(k p) -> p k", p=P)).then_inc(c_loaded, 16)
            act.wait_ge(c_loaded, 16)
            act.activation(sig[:, :], cv[:, :], ACT.Sigmoid).then_inc(silu_step, 1)
            act.wait_ge(lam_step, 2)
            act.activation(lam[:, 0:2], lam[:, 0:2], ACT.Exp).then_inc(lam_exp, 1)

            def exps(u):
                act.wait_ge(maxed, u + 1)
                for j in range(2):
                    x = act.activation(e[:, u % 2, j], s[:, u % 2, j], ACT.Exp, bias=nmax[:, u % 2, j:j + 1],
                                       accum_out=total[:, u % 2, j:j + 1])
                x.then_inc(exped, 1)

            def key(u):
                act.wait_ge(flipped, u + 1)
                if u >= 2:
                    act.wait_ge(mixed, u - 1)
                w = 256 if u < diff else 512
                act.activation(at[:, u % 2, 0:w], c.bank[4 + u % 2][:, 0:w], ACT.Copy).then_inc(keyed, 1)

            for u in range(units + 1):
                if u < units:
                    exps(u)
                if u >= 1:
                    key(u - 1)
                if u == units:
                    mod_passed(c, act, c.high_ready, part)
                    for n in range(after, after + AHEAD):
                        split_high(c, act, W + n, (W + n) // RING + 1, n % RING)
            act.wait_ge(mixed, units)
            mod_bias_load(c, act, part)
            act.wait_ge(sub_rv, 1)
            act.activation(ss[:, :, :], ss[:, :, :], ACT.Sqrt).then_inc(sub_rs, 1)
            turn_act(c, act, 4, c.bank)
            act.wait_ge(c.gates_ready, 1)
            act.activation(c.gates[:, :, :], c.gates[:, :, :], ACT.Sigmoid).then_inc(gate_act, 1)
            mod_store_act(c, act, part)

        @block.vector
        def _(dve):
            dve.wait_ge(silu_step, 1)
            dve.wait_ge(silu_zero, 1)
            dve.tensor_tensor(c.silu[:, :, PANELS - 1], sig[:, :], cv[:, :], ALU.mult).then_inc(silu_step, 1)
            dve.wait_ge(c.small_loaded, 16 * 5)
            dve.tensor_tensor(prod[:, :, :], c.lam_in[:, :, 0], c.lam_in[:, :, 1], ALU.mult).then_inc(lam_step, 1)
            dve.wait_ge(lam_step, 1)
            dve.tensor_reduce(lam[:, 0:2], prod[:, :, :], AX, ALU.add).then_inc(lam_step, 1)
            dve.wait_ge(lam_exp, 1)
            linked(c, dve, dve.tensor_tensor(lam[:, 2:3], lam[:, 1:2], lam[:, 0:1], ALU.subtract))
            linked(c, dve, dve.tensor_scalar(lam[:, 2:3], lam[:, 2:3], -LAM_INIT, None, ALU.add))
            linked(c, dve, dve.tensor_scalar(c.subln[:, :], c.subln[:, :], 1.0 - LAM_INIT, None, ALU.mult))
            dve.wait_ge(c.bias_ready, 1)

            def bias(u):
                h, m = u % diff // 2, u % 2
                dve.wait_ge(scored, u + 1)
                if u >= 2:
                    dve.wait_ge(weighed, u - 1)
                b = c.alibi[:, h, m] if u < diff else c.mask[:, m]
                dve.tensor_tensor(s[:, u % 2], c.psum[:, 2 * (u % 2):2 * (u % 2) + 2, 0:S],
                                  b.unsqueeze(1).to_broadcast([P, 2, S]), ALU.add).then_inc(biased, 1)
                dve.wait_ge(biased, u + 1)
                dve.tensor_reduce(nmax[:, u % 2, :], s[:, u % 2], AX, ALU.max, negate=True).then_inc(maxed, 1)

            def weigh(u):
                dve.wait_ge(exped, u + 1)
                if u >= 1:
                    dve.wait_ge(weighed, u)
                if u >= 2:
                    dve.wait_ge(flipped, u - 1)
                linked(c, dve, dve.reciprocal(share[:, :], total[:, u % 2]))
                if u < diff:
                    linked(c, dve, dve.tensor_tensor(share[:, 1:2], share[:, 1:2], lam[:, 2:3], ALU.mult))
                    linked(c, dve, dve.tensor_scalar(a[:, u % 2, 1], e[:, u % 2, 1], share[:, 1:2], None, ALU.mult))
                    dve.scalar_tensor_tensor(a[:, u % 2, 0], e[:, u % 2, 0], share[:, 0:1], a[:, u % 2, 1],
                                             ALU.mult, ALU.add).then_inc(weighed, 1)
                else:
                    dve.tensor_tensor(a[:, u % 2], e[:, u % 2], share[:, :].unsqueeze(2).to_broadcast([P, 2, S]),
                                      ALU.mult).then_inc(weighed, 1)

            def keep(u):
                dve.wait_ge(mixed, u + 1)
                h, m = u // 2, u % 2
                dve.tensor_copy(o[:, m, h * P:h * P + P], c.bank[6][:, 0:P]).then_inc(kept, 1)

            for u in range(units + 2):
                if u < units:
                    bias(u)
                if 1 <= u <= units:
                    weigh(u - 1)
                if u >= 2:
                    keep(u - 2)
                if u == units:
                    mod_passed(c, dve, c.low_ready, part)
                    for n in range(after, after + AHEAD):
                        split_low(c, dve, W + n, n % RING)
            oa = o[:, :, 0:512]
            dve.wait_ge(kept, units)
            linked(c, dve, dve.tensor_tensor(sq[:, :, :], oa, oa, ALU.mult))
            for m in range(TT):
                last = dve.tensor_reduce(ss[:, m], sq[:, m].rearrange("p (h n) -> p h n", h=HA), AX, ALU.add)
            linked(c, dve, last)
            linked(c, dve, dve.tensor_scalar(ss[:, :, :], ss[:, :, :], 1.0 / 128, EPS_LN, ALU.mult, ALU.add))
            dve.reciprocal(ss[:, :, :], ss[:, :, :]).then_inc(sub_rv, 1)
            dve.wait_ge(sub_rs, 1)
            for m in range(TT):
                oh = o[:, m, 0:512].rearrange("p (h n) -> p h n", h=HA)
                linked(c, dve, dve.tensor_tensor(oh, oh, ss[:, m].unsqueeze(2).to_broadcast([P, HA, 128]), ALU.mult))
                last = dve.tensor_tensor(oh, oh, c.subln[:, :].unsqueeze(1).to_broadcast([P, HA, 128]), ALU.mult)
            linked(c, dve, last)
            dve.sem_inc(c.mixer_turned, 1)
            mod_bias_dve(c, dve, part)
            turn_dve(c, dve, 4, c.bank)
    c.chunk += after


def make_routing(c):
    c.pick = c.sb("pick", [P, TT, E], ctx=c.moe)
    c.weight = c.sb("weight", [P, TT, E], ctx=c.moe)
    c.place = c.sb("place", [P, TT, PASSES, E], ctx=c.moe)
    c.spill = c.sb("spill", [1, PASSES * E + 1], I32, ctx=c.moe)
    c.counts = c.sb("counts", [P, E], ctx=c.moe)



def phase_merge(c):
    nc, d = c.nc, c.dram
    W = c.chunk
    after = 8
    rest = PANELS - FIRST_MOD
    w_out, w_e = d["w_out"][0], d["w_exp_in"][0, 0]
    ln_loaded = c.sem("ln1_loaded")
    merged = c.sem("merged")
    added = c.sem("added")
    h_ready = c.sem("h_ready")
    logits_done = c.sem("logits_done")
    logits_kept = c.sem("logits_kept")
    router_split = c.sem("router_split")
    top_ready = c.sem("top_ready")
    exp_ready = c.sem("exp_ready")
    picked = c.sem("picked")
    ranked = c.sem("ranked")
    tri_step = c.sem("tri_step")

    with ExitStack() as local, nc.Block() as block:
        mg = c.o
        gb = c.sb("gb", [P, TT, COLS], ctx=local)
        norm = c.qka[:, :, :, :].rearrange("p j h s -> p j (h s)")
        wr = c.sb("wr", [P, KT, E], ctx=local)
        wrh = c.sb("wrh", [P, KT, E], F32R, ctx=local)
        wrl = c.sb("wrl", [P, KT, E], F32R, ctx=local)
        lt = c.sb("logits_t", [E, S], ctx=local)
        br = c.sb("br", [P, E], ctx=local)
        before = c.sb("before", [P, P], ctx=local)
        ones = c.sb("ones", [P, P], ctx=local)
        number = c.sb("number", [P, E], ctx=local)
        lg = c.sb("lg", [P, TT, E], ctx=local)
        top = c.sb("top", [P, TT, 8], ctx=local)
        index = c.sb("index", [P, TT, 8], mybir.dt.uint32, ctx=local)
        indexf = c.sb("indexf", [P, TT, 8], ctx=local)
        gate = c.sb("gate", [P, TT, TOPK], ctx=local)
        gsum = c.sb("gsum", [P, TT], ctx=local)
        hit = c.sb("hit", [P, TT, TOPK, E], ctx=local)
        spillf = c.sb("spillf", [1, PASSES * E + 1], ctx=local)

        c.chunk += after
        part = ModPart(c, 0, FIRST_MOD, rest, 3, gb[0:rest, 0, :], "mod0b_")
        V = part.W + part.chunks

        @block.sync
        def _(sp):
            for n in range(LOADED, after):
                load_chunk(c, sp, W + n, n % RING, rows_cols(w_out, n % 2 * 512, (n - 4) // 2 * COLS))
            for j in range(part.chunks):
                n = part.W + j
                load_chunk(c, sp, n, n % RING, ada_source(c, 0, FIRST_MOD * PANEL + j), j >= RING)
            for j in range(LOADED):
                load_chunk(c, sp, V + j, (V + j) % RING, rows_cols(w_e, j % 2 * 512, j // 2 * COLS), j < RING)
            sp.wait_ge(c.mod_stored, part.stored)

        @block.gpsimd
        def _(pool):
            pool.memset(ones[:, :], 1.0).then_inc(tri_step, 1)
            pool.wait_ge(tri_step, 1)
            pool.affine_select(out=before[:, :], in_=ones[:, :], compare_op=ALU.is_gt, fill=0.0, base=0,
                               pattern=[[1, P]], channel_multiplier=-1).then_inc(tri_step, 1)
            pool.wait_ge(tri_step, 2)
            pool.iota(number[:, :], pattern=[[1, E]], base=0, channel_multiplier=0,
                      allow_small_or_imprecise_dtypes=True).then_inc(tri_step, 1)

        @block.scalar
        def _(act):
            for j, name in enumerate(("ln1_g", "ln1_b")):
                act.dma_start(norm[:, j, :], d[name][0].partition_broadcast(P)).then_inc(ln_loaded, 16)
            act.dma_start(wr[:, :, :], d["w_router"][0].rearrange("(k p) e -> p k e", p=P)).then_inc(ln_loaded, 16)
            act.dma_start(br[:, :], d["b_router"][0].partition_broadcast(P)).then_inc(ln_loaded, 16)
            for n in range(AHEAD, 4 + AHEAD):
                split_high(c, act, W + n, (W + n) // RING + 1, n % RING)
            turn_act(c, act, 8, c.bank[4:8])
            for n in range(4 + AHEAD, after):
                split_high(c, act, W + n, (W + n) // RING + 1, n % RING)
            mod_bias_load(c, act, part)
            act.wait_ge(ln_loaded, 64)
            act.activation(wrh[:, :, :], wr[:, :, :], ACT.Copy).then_inc(router_split, 1)
            root_act(c, act, 1)
            turn_act(c, act, 12, c.bank[4:8])
            act.wait_ge(logits_done, 1)
            act.activation(lt[:, :], c.bank[0][0:E, 0:S], ACT.Copy).then_inc(logits_kept, 1)
            act.wait_ge(top_ready, 1)
            act.activation(gate[:, :, :], gate[:, :, :], ACT.Exp).then_inc(exp_ready, 1)
            mod_passed(c, act, c.high_ready, part)
            for n in range(V, V + AHEAD):
                split_high(c, act, n, n // RING + 1, n % RING)
            mod_store_act(c, act, part)

        @block.vector
        def _(dve):
            dve.wait_ge(c.gated, 1)
            for p in range(2):
                for n in range(2 * p + AHEAD, 2 * p + AHEAD + 2):
                    split_low(c, dve, W + n, n % RING)
                dve.wait_ge(c.used, W + 2 * p + 2)
                cols = slice(p * COLS, p * COLS + COLS)
                for m in range(TT):
                    linked(c, dve, dve.tensor_tensor(mg[:, m, cols], c.bank[4 * p + m][:, :],
                                                     c.gates[:, m, cols], ALU.mult))
                    linked(c, dve, dve.tensor_tensor(gb[:, m, :], c.bank[4 * p + 2 + m][:, :],
                                                     c.gates[:, m, D + p * COLS:D + p * COLS + COLS], ALU.mult))
                    dve.tensor_tensor(mg[:, m, cols], mg[:, m, cols], gb[:, m, :], ALU.add).then_inc(merged, 1)
                    dve.wait_ge(merged, 2 * p + m + 1)
            turn_dve(c, dve, 8, c.bank[4:8])
            for p in range(2):
                for n in range(4 + 2 * p + AHEAD, min(4 + 2 * p + AHEAD + 2, after)):
                    split_low(c, dve, W + n, n % RING)
                dve.wait_ge(c.used, W + 4 + 2 * p + 2)
                cols = slice(p * COLS, p * COLS + COLS)
                for m in range(TT):
                    last = dve.scalar_tensor_tensor(c.x[:, m, cols], c.x[:, m, cols], RES, c.bank[2 * p + m][:, :],
                                                    ALU.mult, ALU.add)
            last.then_inc(added, 1)
            dve.wait_ge(added, 1)
            dve.wait_ge(router_split, 1)
            dve.tensor_tensor(wrl[:, :, :], wr[:, :, :], wrh[:, :, :].bitcast(F32), ALU.subtract
                              ).then_inc(router_split, 1)
            layer_norm_dve(c, dve, 1, c.x, norm[:, 0, :], norm[:, 1, :])
            dve.sem_inc(h_ready, 1)
            turn_dve(c, dve, 12, c.bank[4:8])
            dve.wait_ge(logits_done, 2)
            linked(c, dve, dve.tensor_tensor(lg[:, :, :], c.bank[0][:, S:S + TT * E].rearrange("p (m e) -> p m e", m=TT),
                                             br[:, :].unsqueeze(1).to_broadcast([P, TT, E]), ALU.add))
            for m in range(TT):
                last = dve.max(top[:, m, :], lg[:, m, :])
            linked(c, dve, last)
            for m in range(TT):
                last = dve.max_index(index[:, m, :], top[:, m, :], lg[:, m, :])
            linked(c, dve, last)
            linked(c, dve, dve.tensor_copy(indexf[:, :, :], index[:, :, :]))
            dve.tensor_tensor(gate[:, :, :], top[:, :, 0:TOPK], top[:, :, 0:1].to_broadcast([P, TT, TOPK]),
                              ALU.subtract).then_inc(top_ready, 1)
            dve.wait_ge(exp_ready, 1)
            linked(c, dve, dve.tensor_reduce(gsum[:, :], gate[:, :, :], AX, ALU.add))
            linked(c, dve, dve.reciprocal(gsum[:, :], gsum[:, :]))
            linked(c, dve, dve.tensor_tensor(gate[:, :, :], gate[:, :, :],
                                             gsum[:, :].unsqueeze(2).to_broadcast([P, TT, TOPK]), ALU.mult))
            dve.wait_ge(tri_step, 3)
            for m in range(TT):
                last = dve.tensor_tensor(hit[:, m], number[:, :].unsqueeze(1).to_broadcast([P, TOPK, E]),
                                         indexf[:, m, 0:TOPK].unsqueeze(2).to_broadcast([P, TOPK, E]), ALU.is_equal)
            linked(c, dve, last)
            for m in range(TT):
                last = dve.tensor_reduce(c.pick[:, m], hit[:, m].rearrange("p k e -> p e k"), AX, ALU.add)
            last.then_inc(picked, 1)
            dve.wait_ge(picked, 1)
            for m in range(TT):
                last = dve.tensor_tensor(hit[:, m], hit[:, m], gate[:, m].unsqueeze(2).to_broadcast([P, TOPK, E]),
                                         ALU.mult)
            linked(c, dve, last)
            for m in range(TT):
                last = dve.tensor_reduce(c.weight[:, m], hit[:, m].rearrange("p k e -> p e k"), AX, ALU.add)
            linked(c, dve, last)
            dve.wait_ge(ranked, 1)
            for m in range(TT):
                last = dve.scalar_tensor_tensor(c.place[:, m, 0], c.bank[1][:, m * E:m * E + E], 1.0, c.pick[:, m],
                                                ALU.add, ALU.mult)
            linked(c, dve, last)
            linked(c, dve, dve.tensor_scalar(c.place[:, :, 0], c.place[:, :, 0], -1.0, None, ALU.add))
            for b in range(1, PASSES):
                last = dve.tensor_scalar(c.place[:, :, b], c.place[:, :, 0], -float(CAP * b), None, ALU.add)
            linked(c, dve, last)
            for b in range(PASSES):
                last = dve.tensor_scalar(spillf[:, b * E:b * E + E], c.bank[2][0:1, 0:E], float(CAP * b), None,
                                         ALU.is_gt)
            linked(c, dve, last)
            linked(c, dve, dve.tensor_reduce(spillf[:, PASSES * E:PASSES * E + 1], spillf[:, E:PASSES * E],
                                             AX, ALU.max))
            linked(c, dve, dve.tensor_copy(c.spill[:, :], spillf[:, :]))
            mod_passed(c, dve, c.low_ready, part)
            mod_bias_dve(c, dve, part)
            for n in range(V, V + AHEAD):
                split_low(c, dve, n, n % RING)

        @block.tensor
        def _(pe):
            for p in range(2):
                multiply_rows(c, pe, W + 2 * p, 2 * p, 0, c.bank[4 * p:4 * p + 2], True, True)
                multiply_rows(c, pe, W + 2 * p + 1, 2 * p + 1, CK, c.bank[4 * p + 2:4 * p + 4], True, True)
            pe.wait_ge(merged, 4)
            turn_pe(c, pe, 8, mg, c.bank[4:8])
            turned_all(c, pe, 8)
            for p in range(2):
                for h in range(2):
                    n = 4 + 2 * p + h
                    multiply_rows(c, pe, W + n, n % RING, h * CK, c.bank[2 * p:2 * p + 2], h == 0, h == 1)
            pe.wait_ge(added, 1)
            for j in range(3):
                mod_chunk(c, pe, part, j)
            pe.wait_ge(h_ready, 1)
            turn_pe(c, pe, 12, c.x, c.bank[4:8])
            turned_all(c, pe, 12)
            pe.wait_ge(router_split, 2)
            for k in range(KT):
                for j, (w, x) in enumerate(((wrh, c.xth), (wrl, c.xth), (wrh, c.xtl))):
                    mm = pe.matmul(c.bank[0][0:E, 0:S], w[:, k, :], x[:, k, :],
                                   start=k == 0 and j == 0, stop=k == KT - 1 and j == 2)
            mm.then_inc(logits_done, 1)
            pe.wait_ge(logits_kept, 1)
            for m in range(TT):
                mm = pe.transpose(c.bank[0][:, S + m * E:S + m * E + E], lt[:, m * P:m * P + P], c.ident[0:E, 0:E])
            mm.then_inc(logits_done, 1)
            for j in range(3, part.chunks):
                mod_chunk(c, pe, part, j)
            pe.wait_ge(picked, 1)
            pe.wait_ge(tri_step, 3)
            pe.matmul(c.bank[1][:, 0:E], before[:, :], c.pick[:, 0], start=True, stop=True)
            pe.matmul(c.bank[1][:, E:2 * E], before[:, :], c.pick[:, 1], start=True, stop=False)
            pe.matmul(c.bank[1][:, E:2 * E], ones[:, :], c.pick[:, 0], start=False, stop=True)
            pe.matmul(c.bank[2][:, 0:E], ones[:, :], c.pick[:, 0], start=True, stop=False)
            pe.matmul(c.bank[2][:, 0:E], ones[:, :], c.pick[:, 1], start=False, stop=True).then_inc(ranked, 1)
    c.chunk = V



ITEM = 12
HID = 4
SLOTS = 2 * CAP


class Items:

    def __init__(self, c, name):
        def sem(signal):
            return c.sem(name + signal)

        self.chosen = sem("chosen")
        self.gathered = sem("gathered")
        self.rows = sem("rows")
        self.hid_kept = sem("hid_kept")
        self.folded = sem("folded")
        self.turned = sem("turned")
        self.turn_kept = sem("turn_kept")
        self.glu_ready = sem("glu_ready")
        self.sig_ready = sem("sig_ready")
        self.hidden = sem("hidden")
        self.y_high = sem("y_high")
        self.y_low = sem("y_low")
        self.step = sem("step")


FRONT, REST, NEXT_FRONT = 0, 4, 8


def second_layer(more):
    return 12 if more else 8


def chunk_number(st, seq, j):
    return seq * ITEM + (st.first + j)


def lap_of(st, seq, j):
    return seq * (ITEM // RING) + (st.first_lap + j // RING + 1)


def choose(c, dve, it, seq, item):
    for m in range(TT):
        x = dve.tensor_scalar(c.choice[:, m, :], c.slot_number[:, :], c.place_of[:, m, ds(item, 1)], None, ALU.is_equal)
    x.then_inc(it.chosen, 1)


def gather(c, pe, it, seq, g):
    pe.wait_ge(it.chosen, seq + 1)
    bank = c.bank[4 + g]
    for k in range(CK):
        kk = g * CK + k
        for j, part in enumerate((c.hh, c.hl)):
            for m in range(TT):
                mm = pe.matmul(bank[:, (2 * k + j) * CAP:(2 * k + j + 1) * CAP],
                               part[:, m, kk * P:kk * P + P], c.choice[:, m, 0:CAP],
                               start=m == 0, stop=m == TT - 1)
    mm.then_inc(it.gathered, 1)


def keep_rows(c, act, it, seq, g):
    act.wait_ge(it.gathered, seq * 2 + (g + 1))
    act.activation(c.xs[:, g * CK:g * CK + CK, :], c.bank[4 + g].rearrange("p (k s) -> p k s", k=CK), ACT.Copy
                   ).then_inc(it.rows, 1)


def combine(c, pe, it, seq):
    pe.wait_ge(it.y_high, seq * 2 + 4)
    pe.wait_ge(it.y_low, seq * 2 + 4)
    for m in range(TT):
        for h in range(2):
            for y in (c.yh, c.yl):
                mm = pe.matmul(c.bank[2 * m + h], c.back[:, m * P:m * P + P], y[:, h * COLS:h * COLS + COLS],
                               start=False, stop=False, skip_group_check=True)
    return mm


def panel(c, st, pe, seq, at, bank, lhs, ready=None):
    for h in range(2):
        if ready:
            ready(h)
        pe.wait_ge(st.low_ready, chunk_number(st, seq, at + h) + 1)
        for k in range(CK):
            for q, w in enumerate((c.wh, c.wl)):
                mm = pe.matmul(bank, lhs[:, h * CK + k, :], w[:, (at + h) % RING, k],
                               start=h == 0 and k == 0 and q == 0, stop=h == 1 and k == CK - 1 and q == 1)
        mm.then_inc(st.used, 1)


def fold(c, pe, it, seq, p):
    pe.wait_ge(it.hid_kept, seq * HID + (p + 1))
    for b in range(COLS // P):
        j = (p % 2) * 4 + b
        mm = pe.matmul(c.bank[6 + p // 2][:, j * CAP:j * CAP + CAP], c.hid[:, p, b * P:b * P + P],
                       c.stack[:, :], start=True, stop=True)
    mm.then_inc(it.folded, 1)


def front_pe(c, st, pe, it, seq, item, at):
    panel(c, st, pe, seq, at, c.bank[4], c.xs, lambda h: pe.wait_ge(it.rows, item * 2 + (h + 1)))
    panel(c, st, pe, seq, at + 2, c.bank[5], c.xs)


def rest_pe(c, st, pe, it, seq, more, combine_before):
    pe.wait_ge(it.y_low, seq * 2 + 1)
    panel(c, st, pe, seq, REST, c.bank[4], c.xs)
    if combine_before:
        combine(c, pe, it, seq - 1)
    pe.wait_ge(it.hid_kept, seq * HID + 2)
    for m in range(TT):
        pe.transpose(c.bank[5][:, m * P:m * P + P], c.choice[:, m, :].bitcast(F32), c.ident[:, :])
    for m in range(TT):
        mm = pe.matmul(c.bank[5][:, S:S + 1], c.choice[:, m, :].bitcast(F32), c.weight[:, m, ds(it.expert, 1)],
                       start=m == 0, stop=m == TT - 1)
    mm.then_inc(it.turned, 1)
    fold(c, pe, it, seq, 1)
    pe.wait_ge(it.turn_kept, seq + 1)
    panel(c, st, pe, seq, REST + 2, c.bank[5], c.xs)
    pe.wait_ge(it.hidden, seq + 1)
    fold(c, pe, it, seq, 2)
    if more:
        gather(c, pe, it, seq + 1, 0)
    fold(c, pe, it, seq, 3)
    if more:
        gather(c, pe, it, seq + 1, 1)
        front_pe(c, st, pe, it, seq, seq + 1, NEXT_FRONT)
        pe.wait_ge(it.glu_ready, seq + 1)
        fold(c, pe, it, seq + 1, 0)
    pe.wait_ge(it.hidden, seq + 2)
    for g in range(2):
        if more:
            pe.wait_ge(it.hid_kept, seq * HID + (HID + 1 + g))
        panel(c, st, pe, seq, second_layer(more) + 2 * g, c.bank[4 + g], c.acts)


def keep_hidden(c, st, act, it, seq, at, p):
    act.wait_ge(st.used, chunk_number(st, seq, at + 2))
    act.activation(c.hid[:, p, :], c.bank[4 + p % 2], ACT.Copy).then_inc(it.hid_kept, 1)


def high_at(c, st, act, seq, j):
    split_high(st, act, chunk_number(st, seq, j), lap_of(st, seq, j), j % RING)


def low_at(c, st, dve, seq, j):
    split_low(st, dve, chunk_number(st, seq, j), j % RING)


def front_act(c, st, act, it, seq):
    for p in range(2):
        high_at(c, st, act, seq, 2 * p + 2)
        high_at(c, st, act, seq, 2 * p + 3)
        keep_hidden(c, st, act, it, seq, 2 * p, p)


def front_dve(c, st, dve, seq):
    for j in range(AHEAD, AHEAD + REST):
        low_at(c, st, dve, seq, j)



def rest_act(c, st, act, it, seq, more):
    def high(*chunks):
        for j in chunks:
            if j < ITEM or more:
                high_at(c, st, act, seq, j)

    def keep_output(g):
        act.wait_ge(st.used, chunk_number(st, seq, second_layer(more) + 2 + 2 * g))
        act.activation(c.yh[:, g * COLS:g * COLS + COLS], c.bank[4 + g], ACT.Copy, scale=c.slot_weight[:, 0:1]
                       ).then_inc(it.y_high, 1)

    high(6, 7)
    keep_hidden(c, st, act, it, seq, REST, 2)
    act.wait_ge(it.turned, seq + 1)
    act.activation(c.back[:, :], c.bank[5][:, 0:S], ACT.Copy)
    act.activation(c.slot_weight[:, :], c.bank[5][:, S:S + 1], ACT.Copy).then_inc(it.turn_kept, 1)
    high(8, 9)
    keep_hidden(c, st, act, it, seq, REST + 2, 3)
    high(10)
    if more:
        keep_rows(c, act, it, seq + 1, 0)
    act.wait_ge(it.glu_ready, seq + 1)
    act.activation(c.sig[:, :, :], c.gate_half[:, :, :], ACT.Sigmoid, scale=1.702).then_inc(it.sig_ready, 1)
    high(11)
    if more:
        keep_rows(c, act, it, seq + 1, 1)
        high(12)
        keep_hidden(c, st, act, it, seq, NEXT_FRONT, 0)
        high(13, 14)
        keep_hidden(c, st, act, it, seq, NEXT_FRONT + 2, 1)
    high(15)
    keep_output(0)
    high(16, 17)
    keep_output(1)


def rest_dve(c, st, dve, it, seq, item, more):
    steps, per = 0, 6

    def low(*chunks):
        for j in chunks:
            if j < ITEM or more:
                low_at(c, st, dve, seq, j)

    def step(x):
        nonlocal steps
        steps += 1
        x.then_inc(it.step, 1)
        dve.wait_ge(it.step, seq * per + steps)

    def bias(b0):
        return c.bias_in[:, ds(it.expert * 16 + b0, 8)].unsqueeze(2).to_broadcast([P, 8, CAP])

    def output_low(g):
        dve.wait_ge(it.y_high, seq * 2 + (3 + g))
        cols = slice(g * COLS, g * COLS + COLS)
        dve.scalar_tensor_tensor(c.yl[:, cols], c.bank[4 + g], c.slot_weight[:, 0:1], c.yh[:, cols].bitcast(F32),
                                 ALU.mult, ALU.subtract).then_inc(it.y_low, 1)

    low(6, 7)
    dve.wait_ge(it.folded, seq * HID + 2)
    step(dve.tensor_tensor(c.gate_half[:, :, :], c.bank[6].rearrange("p (j s) -> p j s", j=8), bias(0), ALU.add))
    dve.tensor_scalar(c.gate_half[:, :, :], c.gate_half[:, :, :], 7.0, None, ALU.min).then_inc(it.glu_ready, 1)
    if more:
        dve.wait_ge(it.turned, seq + 1)
        choose(c, dve, it, seq + 1, item + 1)
    low(8, 9, 10)
    dve.wait_ge(it.folded, seq * HID + 4)
    step(dve.tensor_tensor(c.up_half[:, :, :], c.bank[7].rearrange("p (j s) -> p j s", j=8), bias(8), ALU.add))
    step(dve.tensor_scalar(c.up_half[:, :, :], c.up_half[:, :, :], 7.0, -7.0, ALU.min, ALU.max))
    dve.wait_ge(it.glu_ready, seq + 1)
    step(dve.scalar_tensor_tensor(c.up_half[:, :, :], c.up_half[:, :, :], 1.0, c.gate_half[:, :, :],
                                  ALU.add, ALU.mult))
    low(11)
    dve.wait_ge(it.sig_ready, seq + 1)
    step(dve.tensor_tensor(c.up_half[:, :, :], c.up_half[:, :, :], c.sig[:, :, :], ALU.mult))
    step(dve.tensor_copy(c.acts[:, :, 0:CAP], c.up_half[:, :, :]))
    dve.tensor_tensor(c.acts[:, :, CAP:SLOTS], c.up_half[:, :, :], c.acts[:, :, 0:CAP].bitcast(F32),
                      ALU.subtract).then_inc(it.hidden, 1)
    low(12, 13, 14, 15)
    output_low(0)
    low(16, 17)
    output_low(1)
    assert steps == per


def phase_experts(c):
    nc, d = c.nc, c.dram
    W = c.chunk
    w1, w2 = d["w_exp_in"][0], d["w_exp_out"][0]
    it, c.spill_items = Items(c, "item_"), Items(c, "spill_")
    moe_loaded = c.sem("moe_loaded")
    moe_step = c.sem("moe_step")
    set_up = c.sem("set_up")
    bias_turned = c.sem("bias_turned")
    bias_kept = c.sem("bias_kept")
    split_ready = c.sem("split_ready")
    c.first, c.first_lap = W, W // RING

    c.hh = c.sb("hh", [P, TT, D], F32R, ctx=c.exp)
    c.hl = c.sb("hl", [P, TT, D], F32R, ctx=c.exp)
    c.xs = c.sb("xs", [P, KT, SLOTS], F32R, ctx=c.exp)
    c.acts = c.sb("acts", [P, KT, SLOTS], F32R, ctx=c.exp)
    c.hid = c.sb("hid", [P, HID, COLS], ctx=c.exp)
    c.yh = c.sb("yh", [P, D], F32R, ctx=c.exp)
    c.yl = c.sb("yl", [P, D], F32R, ctx=c.exp)
    c.choice = c.sb("choice", [P, TT, SLOTS], F32R, ctx=c.exp)
    c.back = c.sb("back", [P, S], F32R, ctx=c.exp)
    c.slot_number = c.sb("slot_number", [P, SLOTS], ctx=c.exp)
    c.slot_weight = c.sb("slot_weight", [P, 1], ctx=c.exp)
    c.stack = c.sb("stack", [P, CAP], ctx=c.exp)
    c.gate_half = c.sb("gate_half", [P, 8, CAP], ctx=c.exp)
    c.up_half = c.sb("up_half", [P, 8, CAP], ctx=c.exp)
    c.sig = c.sb("sig", [P, 8, CAP], ctx=c.exp)
    c.bias_in = c.sb("bias_in", [P, E * 16], ctx=c.exp)
    c.place_of = c.place[:, :, :, :].rearrange("p m b e -> p m (b e)")

    with ExitStack() as local, nc.Block() as block:
        bias_rows = c.sb("bias_rows", [P, 4, P], ctx=local)
        bias_out = c.sb("bias_out", [E, D], ctx=local)
        weight_t = c.sb("weight_t", [E, S], ctx=local)

        def expert_chunk(e, j):
            if j < 2 * HID:
                return rows_cols(w1[e], j % 2 * 512, j // 2 * COLS)
            return rows_cols(w2[e], j % 2 * 512, (j // 2 - HID) * COLS)

        def by_register(w, e, j):
            m = w[ds(e, 1)].rearrange("a r c -> (a r) c")
            return rows_cols(m, j % 2 * 512, (j // 2 % HID) * COLS)

        @block.sync
        def _(sp):
            def load(seq, j, e, own):
                w = w1 if own < 2 * HID else w2
                load_chunk(c, sp, chunk_number(c, seq, j), j % RING, by_register(w, e, own))

            with sp.Fori(0, E - 1) as i:
                for j, e, own in ((6, i, 6), (7, i, 7), (8, i + 1, 0), (9, i + 1, 1), (10, i + 1, 2),
                                  (11, i + 1, 3), (12, i, 8), (13, i, 9), (14, i, 10), (15, i, 11),
                                  (16, i + 1, 4), (17, i + 1, 5)):
                    load(i, j, e, own)
            for j in range(LOADED, ITEM):
                load_chunk(c, sp, chunk_number(c, E - 1, j), j % RING, expert_chunk(E - 1, j))

        @block.gpsimd
        def _(pool):
            pool.memset(c.stack[:, :], 0.0).then_inc(moe_step, 1)
            pool.iota(c.slot_number[:, :], pattern=[[0, 2], [1, CAP]], base=0, channel_multiplier=0,
                      allow_small_or_imprecise_dtypes=True).then_inc(moe_step, 1)
            pool.wait_ge(moe_step, 2)
            for j in range(2):
                pool.affine_select(out=c.stack[:, :], in_=c.stack[:, :], compare_op=ALU.not_equal, fill=1.0,
                                   base=-j * CAP, pattern=[[-1, CAP]], channel_multiplier=1).then_inc(moe_step, 1)
                pool.wait_ge(moe_step, 3 + j)
            for t in (c.yh, c.yl, c.back):
                pool.memset(t[:, :].bitcast(F32), 0.0).then_inc(moe_step, 1)
            pool.wait_ge(moe_step, 7)
            pool.sem_inc(set_up, 1)

        @block.scalar
        def _(act):
            act.dma_start(bias_rows[:, :, :], d["b_exp_in"][0].rearrange("e (j f) -> (e j) f", f=P)
                          .rearrange("(a p) f -> p a f", p=P)).then_inc(moe_loaded, 16)
            act.dma_start(bias_out[:, :], d["b_exp_out"][0]).then_inc(moe_loaded, 16)
            for m in range(TT):
                act.activation(c.hh[:, m], c.x[:, m], ACT.Copy).then_inc(split_ready, 1)
            act.wait_ge(bias_turned, 1)
            act.activation(weight_t[:, :], c.bank[5][0:E, 0:S], ACT.Copy).then_inc(bias_kept, 1)
            act.activation(c.bias_in[:, :], c.bank[4], ACT.Copy).then_inc(bias_kept, 1)
            act.sem_inc(it.y_high, 2)
            for g in range(2):
                keep_rows(c, act, it, 0, g)
            front_act(c, c, act, it, 0)
            with act.Fori(0, E - 1) as i:
                rest_act(c, c, act, it, i, True)
            rest_act(c, c, act, it, E - 1, False)

        @block.vector
        def _(dve):
            for m in range(TT):
                dve.wait_ge(split_ready, m + 1)
                x = dve.tensor_tensor(c.hl[:, m], c.x[:, m], c.hh[:, m].bitcast(F32), ALU.subtract)
            x.then_inc(split_ready, 1)
            dve.wait_ge(set_up, 1)
            choose(c, dve, it, 0, 0)
            dve.wait_ge(bias_kept, 2)
            dve.sem_inc(it.hidden, 1)
            dve.sem_inc(it.y_low, 2)
            front_dve(c, c, dve, 0)
            with dve.Fori(0, E - 1) as i:
                it.expert = i
                rest_dve(c, c, dve, it, i, i, True)
            it.expert = E - 1
            rest_dve(c, c, dve, it, E - 1, E - 1, False)

        @block.tensor
        def _(pe):
            pe.wait_ge(moe_loaded, 32)
            for a in range(4):
                pe.transpose(c.bank[4][:, a * P:a * P + P], bias_rows[:, a, :], c.ident[:, :])
            for m in range(TT):
                t = pe.transpose(c.bank[5][0:E, m * P:m * P + P], c.weight[:, m, :], c.ident[:, :])
            t.then_inc(bias_turned, 1)
            pe.wait_ge(bias_kept, 2)
            for m in range(TT):
                for h in range(2):
                    pe.matmul(c.bank[2 * m + h], weight_t[:, m * P:m * P + P], bias_out[:, h * COLS:h * COLS + COLS],
                              start=True, stop=False, skip_group_check=True)
            pe.wait_ge(split_ready, 3)
            for g in range(2):
                gather(c, pe, it, 0, g)
            front_pe(c, c, pe, it, 0, 0, FRONT)
            fold(c, pe, it, 0, 0)
            with pe.Fori(0, E - 1) as i:
                it.expert = i
                rest_pe(c, c, pe, it, i, True, True)
            it.expert = E - 1
            rest_pe(c, c, pe, it, E - 1, False, True)
            combine(c, pe, it, E - 1)
    c.chunk += ITEM * E



def phase_spill(c):
    nc, d = c.nc, c.dram
    w1, w2 = d["w_exp_in"][0], d["w_exp_out"][0]
    st = Stream(c, "spill_", RING, 0)
    it = c.spill_items

    def items(eng, name, body):
        any_spill = eng.value_load(c.spill[0:1, PASSES * E:PASSES * E + 1], min_val=0, max_val=1)
        count = eng.alloc_register("spill_seq_" + name)
        eng.reg_mov(count, 0)
        with eng.If(any_spill):
            with eng.Fori(1, PASSES) as b:
                with eng.Fori(0, E) as e:
                    flag = eng.value_load(c.spill[0:1, ds(b * E + e, 1)], min_val=0, max_val=1)
                    with eng.If(flag):
                        seq = eng.snap(count, min_val=0, max_val=S * TOPK // CAP - 1)
                        body(seq, b * E + e, e)
                        eng.reg_add(count, count, 1)
                    eng.nop()
            eng.nop()

    with nc.Block() as block:
        @block.sync
        def _(sp):
            def body(seq, item, e):
                for j in range(ITEM):
                    m = (w1 if j < 2 * HID else w2)[ds(e, 1)].rearrange("a r c -> (a r) c")
                    load_chunk(st, sp, chunk_number(st, seq, j), j % RING,
                               rows_cols(m, j % 2 * 512, (j // 2 % HID) * COLS))
            items(sp, "sp", body)

        @block.scalar
        def _(act):
            act.sem_inc(it.y_high, 2)
            act.sem_inc(st.high_ready, RING)

            def body(seq, item, e):
                for j in range(AHEAD):
                    split_high(st, act, chunk_number(st, seq, j), lap_of(st, seq, j), j)
                for g in range(2):
                    keep_rows(c, act, it, seq, g)
                front_act(c, st, act, it, seq)
                rest_act(c, st, act, it, seq, False)
            items(act, "act", body)

        @block.vector
        def _(dve):
            dve.sem_inc(it.y_low, 2)
            dve.sem_inc(it.hidden, 1)
            dve.sem_inc(st.low_ready, RING)

            def body(seq, item, e):
                it.expert = e
                choose(c, dve, it, seq, item)
                for j in range(AHEAD):
                    split_low(st, dve, chunk_number(st, seq, j), j)
                front_dve(c, st, dve, seq)
                rest_dve(c, st, dve, it, seq, item, False)
            items(dve, "dve", body)

        @block.tensor
        def _(pe):
            pe.sem_inc(st.used, RING)

            def body(seq, item, e):
                it.expert = e
                for g in range(2):
                    gather(c, pe, it, seq, g)
                front_pe(c, st, pe, it, seq, seq, FRONT)
                fold(c, pe, it, seq, 0)
                rest_pe(c, st, pe, it, seq, False, False)
                combine(c, pe, it, seq)
            items(pe, "pe", body)



D2 = D // 2
CONV = 3
HG = 4
CH = S // CHUNK


def high(c, act, n):
    split_high(c, act, n, n // RING + 1, n % RING)


def rms_act(c, act, v, junk):
    act.wait_ge(c.x_ready, v)
    for m in range(TT):
        a = act.activation(junk[:, m], c.x[:, m], ACT.Square, accum_out=c.ss[:, m:m + 1])
    a.then_inc(c.squared, 1)
    root_act(c, act, v)


def rms_dve(c, dve, v, h, j):
    shift, scale = c.mod[:, 3 * j], c.mod[:, 3 * j + 1]
    linked(c, dve, dve.scalar_tensor_tensor(scale, scale, 1.0, c.norm[:, j, :], ALU.add, ALU.mult))
    dve.wait_ge(c.squared, v - FIRST_RMS + 1)
    linked(c, dve, dve.tensor_scalar(c.ss[:, :], c.ss[:, :], 1.0 / D, EPS_RMS, ALU.mult, ALU.add))
    dve.reciprocal(c.rv[:, :], c.ss[:, :]).then_inc(c.rv_ready, 1)
    dve.wait_ge(c.rs_ready, v + 1)
    for m in range(TT):
        last = dve.scalar_tensor_tensor(h[:, m], c.x[:, m], c.rs[:, m:m + 1], scale, ALU.mult, ALU.mult)
    linked(c, dve, last)
    for m in range(TT):
        last = dve.tensor_tensor(h[:, m], h[:, m], shift, ALU.add)
    last.then_inc(c.h_ready, 1)


FIRST_RMS = 3


def make_second(c):
    c.mod = c.sb("mod", [P, 6, D], ctx=c.two)
    c.norm = c.sb("norm", [P, 2, D], ctx=c.two)
    c.ss = c.sb("ss2", [P, TT], ctx=c.two)
    c.x_ready = c.sem("x_ready")
    c.masks_ready = c.sem("masks_ready")
    c.squared = c.sem("squared")
    c.h_ready = c.sem("h2_ready")
    c.norm_loaded = c.sem("norm_loaded2")


def norm_load(c, act, layer, j):
    act.dma_start(c.norm[:, j, :], c.dram[("norm_mix_2", "norm_mlp_2")[j]][layer].partition_broadcast(P)
                  ).then_inc(c.norm_loaded, 16)



def phase_second(c):
    nc, d = c.nc, c.dram
    W = c.second
    ln_loaded = c.sem("ln2_loaded")

    with ExitStack() as local, nc.Block() as block:
        ln = c.sb("ln2", [P, 2, D], ctx=local)

        @block.sync
        def _(sp):
            sp.wait_ge(ln_loaded, 32)
            for n in range(W, W + LOADED):
                load_chunk(c, sp, n, n % RING, static_source(c, n))

        @block.scalar
        def _(act):
            for j, name in enumerate(("ln2_g", "ln2_b")):
                act.dma_start(ln[:, j, :], d[name][0].partition_broadcast(P)).then_inc(ln_loaded, 16)
            norm_load(c, act, 0, 0)
            norm_load(c, act, 0, 1)
            act.wait_ge(c.mod_stored, 32)
            mod_load(c, act, 0, range(6))
            root_act(c, act, 2)
            for j in range(AHEAD):
                high(c, act, W + j)

        @block.vector
        def _(dve):
            for m in range(TT):
                last = dve.scalar_tensor_tensor(c.x[:, m].rearrange("p (h n) -> p h n", h=2),
                                                c.x[:, m].rearrange("p (h n) -> p h n", h=2), RES,
                                                c.psum[:, 2 * m:2 * m + 2, :], ALU.mult, ALU.add)
            linked(c, dve, last)
            dve.wait_ge(ln_loaded, 32)
            layer_norm_dve(c, dve, 2, c.x, ln[:, 0, :], ln[:, 1, :])
            dve.sem_inc(c.x_ready, FIRST_RMS)
            for j in range(AHEAD):
                split_low(c, dve, W + j, (W + j) % RING)



SCAN_MOD = 4
STICK_MOD = PANELS - SCAN_MOD
SECOND = (("w_in_ab_2", 14), ("mod1a", PANEL * SCAN_MOD), ("w_out_ab_2", 4), ("mlp0", 32),
          ("w_qkv_2", 12), ("mod1b", PANEL * STICK_MOD), ("w_out_c_2", 4), ("mlp1", 32))


def static_source(c, n):
    k = n - c.second
    for name, count in SECOND:
        if k < count:
            if name == "mod1a":
                return ada_source(c, 1, k)
            if name == "mod1b":
                return ada_source(c, 1, SCAN_MOD * PANEL + k)
            if name in ("mlp0", "mlp1"):
                return mlp_source(c, int(name[3]), k // 8, k % 8)
            return rows_cols(c.dram[name][0], k % 2 * 512, k // 2 * COLS)
        k -= count


def taken_whole(c, n):
    k = n - c.second
    for name, count in SECOND:
        if k < count:
            return k >= 0 and name == "mod1a"
        k -= count


def mlp_source(c, layer, quarter, j):
    if j < 4:
        return rows_cols(c.dram["mlp_w1_2"][layer], j % 2 * 512, quarter * 1024 + j // 2 * COLS)
    j -= 4
    return rows_cols(c.dram["mlp_w2_2"][layer], quarter * 1024 + j // 2 * 512, j % 2 * COLS)


def load_static(c, sp, first, end):
    for n in range(c.chunk + first, c.chunk + end):
        load_chunk(c, sp, n, n % RING, static_source(c, n), taken_whole(c, n - RING))


def low(c, dve, n):
    split_low(c, dve, n, n % RING)


def phase_project_ab(c):
    nc, d = c.nc, c.dram
    W = c.chunk
    panels = 7
    kinds = "TTTTTNN"
    evacuated = c.sem("ab_evacuated")
    conv_loaded = c.sem("conv_loaded")
    mask_step = c.sem("mask_step")
    sigmoid_ready = c.sem("hg_sigmoid")
    cm = c.hgrn
    c.h = c.sb("h", [P, TT, D], ctx=cm)
    c.ab = c.sb("ab", [P, 4, S], ctx=cm)
    c.ac = c.sb("ac", [P, 4, S], ctx=cm)
    c.ya = c.sb("ya", [P, 4, S], ctx=cm)
    c.q = c.sb("q", [P, HG, S], ctx=cm)
    c.f = c.sb("f", [P, HG, S], ctx=cm)
    c.v = c.sb("v", [P, TT, D2], ctx=cm)
    c.hg = c.sb("hg", [P, TT, D2], ctx=cm)
    c.level_mask = c.sb("level_mask", [P, 7, P], ctx=cm)
    c.conv = c.sb("conv", [P, CONV, 4], ctx=cm)
    c.lb_in = c.sb("lb_in", [P, 3, HG], ctx=cm)
    outs = [c.ab, None, None, c.q, c.f, c.v, c.hg]

    with nc.Block() as block:
        @block.sync
        def _(sp):
            load_static(c, sp, LOADED, 2 * panels + RING)

        @block.gpsimd
        def _(pool):
            steps = 0

            def done(x):
                nonlocal steps
                steps += 1
                x.then_inc(mask_step, 1)
                pool.wait_ge(mask_step, steps)

            done(pool.memset(c.level_mask[:, :, :], 0.0))
            for j in range(7):
                w = 2 ** j
                second = c.level_mask[:, j].rearrange("p (b h w) -> p b h w", h=2, w=w)[:, :, 1, :]
                done(pool.memset(second, 1.0))
                done(pool.affine_select(out=second, in_=second, compare_op=ALU.is_ge, fill=0.0, base=0,
                                        pattern=[[-2 * w, P // (2 * w)], [0, w]], channel_multiplier=1))
                done(pool.affine_select(out=second, in_=second, compare_op=ALU.is_ge, fill=0.0, base=w - 1,
                                        pattern=[[2 * w, P // (2 * w)], [0, w]], channel_multiplier=-1))
            pool.sem_inc(c.masks_ready, 1)

        @block.scalar
        def _(act):
            with nc.allow_non_contiguous_dma(reason="3072 numbers, once"):
                act.dma_start(c.conv[:, :, :], d["conv_w_2"][0].rearrange("w (k p) -> p w k", p=P)
                              ).then_inc(conv_loaded, 16)
                act.dma_start(c.lb_in[:, :, :], d["lb_logits_2"].rearrange("r (k p) -> p r k", p=P)
                              ).then_inc(conv_loaded, 16)
            rms_act(c, act, FIRST_RMS, c.h)
            turn_act(c, act, 16, c.bank[4:8])
            for n in range(AHEAD, 2 * panels):
                high(c, act, W + n)
            act.wait_ge(c.used, W + 2 * panels)
            act.activation(c.hg[:, :, :], c.psum[:, 0:2, :], ACT.Sigmoid).then_inc(sigmoid_ready, 1)

        @block.vector
        def _(dve):
            dve.wait_ge(c.norm_loaded, 32)
            dve.wait_ge(c.mod_loaded, 6 * 16)
            rms_dve(c, dve, FIRST_RMS, c.h, 0)
            turn_dve(c, dve, 16, c.bank[4:8])
            for p in range(panels):
                for n in range(2 * p + 2, min(2 * p + 4, 2 * panels)):
                    low(c, dve, W + n)
                dve.wait_ge(c.used, W + 2 * p + 2)
                if p == 2:
                    dve.wait_ge(evacuated, 2)
                if p == 6:
                    dve.wait_ge(sigmoid_ready, 1)
                for b in range(2):
                    bank = c.bank[p % 2 * 2 + b]
                    wide = bank.rearrange("p (k s) -> p k s", k=2)
                    tiles = slice(2 * b, 2 * b + 2)
                    if p == 1:
                        last = dve.tensor_copy(c.ac[:, tiles, :], wide)
                    elif p == 2:
                        last = dve.tensor_tensor(c.ac[:, tiles, :], wide, c.ac[:, tiles, :], ALU.mult)
                    elif kinds[p] == "T":
                        last = dve.tensor_copy(outs[p][:, tiles, :], wide)
                    elif p == 5:
                        last = dve.tensor_copy(outs[p][:, b, :], bank)
                    else:
                        last = dve.tensor_tensor(outs[p][:, b, :], bank, outs[p][:, b, :], ALU.mult)
                last.then_inc(evacuated, 1)
                if p == 2:
                    dve.wait_ge(conv_loaded, 32)
                    dve.wait_ge(evacuated, 3)
                    for k in range(4):
                        last = dve.tensor_scalar(c.ya[:, k, :], c.ac[:, k, :], c.conv[:, 2, k:k + 1], None, ALU.mult)
                    linked(c, dve, last)
                    for back in (1, 2):
                        for k in range(4):
                            last = dve.scalar_tensor_tensor(c.ya[:, k, back:S], c.ac[:, k, 0:S - back],
                                                            c.conv[:, 2 - back, k:k + 1], c.ya[:, k, back:S],
                                                            ALU.mult, ALU.add)
                        linked(c, dve, last)
                    linked(c, dve, dve.tensor_tensor(c.ya[:, :, :], c.ya[:, :, :], c.ab[:, :, :], ALU.mult))

        @block.tensor
        def _(pe):
            pe.wait_ge(c.h_ready, 1)
            turn_pe(c, pe, 16, c.h, c.bank[4:8])
            turned_all(c, pe, 16)
            for p in range(panels):
                if p >= 2:
                    pe.wait_ge(evacuated, p - 1)
                for h in range(2):
                    n = W + 2 * p + h
                    (multiply_cols if kinds[p] == "T" else multiply_rows)(
                        c, pe, n, n % RING, h * CK, c.bank[p % 2 * 2:p % 2 * 2 + 2], h == 0, h == 1)
    c.chunk += 2 * panels



def phase_recur(c):
    nc, d = c.nc, c.dram
    W = c.chunk + PANEL * SCAN_MOD
    widths = [0, 1, 2, 4, 8, 16, 32, 64, 128]
    levels = len(widths)
    HEAD = 3
    lb_step, lb_exp = c.sem("lb_step"), c.sem("lb_exp")
    forget = c.sem("forget")
    spans = c.sem("spans")
    decays = c.sem("decays")
    scaled = c.sem("scaled")
    paired = c.sem("paired")
    masked = c.sem("masked")
    summed = c.sem("summed")
    zeroed = c.sem("zeroed")
    hg_loaded = c.sem("hg_loaded")
    out_step = c.sem("out_step")
    gated = c.sem("hg_gated")
    yb_ready = c.sem("yb_ready")
    ya_split = c.sem("ya_split")
    added = c.sem("ab_added")

    with ExitStack() as local, nc.Block() as block:
        dd = [c.mod[:, 0, :], c.mod[:, 1, :]]
        qq = [c.ab, c.ac]
        kk0 = c.sb("kk0", [P, HG, S], ctx=local)
        kk1 = c.sb("kk1", [P, HG, S], ctx=local)
        kk = [kk0, kk1]
        sm = [c.h[:, 0, :], c.h[:, 1, :]]
        mod_rows = c.sb("mod1a_rows", [SCAN_MOD, COLS], ctx=local)
        part = ModPart(c, 1, 0, SCAN_MOD, 7, mod_rows[:, :], "mod1a_")
        key = c.norm[:, 0, :].rearrange("p (h s) -> p h s", h=HG)
        b = c.f
        lb = c.sb("lb", [P, 3, HG], ctx=local)
        lb2 = c.sb("lb2", [P, 3, HG], ctx=local)
        rest = c.mod[:, 0, :]
        tail = c.sb("tail", [P, HG], ctx=local)
        hnorm = c.sb("hnorm", [P, D2], ctx=local)
        sq = c.sb("hsq", [P, TT, HG], ctx=local)

        def halves(t, w):
            flat = t.rearrange("p h s -> p (h s)") if len(t.shape) == 3 else t
            return flat.rearrange("p (b h w) -> p b h w", h=2, w=w)

        def chunks(t):
            flat = t.rearrange("p h s -> p (h s)") if len(t.shape) == 3 else t
            return flat.rearrange("p (h c s) -> p h c s", h=HG, c=CH)

        @block.sync
        def _(sp):
            load_static(c, sp, RING, part.chunks + 4 + LOADED)
            sp.wait_ge(c.mod_stored, part.stored)

        @block.gpsimd
        def _(pool):
            pool.memset(rest, 1.0).then_inc(zeroed, 1)
            pool.wait_ge(zeroed, 1)
            pool.memset(rest.rearrange("p (c s) -> p c s", s=CHUNK)[:, :, 0:1], 0.0).then_inc(zeroed, 1)
            for t in (qq[0], qq[1], kk0, kk1):
                pool.memset(t[:, :, :], 0.0).then_inc(zeroed, 1)
            pool.wait_ge(hg_loaded, 16)
            pool.tensor_tensor(c.hg[:, :, :], c.hg[:, :, :], hnorm[:, :].unsqueeze(1).to_broadcast([P, TT, D2]),
                               ALU.mult).then_inc(gated, 1)

        @block.scalar
        def _(act):
            mod_bias_load(c, act, part)
            act.dma_start(hnorm[:, :], d["hg_norm_2"][0].partition_broadcast(P)).then_inc(hg_loaded, 16)
            act.activation(c.f[:, :, :], c.f[:, :, :], ACT.Sigmoid).then_inc(forget, 1)
            act.wait_ge(lb_step, 1)
            act.activation(lb[:, :, :], lb[:, :, :], ACT.Exp).then_inc(lb_exp, 1)
            act.wait_ge(forget, 3)
            act.activation(c.f[:, :, :], c.f[:, :, :], ACT.Ln).then_inc(forget, 1)
            for l in range(1, levels):
                act.wait_ge(spans, l)
                x = dd[l % 2]
                act.activation(x, x, ACT.Exp).then_inc(decays, 1)
            mod_passed(c, act, c.high_ready, part)
            for n in range(AHEAD):
                high(c, act, W + n)
            act.wait_ge(summed, levels)
            act.activation(kk0[:, :, :].rearrange("p h s -> p (h s)").rearrange("p (m n) -> p m n", m=TT),
                           c.psum[:, 4:6, :], ACT.Square).then_inc(out_step, 1)
            act.wait_ge(out_step, 3)
            act.activation(sq[:, :, :], sq[:, :, :], ACT.Sqrt).then_inc(out_step, 1)
            act.activation(c.xth[:, 0:4, :], c.ya[:, :, :], ACT.Copy).then_inc(ya_split, 1)
            turn_act(c, act, 20, c.bank[0:2], 4, 4)
            mod_store_act(c, act, part)
            for n in range(AHEAD, 4 + AHEAD):
                high(c, act, W + n)

        @block.vector
        def _(dve):
            linked(c, dve, dve.tensor_tensor(tail[:, :], c.lb_in[:, 0], c.lb_in[:, 1], ALU.max))
            linked(c, dve, dve.tensor_tensor(tail[:, :], tail[:, :], c.lb_in[:, 2], ALU.max))
            dve.tensor_tensor(lb[:, :, :], c.lb_in[:, :, :], tail[:, :].unsqueeze(1).to_broadcast([P, 3, HG]),
                              ALU.subtract).then_inc(lb_step, 1)
            dve.wait_ge(lb_exp, 1)
            linked(c, dve, dve.tensor_reduce(tail[:, :], lb[:, :, :].rearrange("p r h -> p h r"), AX, ALU.add))
            linked(c, dve, dve.reciprocal(tail[:, :], tail[:, :]))
            linked(c, dve, dve.tensor_tensor(lb2[:, 0], lb[:, 0], tail[:, :], ALU.mult))
            linked(c, dve, dve.tensor_scalar(lb2[:, 1], lb2[:, 0], -1.0, 1.0, ALU.mult, ALU.add))
            dve.wait_ge(forget, 1)
            for h in range(HG):
                x = dve.tensor_scalar(c.f[:, h], c.f[:, h], lb2[:, 1, h:h + 1], lb2[:, 0, h:h + 1], ALU.mult, ALU.add)
            x.then_inc(forget, 1)
            dve.wait_ge(forget, 2)
            dve.tensor_scalar(key, c.f[:, :, :], -1.0, 1.0, ALU.mult, ALU.add).then_inc(forget, 1)
            dve.wait_ge(zeroed, 6)
            dve.wait_ge(forget, 4)
            fb = b[:, :, :].rearrange("p h s -> p (h s)")
            linked(c, dve, dve.tensor_tensor_scan(fb, rest, fb, 0.0, ALU.mult, ALU.add))

            def span(l):
                w = widths[l]
                x = dd[l % 2]
                if l >= 3:
                    dve.wait_ge(scaled, l - 2)
                if w <= CHUNK:
                    v, o = halves(b[:, :, :], w), halves(x, w)
                    ref = v[:, :, 0, w - 1:w].to_broadcast([P, HG * S // (2 * w), w])
                    if w < CHUNK:
                        dve.tensor_tensor(o[:, :, 1], v[:, :, 1], ref, ALU.subtract)
                    else:
                        dve.tensor_copy(o[:, :, 1], v[:, :, 1])
                    dve.tensor_tensor(o[:, :, 0], ref, v[:, :, 0], ALU.subtract).then_inc(spans, 1)
                else:
                    v, o = chunks(b[:, :, :]), chunks(x)

                    def last_of(ch):
                        return v[:, :, ch, CHUNK - 1:CHUNK].to_broadcast([P, HG, CHUNK])

                    linked(c, dve, dve.tensor_tensor(tail[:, :], v[:, :, 0, CHUNK - 1], v[:, :, 1, CHUNK - 1], ALU.add))
                    dve.tensor_tensor(o[:, :, 0], tail[:, :].unsqueeze(2).to_broadcast([P, HG, CHUNK]), v[:, :, 0],
                                      ALU.subtract)
                    dve.tensor_tensor(o[:, :, 1], last_of(1), v[:, :, 1], ALU.subtract)
                    dve.tensor_copy(o[:, :, 2], v[:, :, 2])
                    dve.tensor_tensor(o[:, :, 3], last_of(2), v[:, :, 3], ALU.add).then_inc(spans, 1)

            def scale(l):
                w = widths[l]
                dve.wait_ge(decays, l)
                if l >= 3:
                    dve.wait_ge(paired, l - 1)
                dve.tensor_tensor(halves(qq[l % 2][:, :, :], w)[:, :, 1], halves(c.q[:, :, :], w)[:, :, 1],
                                  halves(dd[l % 2], w)[:, :, 1], ALU.mult)
                dve.tensor_tensor(halves(kk[l % 2][:, :, :], w)[:, :, 0], halves(key, w)[:, :, 0],
                                  halves(dd[l % 2], w)[:, :, 0], ALU.mult).then_inc(scaled, 1)

            def mask(l):
                dve.wait_ge(paired, l + 1)
                if l >= 2:
                    dve.wait_ge(summed, l - 1)
                if l == levels - 1:
                    dve.tensor_copy(sm[l % 2][:, 0:512], c.bank[2 * (l % 2)]).then_inc(masked, 1)
                    return
                m = c.ident[:, :] if l == 0 else c.level_mask[:, l - 1]
                dve.tensor_tensor(sm[l % 2].rearrange("p (n t) -> p n t", n=8),
                                  c.psum[:, 2 * (l % 2):2 * (l % 2) + 2, :].rearrange("p b (n t) -> p (b n) t", t=P),
                                  m.unsqueeze(1).to_broadcast([P, 8, P]), ALU.mult).then_inc(masked, 1)

            dve.wait_ge(c.masks_ready, 1)
            for s in range(1, levels + 2):
                if s < levels:
                    span(s)
                if 2 <= s <= levels:
                    scale(s - 1)
                if s <= levels:
                    mask(s - 1) if s == 1 else None
                if s >= 3:
                    mask(s - 2)
            mod_passed(c, dve, c.low_ready, part)
            mod_bias_dve(c, dve, part)
            for n in range(AHEAD):
                low(c, dve, W + n)
            dve.wait_ge(out_step, 1)
            squares = kk0[:, :, :].rearrange("p h s -> p (h s)").rearrange("p (m h n) -> p (m h) n", m=TT, h=HG)
            linked(c, dve, dve.tensor_reduce(sq[:, :, :].rearrange("p m h -> p (m h)"), squares, AX, ALU.add))
            dve.tensor_scalar(sq[:, :, :], sq[:, :, :], 1.0 / P, EPS_RMS, ALU.mult, ALU.add).then_inc(out_step, 1)
            dve.wait_ge(out_step, 2)
            dve.reciprocal(sq[:, :, :], sq[:, :, :]).then_inc(out_step, 1)
            dve.wait_ge(out_step, 4)
            for m in range(TT):
                last = dve.tensor_tensor(c.v[:, m].rearrange("p (h n) -> p h n", h=HG),
                                         c.bank[4 + m].rearrange("p (h n) -> p h n", h=HG),
                                         sq[:, m].unsqueeze(2).to_broadcast([P, HG, P]), ALU.mult)
            linked(c, dve, last)
            dve.wait_ge(gated, 1)
            dve.tensor_tensor(c.v[:, :, :], c.v[:, :, :], c.hg[:, :, :], ALU.mult).then_inc(yb_ready, 1)
            dve.wait_ge(ya_split, 1)
            dve.tensor_tensor(c.xtl[:, 0:4, :], c.ya[:, :, :], c.xth[:, 0:4, :].bitcast(F32), ALU.subtract
                              ).then_inc(ya_split, 1)
            turn_dve(c, dve, 20, c.bank[0:2], 4, 4)
            for p in range(2):
                low(c, dve, W + 2 * p + 2)
                low(c, dve, W + 2 * p + 3)
                add_gated(c, dve, W + 2 * p + 2, c.bank[2 * p + 2:2 * p + 4], p, c.mod[:, 2])
            dve.sem_inc(c.x_ready, 1)

        @block.tensor
        def _(pe):
            def pairs(l):
                q, k = (c.q, key) if l == 0 else (qq[l % 2], kk[l % 2])
                if l == 0:
                    pe.wait_ge(forget, 3)
                else:
                    pe.wait_ge(scaled, l)
                if l >= 2:
                    pe.wait_ge(masked, l - 1)
                for m in range(TT if l < levels - 1 else 1):
                    for h in range(HG):
                        m2 = m if l < levels - 1 else 1
                        mm = pe.matmul(c.bank[2 * (l % 2) + m][:, h * P:h * P + P], k[:, h, m * P:m * P + P],
                                       q[:, h, m2 * P:m2 * P + P], start=True, stop=True)
                mm.then_inc(paired, 1)

            def sums(l):
                pe.wait_ge(masked, l + 1)
                for m in range(TT if l < levels - 1 else 1):
                    for h in range(HG):
                        m2 = m if l < levels - 1 else 1
                        mm = pe.matmul(c.bank[4 + m2][:, h * P:h * P + P],
                                       sm[l % 2][:, (m * HG + h) * P:(m * HG + h + 1) * P],
                                       c.v[:, m, h * P:h * P + P], start=l == 0 and h == 0, stop=l >= levels - 2,
                                       skip_group_check=True)
                mm.then_inc(summed, 1)

            for j in range(HEAD):
                mod_chunk(c, pe, part, j)
            for l in range(levels + 1):
                if l < levels:
                    pairs(l)
                if l >= 1:
                    sums(l - 1)
                mod_chunk(c, pe, part, HEAD + l)
            pe.wait_ge(yb_ready, 1)
            turn_pe(c, pe, 20, c.v, c.bank[0:2], 4)
            pe.wait_ge(ya_split, 2)
            turned_all(c, pe, 20, 4)
            for p in range(2):
                for h in range(2):
                    n = W + 2 * p + h
                    multiply_rows(c, pe, n, n % RING, h * CK, c.bank[2 * p + 2:2 * p + 4], h == 0, h == 1)
    c.chunk = W + 4


def add_gated(c, dve, used, banks, p, gate):
    dve.wait_ge(c.used, used)
    cols = slice(p * COLS, p * COLS + COLS)
    for m in range(TT):
        last = dve.tensor_tensor(c.h[:, m, cols], banks[m], gate[:, cols], ALU.mult)
    linked(c, dve, last)
    for m in range(TT):
        last = dve.tensor_tensor(c.x[:, m, cols], c.x[:, m, cols], c.h[:, m, cols], ALU.add)
    linked(c, dve, last)



QUARTERS = 4
QUARTER = 8


def make_mlp(c):
    c.relu_ready = c.sem("relu_ready")
    c.act_high = c.sem("act_high")
    c.square_ready = c.sem("square_ready")
    c.act_ready = c.sem("act_ready")


def phase_mlp(c, layer):
    nc, d = c.nc, c.dram
    W = c.chunk
    last_phase = layer == 1
    done = layer * 2 * QUARTERS
    v, turn = FIRST_RMS + 1 + 2 * layer, 22 + 12 * layer
    n_chunks = QUARTERS * QUARTER

    with ExitStack() as local, nc.Block() as block:
        c.h = c.sb(f"h_mlp{layer}", [P, TT, D], ctx=local)
        relu = c.sb(f"relu{layer}", [P, 2, CK, S], ctx=local)
        square = c.sb(f"square{layer}", [P, CK, S], ctx=local)
        ah = c.sb(f"act_h{layer}", [P, KT, S], F32R, ctx=local)
        al = c.sb(f"act_l{layer}", [P, KT, S], F32R, ctx=local)

        def panel_banks(p):
            return c.psum[:, 4 + 2 * p:6 + 2 * p, :].rearrange("q b (k s) -> q (b k) s", k=2)

        @block.sync
        def _(sp):
            def load(i, q, j):
                load_chunk(c, sp, i * QUARTER + (W + q * QUARTER + j), (W + j) % RING,
                           mlp_source(c, layer, i + q, j))

            with sp.Fori(0, QUARTERS - 1) as i:
                for j in range(LOADED, QUARTER):
                    load(i, 0, j)
                for j in range(LOADED):
                    load(i, 1, j)
            for n in range(n_chunks - QUARTER + LOADED, n_chunks + LOADED):
                if not last_phase or n < n_chunks:
                    load_chunk(c, sp, W + n, (W + n) % RING, static_source(c, W + n))

        @block.scalar
        def _(act):
            if not last_phase:
                norm_load(c, act, 1, 0)
                act.wait_ge(c.mod_stored, 48)
                mod_load(c, act, 1, range(2))
            rms_act(c, act, v, c.h)
            turn_act(c, act, turn, c.bank[4:8])
            act.sem_inc(c.relu_ready, 2) if layer == 0 else None

            def quarter(i, more):
                def high_of(j):
                    if j < QUARTER or more:
                        split_high(c, act, i * QUARTER + (W + j), i * (QUARTER // RING) + ((W + j) // RING + 1),
                                   (W + j) % RING)

                for p in range(2):
                    high_of(2 * p + 2)
                    high_of(2 * p + 3)
                    act.wait_ge(c.used, i * QUARTER + (W + 2 * p + 2))
                    act.wait_ge(c.act_ready, i * 2 + (done + p + 1))
                    act.activation(relu[:, p], panel_banks(p), ACT.Relu).then_inc(c.relu_ready, 1)
                    act.wait_ge(c.relu_ready, i * 2 + (done + p + 3))
                    act.activation(ah[:, CK * p:CK * p + CK, :], relu[:, p], ACT.Square).then_inc(c.act_high, 1)
                for j in range(6, 10):
                    high_of(j)

            with act.Fori(0, QUARTERS - 1) as i:
                quarter(i, True)
            quarter(QUARTERS - 1, not last_phase)

        @block.vector
        def _(dve):
            if last_phase:
                dve.wait_ge(c.norm_loaded, 64)
            rms_dve(c, dve, v, c.h, 1)
            turn_dve(c, dve, turn, c.bank[4:8])
            dve.sem_inc(c.act_ready, 2) if layer == 0 else None

            def quarter(i, more):
                def low_of(j):
                    if j < QUARTER or more:
                        split_low(c, dve, i * QUARTER + (W + j), (W + j) % RING)

                for p in range(2):
                    low_of(2 * p + 2)
                    low_of(2 * p + 3)
                    dve.wait_ge(c.relu_ready, i * 2 + (done + p + 3))
                    dve.wait_ge(c.act_ready, i * 2 + (done + p + 2))
                    dve.tensor_tensor(square[:, :, :], relu[:, p], relu[:, p], ALU.mult).then_inc(c.square_ready, 1)
                    dve.wait_ge(c.square_ready, i * 2 + (done + p + 1))
                    dve.wait_ge(c.act_high, i * 2 + (done + p + 1))
                    part = slice(CK * p, CK * p + CK)
                    dve.tensor_tensor(al[:, part, :], square[:, :, :], ah[:, part, :].bitcast(F32), ALU.subtract
                                      ).then_inc(c.act_ready, 1)
                for j in range(6, 10):
                    low_of(j)

            with dve.Fori(0, QUARTERS - 1) as i:
                quarter(i, True)
            quarter(QUARTERS - 1, not last_phase)
            for p in range(2):
                add_gated(c, dve, W + n_chunks - 1 + p, (c.bank[p], c.bank[2 + p]), p, c.mod[:, 5])
            dve.sem_inc(c.x_ready, 1)

        @block.tensor
        def _(pe):
            pe.wait_ge(c.h_ready, 2 * layer + 2)
            turn_pe(c, pe, turn, c.h, c.bank[4:8])
            turned_all(c, pe, turn)

            def quarter(i, first):
                for p in range(2):
                    pe.wait_ge(c.relu_ready, i * 2 + (done + p + 1))
                    for h in range(2):
                        j = 2 * p + h
                        multiply_cols(c, pe, i * QUARTER + (W + j), (W + j) % RING, h * CK,
                                      c.bank[4 + 2 * p:6 + 2 * p], h == 0, h == 1)
                for h in range(2):
                    pe.wait_ge(c.act_ready, i * 2 + (done + h + 3))
                    for p in range(2):
                        j = 4 + 2 * h + p
                        multiply_rows(c, pe, i * QUARTER + (W + j), (W + j) % RING, h * CK,
                                      (c.bank[p], c.bank[2 + p]), first and h == 0, False, ah, al, True)

            quarter(0, True)
            with pe.Fori(1, QUARTERS) as i:
                quarter(i, False)
    c.chunk += n_chunks



SB = 16
SD = D // SB


def phase_qkv(c):
    nc, d = c.nc, c.dram
    W = c.chunk
    panels = 6
    gains_loaded = c.sem("gains_loaded")
    evacuated = c.sem("qkv_evacuated")
    squares = c.sem("head_squares")
    head_rv, head_rs = c.sem("head_rv"), c.sem("head_rs")
    normed = c.sem("head_normed")
    qk_turned = c.sem("qk_turned")
    qk_kept = c.sem("qk_kept")
    masked = c.sem("unseen_step")
    cm = c.sbctx
    c.v16 = c.sb("v16", [P, TT, D], ctx=cm)
    c.qt = c.sb("qt", [P, KT, S], ctx=cm)
    c.kt = c.sb("kt", [P, KT, S], ctx=cm)
    c.unseen = c.sb("unseen", [P, P], ctx=cm)
    c.ones = c.sb("ones_sb", [P, S], ctx=cm)

    with ExitStack() as local, nc.Block() as block:
        c.h = c.sb("h_qkv", [P, TT, D], ctx=local)
        tokens = c.sb("qk", [P, 2, TT, D], ctx=local)
        gain = c.sb("qk_gain", [P, 2, SD], ctx=local)
        ss = c.sb("head_ss", [P, TT * SB], ctx=local)
        heads = tokens[:, :, :, :].rearrange("p t m (h n) -> p t (m h) n", n=SD)
        squared = c.h[:, :, :].rearrange("p m n -> p (m n)")

        @block.sync
        def _(sp):
            load_static(c, sp, LOADED, 2 * panels + RING)

        @block.gpsimd
        def _(pool):
            pool.memset(c.ones[:, :], 1.0).then_inc(masked, 1)
            pool.wait_ge(masked, 1)
            pool.memset(c.unseen[:, :], 0.0).then_inc(masked, 1)
            pool.wait_ge(masked, 2)
            pool.affine_select(out=c.unseen[:, :], in_=c.unseen[:, :], compare_op=ALU.is_gt, fill=NEG, base=0,
                               pattern=[[-1, P]], channel_multiplier=1).then_inc(masked, 1)
            pool.wait_ge(masked, 3)

        @block.scalar
        def _(act):
            for j, name in enumerate(("q_norm_2", "k_norm_2")):
                act.dma_start(gain[:, j, :], d[name][0].partition_broadcast(P)).then_inc(gains_loaded, 16)
            norm_load(c, act, 1, 1)
            rms_act(c, act, FIRST_RMS + 2, c.h)
            turn_act(c, act, 26, c.bank[4:8])
            for p in range(panels):
                for n in range(2 * p + 2, min(2 * p + 4, 2 * panels)):
                    high(c, act, W + n)
                if p in (1, 3):
                    t = p // 2
                    act.wait_ge(evacuated, p + 1)
                    act.activation(squared, tokens[:, t].rearrange("p m n -> p (m n)"), ACT.Square
                                   ).then_inc(squares, 1)
                    act.wait_ge(head_rv, t + 1)
                    act.activation(ss[:, :], ss[:, :], ACT.Sqrt).then_inc(head_rs, 1)
                if p in (3, 5):
                    t = p // 2 - 1
                    for b in range(4):
                        act.wait_ge(qk_turned, 4 * t + b + 1)
                        act.activation((c.qt, c.kt)[t][:, 2 * b:2 * b + 2, :],
                                       c.bank[4 + b].rearrange("p (k s) -> p k s", k=2), ACT.Copy).then_inc(qk_kept, 1)

        @block.vector
        def _(dve):
            dve.wait_ge(c.norm_loaded, 48)
            dve.wait_ge(c.mod_loaded, 8 * 16)
            rms_dve(c, dve, FIRST_RMS + 2, c.h, 0)
            turn_dve(c, dve, 26, c.bank[4:8])
            dve.wait_ge(gains_loaded, 32)
            linked(c, dve, dve.tensor_scalar(gain[:, 0], gain[:, 0], SD ** -0.5, None, ALU.mult))
            for p in range(panels):
                for n in range(2 * p + 2, min(2 * p + 4, 2 * panels)):
                    low(c, dve, W + n)
                dve.wait_ge(c.used, W + 2 * p + 2)
                cols = slice(p % 2 * COLS, p % 2 * COLS + COLS)
                out = c.v16 if p >= 4 else tokens[:, p // 2]
                dve.tensor_copy(out[:, :, cols], c.psum[:, p % 2 * 2:p % 2 * 2 + 2, :]).then_inc(evacuated, 1)
                if p in (1, 3):
                    t = p // 2
                    dve.wait_ge(squares, t + 1)
                    linked(c, dve, dve.tensor_reduce(ss[:, :], c.h[:, :, :].rearrange("p m (h n) -> p (m h) n", n=SD),
                                                     AX, ALU.add))
                    linked(c, dve, dve.tensor_scalar(ss[:, :], ss[:, :], 1.0 / SD, EPS_RMS, ALU.mult, ALU.add))
                    dve.reciprocal(ss[:, :], ss[:, :]).then_inc(head_rv, 1)
                    dve.wait_ge(evacuated, p + 1)
                    linked(c, dve, dve.tensor_tensor(heads[:, t], heads[:, t], gain[:, t].unsqueeze(1).to_broadcast(
                        [P, TT * SB, SD]), ALU.mult))
                    dve.wait_ge(head_rs, t + 1)
                    dve.tensor_tensor(heads[:, t], heads[:, t], ss[:, :].unsqueeze(2).to_broadcast([P, TT * SB, SD]), ALU.mult
                                      ).then_inc(normed, 1)

        @block.tensor
        def _(pe):
            pe.wait_ge(c.h_ready, 3)
            turn_pe(c, pe, 26, c.h, c.bank[4:8])
            turned_all(c, pe, 26)
            for p in range(panels):
                if p >= 2:
                    pe.wait_ge(evacuated, p - 1)
                for h in range(2):
                    n = W + 2 * p + h
                    multiply_rows(c, pe, n, n % RING, h * CK, c.bank[p % 2 * 2:p % 2 * 2 + 2], h == 0, h == 1)
                if p in (3, 5):
                    t = p // 2 - 1
                    pe.wait_ge(normed, t + 1)
                    for k in range(KT):
                        if t == 1 and k % 2 == 0:
                            pe.wait_ge(qk_kept, k // 2 + 1)
                        for m in range(TT):
                            x = pe.transpose(c.bank[4 + k // 2][:, (k % 2) * S + m * P:(k % 2) * S + m * P + P],
                                             tokens[:, t, m, k * P:k * P + P], c.ident[:, :])
                        if k % 2:
                            x.then_inc(qk_turned, 1)
    c.chunk += 2 * panels



def phase_stick(c):
    nc, d = c.nc, c.dram
    W = c.chunk + PANEL * STICK_MOD
    units = SB
    scored = c.sem("z_scored")
    broken = c.sem("broken")
    swept = c.sem("swept")
    weighed = c.sem("stick_weighed")
    flipped = c.sem("stick_flipped")
    keyed = c.sem("stick_keyed")
    mixed = c.sem("stick_mixed")
    kept = c.sem("stick_kept")
    edge = c.sem("edge")
    silu_zero, silu_split = c.sem("silu1b_zero"), c.sem("silu1b_split")

    with ExitStack() as local, nc.Block() as block:
        c.h = o = c.sb("o16", [P, TT, D], ctx=local)
        beta = c.sb("beta", [P, 3, 2, S], ctx=local)
        rest = c.sb("one_minus_beta", [P, 2, 2, S], ctx=local)
        later = c.sb("later", [P, 2, S + 1], ctx=local)
        at = c.sb("weights_t", [P, 2, 512], ctx=local)
        silu = mod_silu(c, "silu1b", STICK_MOD, local)
        mod_rows = c.sb("mod1b_rows", [STICK_MOD, COLS], ctx=local)
        part = ModPart(c, 1, SCAN_MOD, STICK_MOD, 7, mod_rows[:, :], "mod1b_")

        def width(u):
            return P * (u % 2 + 1)

        @block.sync
        def _(sp):
            load_static(c, sp, RING, part.chunks + 4 + LOADED)
            sp.wait_ge(c.mod_stored, part.stored)

        @block.gpsimd
        def _(pool):
            pool.memset(silu[:, :, :].bitcast(F32), 0.0).then_inc(silu_zero, 1)
            pool.memset(later[:, :, :], 1.0).then_inc(edge, 1)

        @block.tensor
        def _(pe):
            def scores(u):
                if u >= 2:
                    pe.wait_ge(broken, u - 1)
                m, w = u % 2, width(u)
                for j in range(2):
                    half = slice(j * 64, j * 64 + 64)
                    bank = c.bank[2 * m + j]
                    pe.matmul(bank[:, 0:w], c.qt[half, u // 2, m * P:m * P + P], c.kt[half, u // 2, 0:w],
                              start=True, stop=False)
                    mm = pe.matmul(bank[:, w - P:w], c.ident[:, :], c.unseen[:, :], start=False, stop=True)
                mm.then_inc(scored, 1)

            def flip(u):
                pe.wait_ge(weighed, u + 1)
                if u >= 2:
                    pe.wait_ge(keyed, u - 1)
                for j in range(2):
                    for k in range(u % 2 + 1):
                        t = pe.transpose(c.bank[4 + u % 2][:, (2 * j + k) * P:(2 * j + k) * P + P],
                                         beta[:, u % 3, j, k * P:k * P + P], c.ident[:, :])
                t.then_inc(flipped, 1)

            def mix(u):
                pe.wait_ge(keyed, u + 1)
                if u >= 1:
                    pe.wait_ge(kept, u)
                for j in range(2):
                    for k in range(u % 2 + 1):
                        v0 = (u // 2 * 2 + j) * SD
                        mm = pe.matmul(c.bank[6][:, j * SD:j * SD + SD],
                                       at[:, u % 2, (2 * j + k) * P:(2 * j + k) * P + P], c.v16[:, k, v0:v0 + SD],
                                       start=k == 0, stop=k == u % 2)
                mm.then_inc(mixed, 1)

            scores(0)
            pe.wait_ge(silu_split, 2)
            for u in range(units + 2):
                if u + 1 < units:
                    scores(u + 1)
                mod_split_pe(c, pe, part, u, silu)
                if 2 <= u < units + 2:
                    mix(u - 2)
                if 1 <= u <= units:
                    flip(u - 1)
            pe.wait_ge(part.done, 1)
            pe.wait_ge(kept, units)
            turn_pe(c, pe, 30, o, c.bank[4:8])
            turned_all(c, pe, 30)
            for p in range(2):
                for h in range(2):
                    n = W + 2 * p + h
                    multiply_rows(c, pe, n, n % RING, h * CK, c.bank[2 * p:2 * p + 2], h == 0, h == 1)

        @block.scalar
        def _(act):
            mod_bias_load(c, act, part)

            def split(u):
                z = c.psum[:, 2 * (u % 2):2 * (u % 2) + 2, 0:width(u)]
                act.wait_ge(scored, u + 1)
                if u >= 3:
                    act.wait_ge(flipped, u - 2)
                act.activation(beta[:, u % 3, :, 0:width(u)], z, ACT.Sigmoid)
                if u >= 2:
                    act.wait_ge(swept, u - 1)
                act.activation(rest[:, u % 2, :, 0:width(u)], z, ACT.Sigmoid, scale=-1.0).then_inc(broken, 1)

            def key(u):
                act.wait_ge(flipped, u + 1)
                if u >= 2:
                    act.wait_ge(mixed, u - 1)
                w = width(u)
                act.activation(at[:, u % 2].rearrange("p (j k) -> p j k", j=2)[:, :, 0:w],
                               c.bank[4 + u % 2].rearrange("p (j k) -> p j k", j=2)[:, :, 0:w], ACT.Copy
                               ).then_inc(keyed, 1)

            mod_silu_act(c, act, silu, STICK_MOD, silu_zero, silu_split)
            for n in range(AHEAD):
                high(c, act, part.W + n)
            for u in range(units + 1):
                if u < units:
                    split(u)
                if u >= 1:
                    key(u - 1)
                if u < part.chunks:
                    high(c, act, part.W + AHEAD + u)
            turn_act(c, act, 30, c.bank[4:8])
            mod_store_act(c, act, part)
            act.wait_ge(c.mod_stored, part.stored)
            mod_load(c, act, 1, range(2, 6))
            for n in range(AHEAD, 4 + AHEAD):
                high(c, act, W + n)

        @block.vector
        def _(dve):
            dve.wait_ge(edge, 1)

            def weigh(u):
                w = width(u)
                dve.wait_ge(broken, u + 1)
                if u >= 1:
                    dve.wait_ge(weighed, u)
                for j in range(2):
                    x = dve.tensor_tensor_scan(later[:, j, S - w:S][:, ::-1], rest[:, u % 2, j, 0:w][:, ::-1],
                                               c.ones[:, 0:w], 1.0, ALU.mult, ALU.mult)
                x.then_inc(swept, 1)
                dve.wait_ge(swept, u + 1)
                b = beta[:, u % 3, :, 0:w]
                dve.tensor_tensor(b, b, later[:, :, S - w + 1:S + 1], ALU.mult).then_inc(weighed, 1)

            def keep(u):
                dve.wait_ge(mixed, u + 1)
                dve.tensor_copy(o[:, u % 2, u // 2 * P:u // 2 * P + P], c.bank[6][:, 0:P]).then_inc(kept, 1)

            mod_silu_dve(c, dve, silu, STICK_MOD, silu_split)
            for n in range(AHEAD):
                low(c, dve, part.W + n)
            for u in range(units + 2):
                if u < units:
                    weigh(u)
                if u >= 2:
                    keep(u - 2)
                if u < part.chunks:
                    low(c, dve, part.W + AHEAD + u)
                if u == part.chunks + 1:
                    mod_rows_dve(c, dve, part)
            turn_dve(c, dve, 30, c.bank[4:8])
            dve.wait_ge(c.mod_loaded, 12 * 16)
            for p in range(2):
                low(c, dve, W + 2 * p + 2)
                low(c, dve, W + 2 * p + 3)
                add_gated(c, dve, W + 2 * p + 2, c.bank[2 * p:2 * p + 2], p, c.mod[:, 2])
            dve.sem_inc(c.x_ready, 1)
    c.chunk = W + 4


def phase_store(c, out):
    stored = c.sem("stored")
    with c.nc.Block() as block:
        @block.sync
        def _(sp):
            sp.wait_ge(c.x_ready, FIRST_RMS + 4)
            for m in range(TT):
                sp.dma_start(out[0, m * P:m * P + P, :], c.x[:, m]).then_inc(stored, 16)
            sp.wait_ge(stored, 16 * TT)


def program(nc, dram, out):
    with ExitStack() as ctx:
        c = make(nc, ctx, dram)
        with ExitStack() as c.moe:
            make_routing(c)
            with ExitStack() as c.mix:
                phase_in(c)
                phase_attend(c)
                phase_merge(c)
            with ExitStack() as c.exp:
                phase_experts(c)
                phase_spill(c)
        c.second = c.chunk
        with ExitStack() as c.two:
            make_second(c)
            phase_second(c)
            with ExitStack() as c.hgrn:
                phase_project_ab(c)
                phase_recur(c)
            make_mlp(c)
            phase_mlp(c, 0)
            with ExitStack() as c.sbctx:
                phase_qkv(c)
                phase_stick(c)
            phase_mlp(c, 1)
        phase_store(c, out)


NAMES = ["x", "ln_in_g", "ln_in_b", "w_in", "b_gate", "lambda_q1", "lambda_k1", "lambda_q2", "lambda_k2",
         "subln_w", "rel_bias", "w_branch_a", "w_branch_b", "w_out", "ln1_g", "ln1_b", "w_router", "b_router",
         "w_exp_in", "b_exp_in", "w_exp_out", "b_exp_out", "ln2_g", "ln2_b", "c_2", "ada_w_2", "ada_b_2",
         "norm_mix_2", "norm_mlp_2", "w_in_ab_2", "conv_w_2", "hg_norm_2", "lb_logits_2", "w_out_ab_2",
         "w_qkv_2", "q_norm_2", "k_norm_2", "w_out_c_2", "mlp_w1_2", "mlp_w2_2"]


def kernel(**inputs):
    import numpy as np
    import concourse.bacc as bacc
    from concourse.bass_utils import run_bass_kernel_spmd

    nc = bacc.Bacc("TRN2", target_bir_lowering=False, num_devices=1)
    arrays = {f"in_{n}": np.ascontiguousarray(inputs[n]) for n in NAMES}
    dram = {n: nc.dram_tensor(f"in_{n}", arrays[f"in_{n}"].shape, F32, kind="ExternalInput").ap() for n in NAMES}
    out = nc.dram_tensor("out", (1, S, D), F32, kind="ExternalOutput").ap()
    program(nc, dram, out)
    return run_bass_kernel_spmd(nc, [arrays], core_ids=[0]).results[0]["out"]
```
